# Optimizing a Trainium2 kernel written in Bass

```python
import math
import jax, jax.numpy as jnp
from jax import lax
import numpy as np

D_MODEL = 1024
BATCH = 1
SEQ = 256
DEPTH = 1

HEAD_DIM = 64
HEADS_PER_GROUP = 8
ATTN_GROUPS = ((128, 1), (512, 4), (2048, 16))
N_GROUPS = len(ATTN_GROUPS)
N_ATTN_HEADS = N_GROUPS * HEADS_PER_GROUP
ATTN_WIDTH = HEADS_PER_GROUP * HEAD_DIM
QKV_WIDTH = N_GROUPS * 3 * ATTN_WIDTH
BLOCK = 128
POOL_WINDOWS = (2, 4, 8, 16)
POOL_GROUPS = len(POOL_WINDOWS)
POOL_WIDTH = D_MODEL // 2
PGW = POOL_WIDTH // POOL_GROUPS
NUM_BUCKETS = 32
MAX_DISTANCE = 2048
EPS = 1e-6
SPLIT_SIZES = (QKV_WIDTH, ATTN_WIDTH, POOL_WIDTH, POOL_WIDTH, D_MODEL, D_MODEL)
SPLIT_POINTS = (QKV_WIDTH,
                QKV_WIDTH + ATTN_WIDTH,
                QKV_WIDTH + ATTN_WIDTH + POOL_WIDTH,
                QKV_WIDTH + ATTN_WIDTH + 2 * POOL_WIDTH,
                QKV_WIDTH + ATTN_WIDTH + 2 * POOL_WIDTH + D_MODEL)
IN_WIDTH = QKV_WIDTH + ATTN_WIDTH + 2 * POOL_WIDTH + 2 * D_MODEL


def rmsnorm(x, g):
    xf = x.astype(jnp.float32)
    y = xf * lax.rsqrt(jnp.mean(xf * xf, axis=-1, keepdims=True) + EPS)
    return (y * g.astype(jnp.float32)).astype(x.dtype)

def t5_bucket(n):
    max_exact = NUM_BUCKETS // 2
    nf = jnp.maximum(n, 1).astype(jnp.float32)
    large = max_exact + (jnp.log(nf / max_exact) / math.log(MAX_DISTANCE / max_exact)
                         * (NUM_BUCKETS - max_exact)).astype(jnp.int32)
    large = jnp.minimum(large, NUM_BUCKETS - 1)
    return jnp.where(n < max_exact, n, large)

def to_sub(t, dil):
    B, S = t.shape[:2]
    L = S // dil
    t = t.reshape((B, L, dil) + t.shape[2:])
    t = jnp.moveaxis(t, 2, 1)
    return t.reshape((B * dil, L) + t.shape[3:])

def from_sub(t, B, dil):
    L = t.shape[1]
    t = t.reshape((B, dil, L) + t.shape[2:])
    t = jnp.moveaxis(t, 1, 2)
    return t.reshape((B, L * dil) + t.shape[3:])

def dilated_window_attention(q, k, v, dil, n_back, bias_g):
    B, S, H, Dh = q.shape
    L = S // dil
    nb = -(-L // BLOCK)
    pad = nb * BLOCK - L
    Bd = B * dil

    def sub(t):
        return jnp.pad(to_sub(t, dil), ((0, 0), (0, pad), (0, 0), (0, 0)))

    def band(t):
        tp = jnp.pad(t, ((0, 0), (BLOCK, 0), (0, 0), (0, 0)))
        prev = tp[:, :-BLOCK].reshape(Bd, nb, BLOCK, H, Dh)
        cur = t.reshape(Bd, nb, BLOCK, H, Dh)
        return jnp.concatenate([prev, cur], axis=2)

    qb = sub(q).reshape(Bd, nb, BLOCK, H, Dh)
    kb = band(sub(k))
    vb = band(sub(v))

    i = jnp.arange(BLOCK)[:, None]
    j = jnp.arange(2 * BLOCK)[None, :]
    dist = BLOCK + i - j
    band_ok = (dist >= 0) & (dist <= n_back)
    key_ok = (jnp.arange(nb)[:, None, None] * BLOCK - BLOCK + j[None]) >= 0
    mask = band_ok[None] & key_ok
    bucket = t5_bucket(jnp.clip(dist, 0, n_back) * dil)
    bias = jnp.transpose(bias_g[bucket].astype(jnp.float32), (2, 0, 1))

    logits = jnp.einsum('znqhd,znkhd->znhqk', qb, kb).astype(jnp.float32) * (HEAD_DIM ** -0.5)
    logits = jnp.where(mask[None, :, None], logits + bias[None, None], -jnp.inf)
    m = jnp.max(logits, axis=-1, keepdims=True)
    p = jnp.exp(logits - m)
    denom = jnp.sum(p, axis=-1)
    o = jnp.einsum('znhqk,znkhd->znqhd', p.astype(vb.dtype), vb).astype(jnp.float32)
    o = o / jnp.moveaxis(denom, 2, 3)[..., None]
    lse = jnp.moveaxis(m[..., 0] + jnp.log(denom), 2, 3)

    o = o.reshape(Bd, nb * BLOCK, H, Dh)[:, :L]
    lse = lse.reshape(Bd, nb * BLOCK, H)[:, :L]
    return from_sub(o, B, dil), from_sub(lse, B, dil)

def multiscale_pool(u):
    B, S, C = u.shape
    uf = u.astype(jnp.float32)
    csp = jnp.pad(jnp.cumsum(uf, axis=1), ((0, 0), (1, 0), (0, 0)))
    t = jnp.arange(S)
    outs = []
    for g, win in enumerate(POOL_WINDOWS):
        cg = csp[:, :, g * PGW:(g + 1) * PGW]
        lo = jnp.maximum(t + 1 - win, 0)
        s = cg[:, 1:] - cg[:, lo]
        cnt = jnp.minimum(t + 1, win).astype(jnp.float32)
        outs.append(s / cnt[None, :, None])
    return jnp.concatenate(outs, axis=-1) - uf

def first_inputs(seed: int = 0) -> dict:
    key = jax.random.key(seed)
    ks = jax.random.split(key, 14)
    f32 = jnp.float32
    nrm = lambda k, shape, s: (jax.random.normal(k, shape, f32) * s).astype(f32)
    return {
        "x": nrm(ks[0], (BATCH, SEQ, D_MODEL), 1.0),
        "c": nrm(ks[1], (BATCH, D_MODEL), 1.0),
        "norm_g": 1.0 + nrm(ks[2], (DEPTH, D_MODEL), 0.05),
        "w_ada": nrm(ks[3], (DEPTH, D_MODEL, 3 * D_MODEL), 0.5 * D_MODEL ** -0.5),
        "b_ada": nrm(ks[4], (DEPTH, 3 * D_MODEL), 0.01),
        "w_in": nrm(ks[5], (DEPTH, D_MODEL, IN_WIDTH), D_MODEL ** -0.5),
        "pool_w": nrm(ks[6], (DEPTH, POOL_GROUPS, PGW, PGW), PGW ** -0.5),
        "pool_scale": 1.0 + nrm(ks[7], (DEPTH, POOL_WIDTH), 0.1),
        "w_attn_br": nrm(ks[8], (DEPTH, ATTN_WIDTH, D_MODEL), ATTN_WIDTH ** -0.5),
        "w_pool_br": nrm(ks[9], (DEPTH, POOL_WIDTH, D_MODEL), POOL_WIDTH ** -0.5),
        "w_out": nrm(ks[10], (DEPTH, D_MODEL, D_MODEL), D_MODEL ** -0.5),
        "rel_bias": nrm(ks[11], (NUM_BUCKETS, N_ATTN_HEADS), 0.5),
        "final_g": 1.0 + nrm(ks[12], (D_MODEL,), 0.05),
    }

def first_block(x, c, norm_g, w_ada, b_ada, w_in, pool_w, pool_scale, w_attn_br, w_pool_br, w_out, rel_bias, final_g):
    B, S, D = x.shape
    for l in range(DEPTH):
        mod = c @ w_ada[l] + b_ada[l]
        shift, scale, gate = jnp.split(mod, 3, axis=-1)
        h = rmsnorm(x, norm_g[l]) * (1.0 + scale[:, None]) + shift[:, None]

        proj = h @ w_in[l]
        qkv, z_attn, u_pool, z_pool, g_attn, g_pool = jnp.split(proj, SPLIT_POINTS, axis=-1)
        qkv = qkv.reshape(B, S, N_GROUPS, 3, HEADS_PER_GROUP, HEAD_DIM)

        outs, lses = [], []
        for gi, (win, dil) in enumerate(ATTN_GROUPS):
            bias_g = rel_bias[:, gi * HEADS_PER_GROUP:(gi + 1) * HEADS_PER_GROUP]
            o, lse = dilated_window_attention(qkv[:, :, gi, 0], qkv[:, :, gi, 1], qkv[:, :, gi, 2],
                                              dil, win // dil, bias_g)
            outs.append(o)
            lses.append(lse)
        wts = jax.nn.softmax(jnp.stack(lses, axis=0), axis=0)
        attn = jnp.sum(wts[..., None] * jnp.stack(outs, axis=0), axis=0)
        attn = attn.reshape(B, S, ATTN_WIDTH).astype(x.dtype)
        y_attn = (attn * jax.nn.silu(z_attn)) @ w_attn_br[l]

        pooled = multiscale_pool(u_pool).reshape(B, S, POOL_GROUPS, PGW)
        mixed = jnp.einsum('bsgc,gce->bsge', pooled, pool_w[l].astype(jnp.float32))
        mixed = (mixed.reshape(B, S, POOL_WIDTH) * pool_scale[l]).astype(x.dtype)
        y_pool = (mixed * jax.nn.silu(z_pool)) @ w_pool_br[l]

        merged = jax.nn.sigmoid(g_attn) * y_attn + jax.nn.sigmoid(g_pool) * y_pool
        x = x + gate[:, None] * (merged @ w_out[l])
    return rmsnorm(x, final_g)


DEPTH_2 = 2

GRID_W = 64
CTX_LEN = 256

MIX_HALF = D_MODEL // 2
RET_HEADS = 4
RET_DV = MIX_HALF // RET_HEADS
RET_DK = RET_DV // 2
RET_DECAY_BASE = 5
GLA_HEADS = 4
GLA_DV = MIX_HALF // GLA_HEADS
GLA_DK = GLA_DV // 2
GLA_GATE_RANK = 16
GLA_GATE_TAU = 16.0
SCAN_CHUNK = 64
RET_QK = RET_HEADS * RET_DK
RET_V = RET_HEADS * RET_DV
GLA_QK = GLA_HEADS * GLA_DK
GLA_V = GLA_HEADS * GLA_DV
EVEN_SPLITS = (RET_QK, RET_QK, RET_V, RET_V, GLA_QK, GLA_QK, GLA_V, GLA_V, 2 * GLA_GATE_RANK)
EVEN_PROJ = 2 * RET_QK + 2 * RET_V + 2 * GLA_QK + 2 * GLA_V + 2 * GLA_GATE_RANK

ATT_HEAD_DIM = 64
ATT_Q_HEADS = D_MODEL // ATT_HEAD_DIM
ATT_GROUP = 4
ATT_KV_HEADS = ATT_Q_HEADS // ATT_GROUP
WINDOW = 128
ATT_BLOCK = 128
ATT_QW = ATT_Q_HEADS * ATT_HEAD_DIM
ATT_KVW = ATT_KV_HEADS * ATT_HEAD_DIM
ATT_PROJ = ATT_QW + 2 * ATT_KVW
ROPE_BASE = 10000.0

D_FF = 4 * D_MODEL
DEEPNORM_ALPHA = (2.0 * DEPTH_2) ** 0.25
DEEPNORM_BETA = (8.0 * DEPTH_2) ** -0.25
LN_EPS = 1e-5
RMS_EPS = 1e-6
N_EVEN = (DEPTH_2 + 1) // 2
N_ODD = DEPTH_2 // 2


def layer_norm(x, g, b):
    xf = x.astype(jnp.float32)
    mu = jnp.mean(xf, axis=-1, keepdims=True)
    var = jnp.mean(jnp.square(xf - mu), axis=-1, keepdims=True)
    return ((xf - mu) * lax.rsqrt(var + LN_EPS) * g + b).astype(x.dtype)

def rms_norm(x, g=None):
    xf = x.astype(jnp.float32)
    y = xf * lax.rsqrt(jnp.mean(jnp.square(xf), axis=-1, keepdims=True) + RMS_EPS)
    if g is not None:
        y = y * g
    return y.astype(x.dtype)

def modulation(cvec, w, b):
    m = jax.nn.silu(cvec) @ w + b
    return jnp.split(m[..., None, :], 6, axis=-1)

def sublayer_residual(x, y, gate, g, b):
    return layer_norm(DEEPNORM_ALPHA * x + gate * y, g, b)

def split_cols(t, sizes):
    idx = np.cumsum(sizes)[:-1].tolist()
    return jnp.split(t, idx, axis=-1)

def split_heads(t, h):
    b, n, _ = t.shape
    return t.reshape(b, n, h, -1).transpose(0, 2, 1, 3)

def merge_heads(t):
    b, h, n, d = t.shape
    return t.transpose(0, 2, 1, 3).reshape(b, n, h * d)

def sq_relu_mlp(h, w1, w2):
    return jnp.square(jax.nn.relu(h @ w1)) @ w2

def chunk_gated_scan(q, k, v, log_a, s0, strict):
    f32 = jnp.float32
    B, H, T, dk = q.shape
    dv = v.shape[-1]
    n = T // SCAN_CHUNK
    qc = q.astype(f32).reshape(B, H, n, SCAN_CHUNK, dk)
    kc = k.astype(f32).reshape(B, H, n, SCAN_CHUNK, dk)
    vc = v.astype(f32).reshape(B, H, n, SCAN_CHUNK, dv)
    bcum = jnp.cumsum(log_a.astype(f32).reshape(B, H, n, SCAN_CHUNK, dk), axis=3)
    b_last = bcum[:, :, :, -1:, :]
    q_dec = qc * jnp.exp(bcum)
    k_inv = kc * jnp.exp(-bcum)
    k_end = kc * jnp.exp(b_last - bcum)
    mask = jnp.tril(jnp.ones((SCAN_CHUNK, SCAN_CHUNK), bool), k=-1 if strict else 0)
    scores = jnp.einsum('bhncd,bhnsd->bhncs', q_dec, k_inv)
    o_intra = jnp.einsum('bhncs,bhnse->bhnce', jnp.where(mask, scores, 0.0), vc)
    kv = jnp.einsum('bhnsd,bhnse->bhnde', k_end, vc)
    chunk_decay = jnp.exp(b_last[:, :, :, 0, :])

    def step(s, inp):
        kv_n, dec_n = inp
        return dec_n[..., None] * s + kv_n, s

    s_final, s_prev = lax.scan(step, s0.astype(f32),
                               (jnp.moveaxis(kv, 2, 0), jnp.moveaxis(chunk_decay, 2, 0)))
    s_prev = jnp.moveaxis(s_prev, 0, 2)
    o_inter = jnp.einsum('bhncd,bhnde->bhnce', q_dec, s_prev)
    o = (o_intra + o_inter).reshape(B, H, T, dv)
    return o.astype(v.dtype), s_final

def bidir_scan(q, k, v, log_a_f, log_a_b, s0_f, s0_b):
    flip = lambda t: jnp.flip(t, axis=2)
    o_f, s_f = chunk_gated_scan(q, k, v, log_a_f, s0_f, strict=False)
    o_b, s_b = chunk_gated_scan(flip(q), flip(k), flip(v), flip(log_a_b), s0_b, strict=True)
    return o_f + flip(o_b), s_f, s_b

def retention_gla_mixer(h, w_in, ret_theta, gla_gk_w, gla_gk_b, gla_norm_g, s0):
    f32 = jnp.float32
    qa, ka, va, ga, qb, kb, vb, gb, lr = split_cols(h @ w_in, EVEN_SPLITS)
    qa = split_heads(qa, RET_HEADS)
    ka = split_heads(ka, RET_HEADS) * RET_DK ** -0.5
    va = split_heads(va, RET_HEADS)
    log_gamma = jnp.log1p(-jnp.exp(ret_theta.astype(f32)))
    la_f = jnp.broadcast_to(log_gamma[0][None, :, None, None], qa.shape)
    la_b = jnp.broadcast_to(log_gamma[1][None, :, None, None], qa.shape)
    o_a, ra_f, ra_b = bidir_scan(qa, ka, va, la_f, la_b, s0[0], s0[1])
    y_a = jax.nn.silu(ga) * merge_heads(rms_norm(o_a))
    qb = split_heads(qb, GLA_HEADS) * GLA_DK ** -0.5
    kb = split_heads(kb, GLA_HEADS)
    vb = split_heads(vb, GLA_HEADS)
    lr_f, lr_b = jnp.split(lr, 2, axis=-1)

    def gate(u, w, b):
        z = (u @ w + b).astype(f32)
        return split_heads(jax.nn.log_sigmoid(z) / GLA_GATE_TAU, GLA_HEADS)

    o_b, sb_f, sb_b = bidir_scan(qb, kb, vb, gate(lr_f, gla_gk_w[0], gla_gk_b[0]),
                                 gate(lr_b, gla_gk_w[1], gla_gk_b[1]), s0[2], s0[3])
    y_b = jax.nn.silu(gb) * merge_heads(rms_norm(o_b, gla_norm_g))
    return jnp.concatenate([y_a, y_b], axis=-1), (ra_f, ra_b, sb_f, sb_b)

def axial_rope(t, row, col):
    f32 = jnp.float32
    half = ATT_HEAD_DIM // 2
    inv_freq = ROPE_BASE ** (-jnp.arange(0, half, 2, dtype=f32) / half)

    def rot(u, p):
        ang = p.astype(f32)[:, None] * inv_freq[None, :]
        cos, sin = jnp.cos(ang), jnp.sin(ang)
        u1, u2 = u[..., :half // 2], u[..., half // 2:]
        return jnp.concatenate([u1 * cos - u2 * sin, u1 * sin + u2 * cos], axis=-1)

    return jnp.concatenate([rot(t[..., :half], row), rot(t[..., half:], col)], axis=-1).astype(t.dtype)

def window_attention(q, k, v, k_c, v_c, sink):
    f32 = jnp.float32
    B, Hq, T, dh = q.shape
    nb = T // ATT_BLOCK
    scale = dh ** -0.5
    qb = q.reshape(B, ATT_KV_HEADS, ATT_GROUP, nb, ATT_BLOCK, dh)
    pad = ((0, 0), (0, 0), (ATT_BLOCK, ATT_BLOCK), (0, 0))
    kp = jnp.pad(k, pad).reshape(B, ATT_KV_HEADS, nb + 2, ATT_BLOCK, dh)
    vp = jnp.pad(v, pad).reshape(B, ATT_KV_HEADS, nb + 2, ATT_BLOCK, dh)
    kb = jnp.concatenate([kp[:, :, 0:nb], kp[:, :, 1:nb + 1], kp[:, :, 2:nb + 2]], axis=3)
    vb = jnp.concatenate([vp[:, :, 0:nb], vp[:, :, 1:nb + 1], vp[:, :, 2:nb + 2]], axis=3)
    qi = jnp.arange(ATT_BLOCK)[:, None]
    kj = jnp.arange(3 * ATT_BLOCK)[None, :]
    in_window = jnp.abs(kj - ATT_BLOCK - qi) <= WINDOW
    kpos = (jnp.arange(nb)[:, None] - 1) * ATT_BLOCK + jnp.arange(3 * ATT_BLOCK)[None, :]
    in_range = (kpos >= 0) & (kpos < T)
    valid = in_window[None] & in_range[:, None, :]
    s_loc = jnp.einsum('bkgnqd,bkncd->bkgnqc', qb, kb).astype(f32) * scale
    s_loc = jnp.where(valid, s_loc, -jnp.inf)
    s_ctx = jnp.einsum('bkgnqd,bkld->bkgnql', qb, k_c).astype(f32) * scale
    s_sink = sink.astype(f32).reshape(1, ATT_KV_HEADS, ATT_GROUP, 1, 1, 1)
    m = jnp.maximum(jnp.maximum(jnp.max(s_loc, -1, keepdims=True), jnp.max(s_ctx, -1, keepdims=True)), s_sink)
    e_loc = jnp.exp(s_loc - m)
    e_ctx = jnp.exp(s_ctx - m)
    denom = jnp.sum(e_loc, -1, keepdims=True) + jnp.sum(e_ctx, -1, keepdims=True) + jnp.exp(s_sink - m)
    o = (jnp.einsum('bkgnqc,bkncd->bkgnqd', e_loc, vb.astype(f32))
         + jnp.einsum('bkgnql,bkld->bkgnqd', e_ctx, v_c.astype(f32))) / denom
    return o.reshape(B, Hq, T, dh).astype(q.dtype)

def context_attention(q_c, k_c, v_c, sink):
    f32 = jnp.float32
    B, Hq, L, dh = q_c.shape
    qg = q_c.reshape(B, ATT_KV_HEADS, ATT_GROUP, L, dh)
    s = jnp.einsum('bkgqd,bkld->bkgql', qg, k_c).astype(f32) * dh ** -0.5
    s_sink = jnp.broadcast_to(sink.astype(f32).reshape(1, ATT_KV_HEADS, ATT_GROUP, 1, 1), s.shape[:-1] + (1,))
    p = jax.nn.softmax(jnp.concatenate([s, s_sink], axis=-1), axis=-1)[..., :L]
    return jnp.einsum('bkgql,bkld->bkgqd', p, v_c.astype(f32)).reshape(B, Hq, L, dh).astype(q_c.dtype)

def second_inputs(seed: int = 0) -> dict:
    key = jax.random.key(seed)
    ks = jax.random.split(key, 19)
    f32 = jnp.float32
    D = D_MODEL

    def nrm(k, shape, fan_in, scale=1.0):
        return jax.random.normal(k, shape, f32) * (scale * fan_in ** -0.5)

    ret_init = -(RET_DECAY_BASE + jnp.arange(RET_HEADS, dtype=f32)) * jnp.log(2.0)
    return {
        'x': jax.random.normal(ks[0], (BATCH, SEQ, D), f32),
        'c': jax.random.normal(ks[1], (BATCH, D), f32),
        'ctx': jax.random.normal(ks[2], (BATCH, CTX_LEN, D), f32),
        'c_ctx': jax.random.normal(ks[3], (D,), f32),
        'w_mod': nrm(ks[4], (DEPTH_2, D, 6 * D), D),
        'b_mod': 0.02 * jax.random.normal(ks[5], (DEPTH_2, 6 * D), f32),
        'ln_g': 1.0 + 0.02 * jax.random.normal(ks[6], (DEPTH_2, 2, D), f32),
        'ln_b': 0.02 * jax.random.normal(ks[7], (DEPTH_2, 2, D), f32),
        'mlp_w1': nrm(ks[8], (DEPTH_2, D, D_FF), D),
        'mlp_w2': nrm(ks[9], (DEPTH_2, D_FF, D), D_FF, DEEPNORM_BETA),
        'ev_w_in': nrm(ks[10], (N_EVEN, D, EVEN_PROJ), D),
        'ev_ret_theta': ret_init + 0.05 * jax.random.normal(ks[11], (N_EVEN, 2, RET_HEADS), f32),
        'ev_gla_gk_w': nrm(ks[12], (N_EVEN, 2, GLA_GATE_RANK, GLA_QK), GLA_GATE_RANK),
        'ev_gla_gk_b': 0.02 * jax.random.normal(ks[13], (N_EVEN, 2, GLA_QK), f32),
        'ev_gla_norm_g': 1.0 + 0.02 * jax.random.normal(ks[14], (N_EVEN, GLA_DV), f32),
        'ev_w_out': nrm(ks[15], (N_EVEN, D, D), D, DEEPNORM_BETA),
        'od_w_qkv': nrm(ks[16], (N_ODD, D, ATT_PROJ), D),
        'od_sink': 0.5 * jax.random.normal(ks[17], (N_ODD, ATT_Q_HEADS), f32),
        'od_w_out': nrm(ks[18], (N_ODD, D, D), D, DEEPNORM_BETA),
    }

def second_block(x, c, ctx, c_ctx, w_mod, b_mod, ln_g, ln_b, mlp_w1, mlp_w2,
              ev_w_in, ev_ret_theta, ev_gla_gk_w, ev_gla_gk_b, ev_gla_norm_g, ev_w_out,
              od_w_qkv, od_sink, od_w_out):
    B, T, _ = x.shape
    rows = T // GRID_W
    row = jnp.repeat(jnp.arange(rows), GRID_W)
    col = jnp.tile(jnp.arange(GRID_W), rows)
    xc = ctx
    for i in range(DEPTH_2):
        last = i == DEPTH_2 - 1
        j = i // 2
        sh1, sc1, g1, sh2, sc2, g2 = modulation(c, w_mod[i], b_mod[i])
        csh1, csc1, cg1, csh2, csc2, cg2 = modulation(c_ctx, w_mod[i], b_mod[i])
        h = x * (1.0 + sc1) + sh1
        hc = xc * (1.0 + csc1) + csh1
        if i % 2 == 0:
            prm = (ev_w_in[j], ev_ret_theta[j], ev_gla_gk_w[j], ev_gla_gk_b[j], ev_gla_norm_g[j])
            s0 = (jnp.zeros((B, RET_HEADS, RET_DK, RET_DV), jnp.float32),
                  jnp.zeros((B, RET_HEADS, RET_DK, RET_DV), jnp.float32),
                  jnp.zeros((B, GLA_HEADS, GLA_DK, GLA_DV), jnp.float32),
                  jnp.zeros((B, GLA_HEADS, GLA_DK, GLA_DV), jnp.float32))
            yc, ctx_states = retention_gla_mixer(hc, *prm, s0)
            y, _ = retention_gla_mixer(h, *prm, ctx_states)
            y = y @ ev_w_out[j]
            if not last:
                yc = yc @ ev_w_out[j]
        else:
            w = od_w_qkv[j]
            q, k, v = split_cols(h @ w, (ATT_QW, ATT_KVW, ATT_KVW))
            q = axial_rope(split_heads(q, ATT_Q_HEADS), row, col)
            k = axial_rope(split_heads(k, ATT_KV_HEADS), row, col)
            v = split_heads(v, ATT_KV_HEADS)
            k_c, v_c = split_cols(hc @ w[:, ATT_QW:], (ATT_KVW, ATT_KVW))
            k_c = split_heads(k_c, ATT_KV_HEADS)
            v_c = split_heads(v_c, ATT_KV_HEADS)
            y = merge_heads(window_attention(q, k, v, k_c, v_c, od_sink[j])) @ od_w_out[j]
            if not last:
                q_c = split_heads(hc @ w[:, :ATT_QW], ATT_Q_HEADS)
                yc = merge_heads(context_attention(q_c, k_c, v_c, od_sink[j])) @ od_w_out[j]
        x = sublayer_residual(x, y, g1, ln_g[i, 0], ln_b[i, 0])
        x = sublayer_residual(x, sq_relu_mlp(x * (1.0 + sc2) + sh2, mlp_w1[i], mlp_w2[i]), g2, ln_g[i, 1], ln_b[i, 1])
        if not last:
            xc = sublayer_residual(xc, yc, cg1, ln_g[i, 0], ln_b[i, 0])
            xc = sublayer_residual(xc, sq_relu_mlp(xc * (1.0 + csc2) + csh2, mlp_w1[i], mlp_w2[i]), cg2, ln_g[i, 1], ln_b[i, 1])
    return x


def setup_inputs(seed=0):
    out = dict(first_inputs(seed))
    for name, value in second_inputs(seed + 1).items():
        if name != "x":
            out[name + "_2"] = value
    return out


def reference(
    x, c, norm_g, w_ada, b_ada, w_in, pool_w, pool_scale, w_attn_br, w_pool_br, w_out, rel_bias,
    final_g, c_2, ctx_2, c_ctx_2, w_mod_2, b_mod_2, ln_g_2, ln_b_2, mlp_w1_2, mlp_w2_2,
    ev_w_in_2, ev_ret_theta_2, ev_gla_gk_w_2, ev_gla_gk_b_2, ev_gla_norm_g_2, ev_w_out_2,
    od_w_qkv_2, od_sink_2, od_w_out_2,
):
    x = first_block(
        x, c, norm_g, w_ada, b_ada, w_in, pool_w, pool_scale, w_attn_br, w_pool_br, w_out,
        rel_bias, final_g,
    )
    return second_block(
        x, c_2, ctx_2, c_ctx_2, w_mod_2, b_mod_2, ln_g_2, ln_b_2, mlp_w1_2, mlp_w2_2, ev_w_in_2,
        ev_ret_theta_2, ev_gla_gk_w_2, ev_gla_gk_b_2, ev_gla_norm_g_2, ev_w_out_2, od_w_qkv_2,
        od_sink_2, od_w_out_2,
    )


_drawn_inputs = setup_inputs


def setup_inputs(seed=0):
    import zlib

    import numpy as np

    out = dict(_drawn_inputs(seed))
    spreads = {}
    factors = {'norm_g': 3.026,
     'b_ada': 8.0,
     'ev_gla_gk_b_2': 8.0,
     'ev_gla_norm_g_2': 28.425,
     'od_sink_2': 35.451}
    for name, (base, spread) in spreads.items():
        noise = np.random.default_rng([zlib.crc32(name.encode()), seed]).standard_normal(out[name].shape)
        drawn = base * np.exp(spread * noise) if base else spread * noise
        out[name] = __import__('jax').numpy.asarray(drawn.astype(out[name].dtype))
    for name, factor in factors.items():
        out[name] = (out[name] * factor).astype(out[name].dtype)
    return out
```

```python
import math
from contextlib import ExitStack

import numpy as np

import concourse.bass as bass
from concourse import mybir

P = 128
D = 1024
KT = D // P
S = 256
NT = S // P
HEADS, HD, GROUPS = 8, 64, 3
DILS = (1, 4, 16)
N_BACK = 128
BUCKETS, MAX_DIST = 32, 2048
POOL_WINDOWS = (2, 4, 8, 16)
RH, DK, DV = 4, 64, 128
RANK, TAU = 16, 16.0
CH = 64
QH, KVH, AHD = 16, 4, 64
WINDOW = 128
ALPHA = (2.0 * 2) ** 0.25
EPS_RMS, EPS_LN = 1e-6, 1e-5
NEG = -1e30
UC = 256
W_IN, EV_IN, QKV, FF = 8192, 3104, 1536, 4096

RAW, SPL, LEAD, GSA, GSB = 2, 4, 3, 3, 2

ROWS = {}
_n = 0
for _name, _len in (("norm_g", 8), ("pool_scale", 4), ("ln_g", 32), ("ln_b", 32), ("c", 8), ("c_2", 8),
                    ("c_ctx", 8), ("final_g", 8), ("gla_g", 1)):
    ROWS[_name] = _n
    _n += _len
NROWS = _n


def constants():
    p = np.arange(P)
    parts, at, n = [], {}, 0

    def put(name, a):
        nonlocal n
        a = np.asarray(a, np.float32).reshape(a.shape[0], -1)
        full = np.zeros((P, a.shape[1]), np.float32)
        full[:a.shape[0]] = a
        parts.append(full)
        at[name] = (n, a.shape[1])
        n += a.shape[1]

    eye = np.eye(P)
    put("ident", eye)
    put("anti", eye[::-1])
    same = (p[:, None] // CH) == (p[None, :] // CH)
    put("tri_f", same & (p[:, None] <= p[None, :]))
    put("tri_b", same & (p[:, None] >= p[None, :]))
    put("strict_b", same & (p[:, None] > p[None, :]))
    c = np.arange(CH)
    put("pos", np.where(p[:, None] < CH, c[None] + 1, CH - c[None]))
    put("edge", np.stack([np.where(p[None, :] > p[:, None], NEG, 0), np.where(p[None, :] < p[:, None], NEG, 0)], 1))
    half = AHD // 2
    inv = (10000.0 ** (-np.arange(0, half, 2, dtype=np.float32) / half)).astype(np.float32)
    pos = np.arange(S)
    ang = np.stack([(pos // 64)[:, None].astype(np.float32) * inv, (pos % 64)[:, None].astype(np.float32) * inv], 1)
    ang = ang.reshape(NT, P, 2, half // 2).transpose(1, 0, 2, 3)
    put("cos", np.cos(ang))
    put("sin", np.sin(ang))
    keep = n
    w = np.arange(384)
    dist = 255 - w
    hot = np.zeros((BUCKETS + 1, GROUPS, 384))
    for g, dil in enumerate(DILS):
        ok = (dist >= 0) & (dist % dil == 0) & (dist <= N_BACK * dil)
        exact = BUCKETS // 2
        nf = np.maximum(dist, 1).astype(np.float32)
        large = exact + (np.log(nf / exact) / math.log(MAX_DIST / exact) * (BUCKETS - exact)).astype(np.int32)
        b = np.where(dist < exact, dist, np.minimum(large, BUCKETS - 1))
        hot[b[ok], g, w[ok]] = 1
        hot[BUCKETS, g, ~ok] = NEG
    put("hot", hot)
    t = np.arange(S)
    m = np.zeros((S, len(POOL_WINDOWS), S))
    for g, win in enumerate(POOL_WINDOWS):
        lo = np.maximum(t + 1 - win, 0)
        inside = (t[:, None] <= t[None, :]) & (t[:, None] >= lo[None, :])
        m[:, g] = inside / np.minimum(t + 1, win)[None, :] - np.eye(S)
    put("pool", m.reshape(NT, P, len(POOL_WINDOWS), S).transpose(1, 2, 0, 3))
    return np.concatenate(parts, 1), at, keep


class Count:

    def __init__(self, sem):
        self.sem, self.n, self.r, self.per = sem, 0, None, 0

    def up(self, k=1):
        self.n += k
        return self.n

    def at(self, back=0):
        v = self.n - back
        return v if self.r is None else v + self.r * self.per

    def loop(self, r, per):
        self.r, self.per = r, per

    def end(self, times):
        self.n += (times - 1) * self.per
        self.r = None


def build(nc, a, out, cst, at, keep, scratch, stop=9):
    f32, f32r = mybir.dt.float32, mybir.dt.float32r
    ALU, ACT, AX = mybir.AluOpType, mybir.ActivationFunctionType, mybir.AxisListType
    ctx = ExitStack()
    with ctx:
        sems = {}

        def sem(name):
            if name not in sems:
                sems[name] = ctx.enter_context(nc.semaphore(name))
            return sems[name]

        def sb(name, shape, dt=f32, where=ctx):
            return where.enter_context(nc.sbuf_tensor(name, shape, dt))

        def flat(t):
            return t[tuple([slice(None)] * len(t.shape))] if len(t.shape) == 2 else \
                t.rearrange({3: "p a b -> p (a b)", 4: "p a b c -> p (a b c)"}[len(t.shape)])

        def spread(v, dims):
            return bass.AP(tensor=v.tensor, offset=v.offset, ap=[list(v.ap[0])] + [list(d) for d in dims])

        C = sb("C", [P, keep])
        vecT = sb("vecT", [P, NROWS])
        cvec = sb("cvec", [P, 3, KT])
        mod = sb("mod", [P, 24 + 48 + 48 + 48 + 16])
        aff = sb("aff", [P, 8, KT])
        ones = sb("ones", [P, P])
        acc = sb("acc", [P, 2, 512])
        seed = sb("seed", [P, 512])
        stat = sb("stat", [P, 64])
        raw = [sb(f"raw{i}", [P, KT * UC]) for i in range(RAW)]
        whi = [sb(f"whi{i}", [P, KT * UC], f32r) for i in range(SPL)]
        wlo = [sb(f"wlo{i}", [P, KT * UC], f32r) for i in range(SPL)]
        bank = [ctx.enter_context(nc.psum_tensor(f"bank{i}", [P, 512], f32)) for i in range(8)]

        def const(name, rows=P):
            o, n = at[name]
            return C[0:rows, o:o + n]

        ident, anti = const("ident"), const("anti")

        xres = sb("xres", [P, NT, D])

        A = ExitStack()
        graw_a = [sb(f"graw_a{i}", [P, 2, 512], where=A) for i in range(GSA)]
        h_hi, h_lo = [sb(n, [P, KT, S], f32r, A) for n in ("h_hi", "h_lo")]
        mz_hi, mz_lo = [sb(n, [P, 4, S], f32r, A) for n in ("mz_hi", "mz_lo")]
        za = sb("za", [P, NT, 512], where=A)
        strip = [sb(f"strip{i}", [P, GROUPS, 256], where=A) for i in range(2)]
        prob = sb("prob", [P, 768], where=A)
        probT = [sb(f"probT{i}", [P, 4, P], where=A) for i in range(2)]
        trA = [flat(t) for t in probT]
        vrow = strip[0][0:NROWS, 0, 0:P]
        relb = strip[1][0:BUCKETS + 1, 0, 0:GROUPS * HEADS]
        pw = prob[:, 0:512].rearrange("p (g e) -> p g e", g=4)
        with ExitStack() as e:
            xrow = sb("xrow", [P, NT, D], where=e)
            hot = sb("hot", [BUCKETS + 1, GROUPS, 384], where=e)
            line = sb("line", [HEADS, GROUPS, 384], where=e)
        with ExitStack() as e:
            u_row = sb("u_row", [P, NT, 512], where=e)
            zpT = sb("zpT", [P, 4, S], where=e)
            poolM = sb("poolM", [P, 4, NT, S], where=e)
        gaT = sb("gaT", [P, KT, S], where=A)
        gpT = sb("gpT", [P, KT, S], where=A)
        with ExitStack() as e:
            qT = sb("qT", [P, GROUPS, 4, S], where=e)
            kT = sb("kT", [P, GROUPS, 4, S], where=e)
            vR = sb("vR", [P, GROUPS, NT, 512], where=e)
        with ExitStack() as e:
            at_hi, at_lo = [sb(n, [P, 4, S], f32r, e) for n in ("at_hi", "at_lo")]
            grow_a = sb("grow_a", [P, D], where=e)
            frow = sb("frow", [P, D], where=e)
            tmpa = sb("tmpa", [P, NT, D], where=e)
        A.close()
        T = 2 * S
        B = ExitStack()
        graw_b = [sb(f"graw_b{i}", [P, 2, 512], where=B) for i in range(GSB)]
        a_hi, a_lo = [sb(n, [P, KT, T], f32r, B) for n in ("a_hi", "a_lo")]
        trB = [sb(f"trB{i}", [P, T], where=B) for i in range(2)]
        with ExitStack() as e:
            gy = sb("gy", [P, 4, D], where=e)
            vv = sb("vv", [P, 4, 512], where=e)
            with ExitStack() as e2:
                crow = sb("crow", [P, 2, D], where=e2)
            qd = sb("qd", [P, 4, T], where=e)
            with ExitStack() as e2:
                lrT = sb("lrT", [RANK + 1, 2, T], where=e2)
                gkw = sb("gkw", [RANK + 1, 2, RH * DK], where=e2)
                lrR = sb("lrR", [P, 4, 2 * RANK], where=e2)
            ki = sb("ki", [P, 4, T], where=e)
            kir = sb("kir", [P, 4, P], where=e)
            with ExitStack() as e2:
                la = sb("la", [P, 4, 512], where=e2)
            kv = sb("kv", [P, 8, DV], where=e)
            sp = sb("sp", [P, 8, DV], where=e)
            dec = sb("dec", [P, 4, 8], where=e)
            lgam = sb("lgam", [P, 12], where=e)
            ssq = sb("ssq", [P, 3, 4, 8], where=e)
            ex = [sb(f"ex{i}", [P, T], where=e) for i in range(2)]
            sc = sb("sc", [P, 4, P], where=e)
            sc2 = sb("sc2", [P, 4, P], where=e)
        with ExitStack() as e:
            Y = sb("Y", [P, 4, D], where=e)
            bns = sb("bns", [P, 4, 2, 6], where=e)
            bna = sb("bna", [P, 4, 8], where=e)
            with ExitStack() as e2:
                cres = sb("cres", [P, 2, D], where=e2)
                with ExitStack() as e3:
                    grow = sb("grow", [P, 2, D], where=e3)
                    lrow = sb("lrow", [P, 2, D], where=e3)
                m_hi, m_lo = [sb(n, [P, KT, T], f32r, e2) for n in ("m_hi", "m_lo")]
                rel_ = sb("relu", [P, T], where=e2)
                sq_ = sb("sq", [P, T], where=e2)
            qrow = sb("qrow", [P, NT, D], where=e)
            krow = sb("krow", [P, 4, KVH, 2, AHD], where=e)
            vrow1 = sb("vrow1", [P, 4, UC], where=e)
            qT1 = sb("qT1", [P, QH // 2, S], where=e)
            kT1 = sb("kT1", [P, KVH, T], where=e)
            prob1 = [sb(f"prob1_{i}", [P, T], where=e) for i in range(2)]
            probT1 = [sb(f"probT1_{i}", [P, 4, P], where=e) for i in range(2)]
            sink = stat[:, 44:60]
        half_m = [flat(t)[:, 0:KT * S].rearrange("p (k n) -> p k n", k=KT) for t in (m_hi, m_lo)]
        B.close()

        def bf(w, n):
            return w[:, 0:n].bitcast(f32)

        def block(w, k0, kt, c0, cols):
            return w[k0:k0 + kt * P, c0:c0 + cols].rearrange("(k p) n -> p k n", p=P)

        units = []

        def add(w, c0, cols, banks, kt=KT, k0=0):
            units.append((block(w, k0, kt, c0, cols), kt, cols, banks))

        w_in = a["w_in"][0]
        ATT = GROUPS * 3 * 512
        for c0 in (ATT + 512, ATT + 768, ATT + 1024, ATT + 1280):
            add(w_in, c0, UC, 1)
        for c0 in range(0, ATT + 512, UC):
            add(w_in, c0, UC, 1)
        for c0 in range(ATT + 1536, W_IN, UC):
            add(w_in, c0, UC, 1)
        for w in ("w_attn_br", "w_pool_br"):
            for c0 in (0, 512):
                add(a[w][0], c0, 512, 2, kt=4)
        for c0 in range(0, D, UC):
            add(a["w_out"][0], c0, UC, 1)
        U_GATES, U_BR, U_OUT = 24, 32, 36
        U_EV = len(units)
        ev = a["ev_w_in_2"][0]
        add(ev, EV_IN - 2 * RANK, 2 * RANK, 1)
        for c0 in (1536, 1792, 2048, 2304, 2560, 2816, 0, 256, 512, 768, 1024, 1280):
            add(ev, c0, UC, 2)
        U_EVO = len(units)
        for c0 in range(0, D, UC):
            add(a["ev_w_out_2"][0], c0, UC, 2)
        U_M0 = len(units)
        for r in range(4):
            for j in range(4):
                add(a["mlp_w1_2"][0], 1024 * r + UC * j, UC, 2)
            for j in range(4):
                add(a["mlp_w2_2"][0], UC * j, UC, 2, k0=1024 * r)
        U_QKV = len(units)
        qkv = a["od_w_qkv_2"][0]
        add(qkv, D, UC, 2)
        add(qkv, D + UC, UC, 2)
        for c0 in range(0, D, UC):
            add(qkv, c0, UC, 1)
        U_OD = len(units)
        for c0 in range(0, D, UC):
            add(a["od_w_out_2"][0], c0, UC, 1)
        U_M1 = len(units)
        for r in range(4):
            for j in range(4):
                add(a["mlp_w1_2"][1], 1024 * r + UC * j, UC, 1)
            for j in range(4):
                add(a["mlp_w2_2"][1], UC * j, UC, 1, k0=1024 * r)

        before = [0]
        for un in units:
            before.append(before[-1] + un[3])

        vblocks = [(a["w_ada"][0], a["b_ada"][0], n, [(0, 4 * n)]) for n in range(6)]
        M0, M0C, M1, M1C = 24, 72, 120, 168
        vblocks += [(a["w_mod_2"][0], a["b_mod_2"][0], n, [(1, M0 + 4 * n), (2, M0C + 4 * n)]) for n in range(12)]
        vblocks += [(a["w_mod_2"][1], a["b_mod_2"][1], n,
                     [(1, M1 + 4 * n)] + ([(2, M1C + 4 * n)] if n < 4 else [])) for n in range(12)]
        vops = [0]
        for vb in vblocks:
            for _ in range(4):
                vops.append(vops[-1] + 2 * len(vb[3]))
        Q_B = 56

        def vslot(q):
            return graw_a[q % GSA] if q < Q_B else graw_b[q % GSB]

        steps = [(qt, h) for qt in range(NT) for h in range(HEADS)]

        def rounds(n):
            return n if n < HEADS else HEADS + 2 * (n - HEADS)

        PRE_Q = 16
        FILLS = 5

        UNIT_Q = {u: 0 if u == U_EV else 1 for u in range(U_EV, U_M0)}
        HEAD_Q = 2
        LOOP_Q = [[0, 1], [2], [3], [4], [5], [6], [7], []]
        LN_TILES = [4, 4, 2, 2]
        res_mul = sem("res_mul")
        res_parts = [(0, i) for i in range(4)] + [(1, i) for i in (2, 3)] + [(k, i) for k in (2, 3) for i in range(2)]
        TILES = 4

        def at_(v, r, per):
            return v if r is None else v + r * per

        def taken(eng, b):
            eng.wait_ge(free[b % 4], b // 4 + 1)

        def all_taken(eng, b):
            for i in range(min(4, b)):
                taken(eng, b - 1 - i)

        load_w, load_c, load_v, load_x, load_f = sem("load_w"), sem("load_c"), sem("load_v"), sem("load_x"), sem("load_f")
        raw_full = [sem(f"raw_full{i}") for i in range(RAW)]
        graw_full = [sem(f"graw_full{i}") for i in range(GSA + GSB)]
        seed_full = sem("seed_full")
        hi_done, lo_done, tile_done = sem("hi_done"), sem("lo_done"), sem("tile_done")
        free = [sem(f"bank_free{i}") for i in range(4)]
        vsum, red_done, mod_done = sem("vsum"), sem("red_done"), sem("mod_done")
        filled = sem("filled")
        tr_full, tr_tmp, tr_hi, tr_lo = sem("tr_full"), sem("tr_tmp"), sem("tr_hi"), sem("tr_lo")
        vchain = sem("vector_chain")
        vec_t, vec_c, cvec_done = sem("vec_t"), sem("vec_c"), sem("cvec_done")
        line_mm, line_done, line_out, strip_full = sem("line_mm"), sem("line_done"), sem("line_out"), [sem("strip_full0"), sem("strip_full1")]
        sq_sum, root, x_scaled = sem("sq_sum"), sem("root"), sem("x_scaled")
        mz_part = sem("mz_part")
        pool_mm, pool_ev, mz_tmp = sem("pool_mm"), sem("pool_ev"), sem("mz_tmp")
        at_s, at_mx, at_p, at_t, at_pt, at_pv, at_z = [sem(n) for n in ("at_s", "at_mx", "at_p", "at_t", "at_pt", "at_pv", "at_z")]
        merged, merged_hi, merged_lo = sem("merged"), sem("merged_hi"), sem("merged_lo")
        rowb, rowb_done = sem("rowb"), sem("rowb_done")
        x_new = sem("x_new")
        load_ctx, load_gk, load_th, load_ln, load_cr = [sem(n) for n in ("load_ctx", "load_gk", "load_th", "load_ln", "load_cr")]
        lr_t, lr_ev, z_mm, la_done, lg_done = [sem(n) for n in ("lr_t", "lr_ev", "z_mm", "la_done", "lg_done")]
        bc_mm, ex_done, qk_done, kt_mm, kir_done, kv_mm, kv_done, s_mm, sc_done, sp_done, o_mm, ss_done, gy_done = \
            [sem(n) for n in ("bc_mm", "ex_done", "qk_done", "kt_mm", "kir_done", "kv_mm", "kv_done", "s_mm",
                              "sc_done", "sp_done", "o_mm", "ss_done", "gy_done")]
        achain, y_scaled, y_zero = sem("act_chain"), sem("y_scaled"), sem("y_zero")
        ln_var, ln_root, ln_n = sem("ln_var"), sem("ln_root"), sem("ln_n")
        sq_done, hid_hi, hid_lo = sem("sq_done"), sem("hid_hi"), sem("hid_lo")
        out_done = sem("out_done")
        load_sk, kq_t, kq_ev = sem("load_sk"), sem("kq_t"), sem("kq_ev")
        wa_s, wa_max, wa_exp, wa_t, wa_pv, wa_o = [
            sem(n) for n in ("wa_s", "wa_max", "wa_exp", "wa_t", "wa_pv", "wa_o")]
        wa_pt = [sem(f"wa_pt{i}") for i in range(2)]
        wsteps = [(qt, h) for qt in range(NT) for h in range(QH)]
        block_ = ctx.enter_context(nc.Block())

        def gfull(q):
            if q < Q_B:
                return graw_full[q % GSA], 16 * (q // GSA + 1)
            return graw_full[GSA + q % GSB], 16 * ((q - Q_B) // GSB + 1)

        @block_.sync
        def _(sp_):
            sp_.dma_start(C[:, :], cst[:, 0:keep]).then_inc(load_c, 16)
            for name, rows, src in (("norm_g", 8, a["norm_g"]), ("pool_scale", 4, a["pool_scale"]),
                                    ("ln_g", 32, a["ln_g_2"]), ("ln_b", 32, a["ln_b_2"]), ("c", 8, a["c"]),
                                    ("c_2", 8, a["c_2"]), ("c_ctx", 8, a["c_ctx_2"]), ("final_g", 8, a["final_g"]),
                                    ("gla_g", 1, a["ev_gla_norm_g_2"])):
                n = int(np.prod(src.shape))
                v = bass.AP(tensor=src.tensor, offset=src.offset, ap=[[P, rows], [1, P]])
                sp_.dma_start(vrow[ROWS[name]:ROWS[name] + rows, :], v).then_inc(load_v, 16)
            sp_.dma_start(xres[:, :, :], a["x"][0].rearrange("(m p) n -> p m n", p=P)).then_inc(load_x, 16)
            sp_.dma_start(hot[:, :, :], cst[0:BUCKETS + 1, at["hot"][0]:at["hot"][0] + GROUPS * 384]
                          .rearrange("p (g w) -> p g w", g=GROUPS)).then_inc(load_w, 16)
            sp_.wait_ge(filled, FILLS)
            sp_.dma_start(relb[0:BUCKETS, :], a["rel_bias"]).then_inc(load_w, 16)

            def load(u):
                src, kt, cols, _ = units[u]
                if u >= RAW:
                    sp_.wait_ge(lo_done, u - RAW + 1)
                sp_.dma_start(raw[u % RAW][:, 0:kt * cols].rearrange("p (k n) -> p k n", k=kt), src)\
                    .then_inc(raw_full[u % RAW], 16)

            for u in range(U_EV + LEAD):
                load(u)
            sp_.wait_ge(x_new, 6)
            sp_.dma_start(crow[:, :, :], a["ctx_2"][0].rearrange("(m p) n -> p m n", p=P)).then_inc(load_ctx, 16)
            for d in range(2):
                sp_.dma_start(gkw[0:RANK, d, :], a["ev_gla_gk_w_2"][0, d]).then_inc(load_gk, 16)
                sp_.dma_start(gkw[RANK:RANK + 1, d, :], a["ev_gla_gk_b_2"][0, d:d + 1]).then_inc(load_gk, 16)
                th = a["ev_ret_theta_2"]
                sp_.dma_start(lgam[64 * d:64 * d + 64, 0:4],
                              bass.AP(tensor=th.tensor, offset=th.offset + 4 * d, ap=[[0, 64], [1, 4]])).then_inc(load_th, 16)
            for u in range(U_EV + LEAD, U_EVO):
                load(u)
            for u in range(U_EVO, U_EVO + LEAD):
                load(u)

            def ln_rows(l, s):
                for i, v in enumerate((a["ln_g_2"], a["ln_b_2"])):
                    sp_.dma_start(lrow[:, i, :], bass.AP(tensor=v.tensor, offset=v.offset + (2 * l + s) * D,
                                                         ap=[[0, P], [1, D]])).then_inc(load_ln, 16)

            sp_.wait_ge(tr_full, 28)
            sp_.dma_start(cres[:, :, :], a["ctx_2"][0].rearrange("(m p) n -> p m n", p=P)).then_inc(load_cr, 16)
            ln_rows(0, 0)
            for u in range(U_EVO + LEAD, U_M0):
                load(u)

            def mlp_loads(l, u0):
                with sp_.Fori(0, 4) as r:
                    for j in range(8):
                        u = u0 + j
                        w = a["mlp_w1_2"][l][:, bass.ds(r * 1024 + UC * j, UC)] if j < 4 else \
                            a["mlp_w2_2"][l][bass.ds(r * 1024, 1024), UC * (j - 4):UC * (j - 3)]
                        sp_.wait_ge(lo_done, at_(u - RAW + 1, r, 8))
                        sp_.dma_start(raw[u % RAW][:, :].rearrange("p (k n) -> p k n", k=KT),
                                      w.rearrange("(k p) n -> p k n", p=P)).then_inc(raw_full[u % RAW], 16)

            mlp_loads(0, U_M0)
            for u in range(U_QKV, U_QKV + LEAD):
                load(u)
            sp_.wait_ge(tile_done, before[U_QKV])
            ln_rows(0, 1)
            sk = a["od_sink_2"]
            sp_.dma_start(sink, bass.AP(tensor=sk.tensor, offset=sk.offset, ap=[[0, P], [1, QH]])).then_inc(load_sk, 16)
            for u in range(U_QKV + LEAD, U_M1):
                load(u)
            sp_.wait_ge(tr_full, 52)
            ln_rows(1, 0)
            mlp_loads(1, U_M1)
            sp_.wait_ge(tile_done, before[U_M1 + 32])
            ln_rows(1, 1)
            for m in range(NT):
                sp_.wait_ge(res_mul, 2 * (len(res_parts) - NT + m + 1))
                sp_.dma_start(out[0, m * P:(m + 1) * P, :], xres[:, m, :]).then_inc(out_done, 16)
            sp_.wait_ge(out_done, 16 * NT)
            sp_.wait_ge(line_out, 16)

        @block_.gpsimd
        def _(pool):
            pool.memset(seed[:, :], 0.0).then_inc(filled, 1)
            pool.memset(ones[:, :], 1.0).then_inc(filled, 1)
            pool.memset(relb, 1.0).then_inc(filled, 1)
            pool.memset(stat[:, 40:41], EPS_RMS).then_inc(filled, 1)
            pool.memset(stat[:, 41:42], EPS_LN).then_inc(filled, 1)
            pool.wait_ge(filled, FILLS)

            def load_q(q):
                w, b, n, vecs = vblocks[q // 4]
                if q % 4 == 0:
                    if q:
                        pool.wait_ge(vsum, vops[q - 3])
                    bias = bass.AP(tensor=b.tensor, offset=b.offset + 512 * n, ap=[[512, 1], [1, 512]])
                    pool.dma_start(seed[0:1, :], bias).then_inc(seed_full, 16)
                ring = GSA if q < Q_B else GSB
                if q >= ring:
                    pool.wait_ge(vsum, vops[q - ring + 1])
                pool.dma_start(vslot(q)[:, :, :], block(w, (q % 4) * 2 * P, 2, 512 * n, 512)).then_inc(gfull(q)[0], 16)

            for q in range(PRE_Q):
                load_q(q)
            pool.wait_ge(line_done, 3)
            pool.dma_start(scratch.rearrange("h (g w) -> h g w", g=GROUPS), line[:, :, :]).then_inc(line_out, 16)
            pool.wait_ge(tr_full, KT)
            pool.wait_ge(line_mm, 3)
            pool.wait_ge(line_out, 16)
            pool.dma_start(poolM[:, :, :, :], cst[:, at["pool"][0]:at["pool"][0] + at["pool"][1]]
                           .rearrange("p (g s t) -> p g s t", g=4, s=NT)).then_inc(load_f, 16)
            pool.dma_start(pw, a["pool_w"][0].rearrange("g c e -> c g e")).then_inc(load_f, 16)
            for u in range(U_GATES):
                load_q(PRE_Q + u)
            for n, (qt, h) in enumerate(steps):
                if n >= 2:
                    pool.wait_ge(at_s, n - 1)
                pool.dma_start(strip[n % 2][:, :, :],
                               bass.AP(tensor=scratch.tensor, offset=scratch.offset + h * GROUPS * 384,
                                       ap=[[1, P], [384, GROUPS], [1, 256]])).then_inc(strip_full[n % 2], 16)
                load_q(PRE_Q + U_GATES + n)
            pool.wait_ge(at_s, len(steps))
            pool.wait_ge(at_pv, rounds(len(steps)))
            fg = a["final_g"]
            Qn = PRE_Q + U_GATES + len(steps)
            pool.dma_start(frow[:, :], bass.AP(tensor=fg.tensor, offset=fg.offset, ap=[[0, P], [1, D]])).then_inc(load_f, 16)

            pool.wait_ge(x_new, 6)
            pool.memset(lrT[:, :, :], 1.0).then_inc(filled, 1)
            q = Qn
            while q < 88:
                load_q(q)
                q += 1

            done = Count(res_mul)

            def residual(l, s, parts):
                k = 2 * l + s
                pool.wait_ge(load_ln, 32 * (k + 1))
                for i, dst in parts:
                    pool.wait_ge(ln_n, sum(LN_TILES[:k]) + i + 1)
                    pool.tensor_tensor(dst, Y[:, i, :], lrow[:, 0, :], ALU.mult).then_inc(res_mul, 1)
                    pool.wait_ge(res_mul, done.up())
                    pool.tensor_tensor(dst, dst, lrow[:, 1, :], ALU.add).then_inc(res_mul, 1)
                    done.up()

            residual(0, 0, [(i, cres[:, i, :]) for i in range(2)] + [(i + 2, xres[:, i, :]) for i in range(2)])
            pool.wait_ge(tr_full, 36)
            pool.memset(Y[:, :, :], 0.0).then_inc(y_zero, 1)
            with pool.Fori(0, 4) as r:
                for j in range(8):
                    n = 22 + j // 4
                    qq = 88 + j
                    if j % 4 == 0:
                        pool.wait_ge(vsum, at_(vops[88] + 2 * (j - 3), r, 16))
                        b = a["b_mod_2"][1:2, bass.ds(r * 1024 + 512 * (n - 18), 512)]
                        pool.dma_start(seed[0:1, :], b).then_inc(seed_full, 16)
                    pool.wait_ge(vsum, at_(vops[88] + 2 * (j - 1), r, 16))
                    w = a["w_mod_2"][1][(qq % 4) * 256:(qq % 4) * 256 + 256, bass.ds(r * 1024 + 512 * (n - 18), 512)]
                    pool.dma_start(vslot(qq)[:, :, :], w.rearrange("(k p) n -> p k n", p=P)).then_inc(gfull(qq)[0], 16)
            residual(0, 1, [(i + 2, xres[:, i, :]) for i in range(2)])
            residual(1, 0, [(i, xres[:, i, :]) for i in range(2)])
            pool.wait_ge(tr_full, 60)
            pool.memset(Y[:, 0:NT, :], 0.0).then_inc(y_zero, 1)
            residual(1, 1, [(i, xres[:, i, :]) for i in range(2)])
            assert done.n == 2 * len(res_parts)

        @block_.tensor
        def _(pe):
            def col_unit(u, hi, lo, T, b):
                _, kt, cols, banks = units[u]
                wh, wl = [w[u % SPL][:, 0:kt * cols].rearrange("p (k n) -> p k n", k=kt) for w in (whi, wlo)]
                pe.wait_ge(lo_done, u + 1)
                per = 512 // T
                for n in range(cols // P):
                    bt = b + n // per
                    if n % per == 0 and bt >= 4:
                        pe.wait_ge(free[bt % 4], bt // 4)
                    o = bank[bt % 4][:, (n % per) * T:(n % per + 1) * T]
                    for k in range(kt):
                        for i, (w, x) in enumerate(((wh, hi), (wl, hi), (wh, lo))):
                            mm = nc.tensor.matmul(o, w[:, k, n * P:(n + 1) * P], x[:, k, 0:T],
                                                  start=(k == 0 and i == 0), stop=(k == kt - 1 and i == 2))
                    if n % per == per - 1:
                        mm.then_inc(tile_done, 1)

            def row_unit(u, hi, lo, tiles, b):
                _, kt, cols, banks = units[u]
                wh, wl = [w[u % SPL][:, 0:kt * cols].rearrange("p (k n) -> p k n", k=kt) for w in (whi, wlo)]
                pe.wait_ge(lo_done, u + 1)
                for i, m in enumerate(tiles):
                    bt = b + i // 2
                    if i % 2 == 0 and bt >= 4:
                        pe.wait_ge(free[bt % 4], bt // 4)
                    o = bank[bt % 4][:, (i % 2) * UC:(i % 2 + 1) * UC]
                    for k in range(kt):
                        for j, (w, x) in enumerate(((wh, hi), (wh, lo), (wl, hi))):
                            mm = nc.tensor.matmul(o, x[:, k, m * P:(m + 1) * P], w[:, k, :],
                                                  start=(k == 0 and j == 0), stop=(k == kt - 1 and j == 2))
                    if i % 2 == 1:
                        mm.then_inc(tile_done, 1)

            def reduce_block(n):
                vecs = vblocks[n][3]
                pe.wait_ge(vsum, vops[4 * n + 4])
                if n:
                    pe.wait_ge(mod_done, n)
                for v in range(len(vecs)):
                    for s in range(4):
                        mm = nc.tensor.matmul(bank[7][:, 4 * v + s:4 * v + s + 1], acc[:, v, s * P:(s + 1) * P],
                                              ones[:, 0:1], start=True, stop=True)
                mm.then_inc(red_done, 1)

            def transposes(t0, kts, T, src):
                for kt in range(kts):
                    t = t0 + kt
                    if t >= 2:
                        pe.wait_ge(tr_tmp, t - 1)
                    for i in range(T // P):
                        mm = nc.tensor.transpose(bank[4 + t % 2][:, i * P:(i + 1) * P], src(i, kt), ident)
                    mm.then_inc(tr_full, 1)

            def broadcast_row(col, b0):
                for k in range(KT):
                    mm = nc.tensor.matmul(bank[b0 + k // 4][:, (k % 4) * P:(k % 4 + 1) * P],
                                          spread(col(k), [[0, P]]), ident, start=True, stop=True)
                mm.then_inc(rowb, 1)

            pend = []
            qn = [0]

            def event(quarters):
                for n in pend:
                    reduce_block(n)
                pend.clear()
                if quarters and (qn[0] + quarters) // 4 > qn[0] // 4:
                    pend.append((qn[0] + quarters) // 4 - 1)
                qn[0] += quarters

            pe.wait_ge(load_c, 16)
            pe.wait_ge(load_v, 16 * 9)
            nc.tensor.transpose(bank[6][:, 0:NROWS], vrow, ident[0:NROWS, 0:NROWS]).then_inc(vec_t, 1)
            pe.wait_ge(load_w, 32)
            for g in range(GROUPS):
                if g == 2:
                    pe.wait_ge(vec_c, 1)
                nc.tensor.matmul(bank[4 + g][0:HEADS, 0:384], relb[:, g * HEADS:(g + 1) * HEADS], hot[:, g, :],
                                 start=True, stop=True).then_inc(line_mm, 1)
            pe.wait_ge(filled, FILLS)
            for n in range(4):
                reduce_block(n)
            pe.wait_ge(line_done, 3)
            pe.wait_ge(x_scaled, 1)
            transposes(0, KT, S, lambda i, k: xrow[:, i, k * P:(k + 1) * P])
            pe.wait_ge(tr_lo, KT)
            vdone = 4
            for u in range(U_GATES):
                if u in (0, 1) or (u >= 4 and (u - 4) % 6 in (4, 5) and u < 22) or u >= 22:
                    row_unit(u, h_hi, h_lo, range(NT), before[u])
                else:
                    col_unit(u, h_hi, h_lo, S, before[u])
                if u >= 4 and u % 4 == 0:
                    reduce_block(vdone)
                    vdone += 1
                if u == 3:
                    pe.wait_ge(load_f, 32)
                    all_taken(pe, 2)
                    for g in range(4):
                        for s in range(NT):
                            mm = nc.tensor.matmul(bank[4 + g // 2][:, (g % 2) * S:(g % 2 + 1) * S],
                                                  u_row[:, s, g * P:(g + 1) * P], poolM[:, g, s, :],
                                                  start=(s == 0), stop=(s == NT - 1))
                        if g % 2:
                            mm.then_inc(pool_mm, 1)
                    for g in range(4):
                        pe.wait_ge(pool_ev, g // 2 + 1)
                        mm = nc.tensor.matmul(bank[6 if g < 2 else 4][:, (g % 2) * S:(g % 2 + 1) * S], pw[:, g, :],
                                              trA[g // 2][:, (g % 2) * S:(g % 2 + 1) * S], start=True, stop=True)
                        if g % 2:
                            mm.then_inc(pool_mm, 1)

            pe.wait_ge(mz_tmp, 2)
            all_taken(pe, before[U_GATES])
            for n, (qt, h) in enumerate(steps):
                W = P * (qt + 1)
                lane = slice(64 * (h % 2), 64 * (h % 2) + 64)
                if n:
                    pe.wait_ge(at_z, n)
                pe.wait_ge(strip_full[n % 2], 16 * (n // 2 + 1))
                for g in range(GROUPS):
                    o = bank[4][:, g * W:(g + 1) * W] if g < 2 else bank[5][:, 0:W]
                    nc.tensor.matmul(o, qT[lane, g, h // 2, qt * P:(qt + 1) * P], kT[lane, g, h // 2, 0:W],
                                     start=True, stop=False)
                    mm = nc.tensor.matmul(o, anti, strip[n % 2][:, g, 256 - W:256], start=False, stop=True)
                mm.then_inc(at_s, 1)
                if n < 8:
                    u = U_GATES + n
                    col_unit(u, h_hi, h_lo, S, before[u])
                if n % 4 == 0:
                    reduce_block(vdone)
                    vdone += 1
                pe.wait_ge(at_p, n + 1)
                for j in range(qt + 1):
                    rc = rounds(n) + j
                    if rc:
                        pe.wait_ge(at_pt, rc)
                    for b in range(3):
                        blk = 3 * j + b
                        mm = nc.tensor.transpose(bank[6][:, b * P:(b + 1) * P], prob[:, blk * P:(blk + 1) * P], ident)
                    mm.then_inc(at_t, 1)
                    pe.wait_ge(at_pt, rc + 1)
                    for b in range(3):
                        blk = 3 * j + b
                        g, kb = divmod(blk, qt + 1)
                        mm = nc.tensor.matmul(bank[5][:, 256:256 + HD], probT[rc % 2][:, b, :],
                                              vR[:, g, kb, h * HD:(h + 1) * HD],
                                              start=(blk == 0), stop=(blk == 3 * (qt + 1) - 1))
                    mm.then_inc(at_pv, 1)
            pe.wait_ge(at_z, len(steps))
            transposes(8, 4, S, lambda i, k: za[:, i, k * P:(k + 1) * P])
            pe.wait_ge(tr_lo, 12)
            pe.wait_ge(mz_part, 2)
            for u in (32, 33):
                col_unit(u, at_hi, at_lo, S, before[u])
            for u in (34, 35):
                col_unit(u, mz_hi, mz_lo, S, before[u])
            reduce_block(vdone)
            broadcast_row(lambda k: mod[:, 16 + k:17 + k], 4)
            pe.wait_ge(merged_lo, 1)
            for u in range(36, 40):
                row_unit(u, h_hi, h_lo, range(NT), before[u])

            qn[0] = PRE_Q + U_GATES + len(steps)
            pe.wait_ge(x_new, 6)
            pe.wait_ge(load_ctx, 16)
            transposes(12, KT, T, lambda i, k: crow[:, i, k * P:(k + 1) * P] if i < 2 else xres[:, i - 2, k * P:(k + 1) * P])
            pe.wait_ge(tr_lo, 20)
            u = U_EV
            b = before[u]
            wh, wl = [w[u % SPL][:, 0:KT * 32].rearrange("p (k n) -> p k n", k=KT) for w in (whi, wlo)]
            pe.wait_ge(lo_done, u + 1)
            pe.wait_ge(free[b % 4], b // 4)
            for m in range(TILES):
                for k in range(KT):
                    for j, (w, x) in enumerate(((wh, a_hi), (wh, a_lo), (wl, a_hi))):
                        mm = nc.tensor.matmul(bank[b % 4][:, m * 32:m * 32 + 32], x[:, k, m * P:(m + 1) * P], w[:, k, :],
                                              start=(k == 0 and j == 0), stop=(k == KT - 1 and j == 2))
            mm.then_inc(tile_done, 1)
            taken(pe, b)
            for d in range(2):
                for i in range(TILES):
                    mm = nc.tensor.transpose(bank[4 + d][0:RANK, i * P:(i + 1) * P], lrR[:, i, RANK * d:RANK * d + RANK], ident)
            mm.then_inc(lr_t, 1)
            pe.wait_ge(lr_ev, 2)
            pe.wait_ge(load_gk, 64)
            for i in range(TILES):
                if i >= 2:
                    pe.wait_ge(la_done, i - 1)
                for d in range(2):
                    mm = nc.tensor.matmul(bank[4 + i % 2][:, 256 * d:256 * d + 256], lrT[:, d, i * P:(i + 1) * P], gkw[:, d, :],
                                          start=True, stop=True)
                mm.then_inc(z_mm, 1)
            event(UNIT_Q[U_EV])

            def decay_sums(h):
                if h:
                    pe.wait_ge(ex_done, 2 * h)
                for i in range(TILES):
                    for d, tri in ((0, "tri_f"), (1, "tri_b")):
                        mm = nc.tensor.matmul(bank[6][64 * d:64 * d + 64, i * P:(i + 1) * P],
                                              la[:, i, 256 * d + DK * h:256 * d + DK * h + DK], const(tri),
                                              start=True, stop=True)
                mm.then_inc(bc_mm, 1)

            def head(hd):
                gla, h = hd < RH, hd % RH
                if hd:
                    pe.wait_ge(gy_done, hd)
                    pe.wait_ge(ss_done, hd)
                pe.wait_ge(qk_done, 4 if gla else 8)
                for i in range(TILES):
                    mm = nc.tensor.transpose(bank[6][:, i * P:(i + 1) * P], ki[:, h, i * P:(i + 1) * P], ident)
                mm.then_inc(kt_mm, 1)
                pe.wait_ge(kir_done, hd + 1)
                for c in range(8):
                    rows = slice(64 * (c % 2), 64 * (c % 2) + 64)
                    mm = nc.tensor.matmul(bank[4 + c % 2][:, (c // 2) * DV:(c // 2 + 1) * DV], kir[rows, c // 2, :],
                                          vv[rows, c // 2, h * DV:(h + 1) * DV], start=True, stop=True)
                mm.then_inc(kv_mm, 1)
                pe.wait_ge(kv_done, 2 * (hd + 1))
                for d in range(2):
                    rows = slice(64 * d, 64 * d + 64)
                    for i in range(TILES):
                        mm = nc.tensor.matmul(bank[4 + d][:, i * P:(i + 1) * P], ki[rows, h, i * P:(i + 1) * P],
                                              qd[rows, h, i * P:(i + 1) * P], start=True, stop=True)
                mm.then_inc(s_mm, 1)
                pe.wait_ge(sc_done, hd + 1)
                pe.wait_ge(sp_done, hd + 1)
                for i in range(TILES):
                    nc.tensor.matmul(bank[6][:, i * P:(i + 1) * P], sc[:, i, :], vv[:, i, h * DV:(h + 1) * DV],
                                     start=True, stop=False, skip_group_check=True)
                    for half in range(2):
                        c = 2 * i + half
                        mm = nc.tensor.matmul(bank[6][64 * half:64 * half + 64, i * P:(i + 1) * P], qd[:, h, c * CH:(c + 1) * CH],
                                              sp[:, c, :], start=False, stop=True, skip_group_check=True)
                mm.then_inc(o_mm, 1)

            def mixer_units(u0):
                for u in range(u0, u0 + 6):
                    if u - u0 < 2:
                        col_unit(u, a_hi, a_lo, T, before[u])
                    else:
                        row_unit(u, a_hi, a_lo, range(TILES), before[u])
                    event(UNIT_Q[u])

            mixer_units(U_EV + 1)
            all_taken(pe, before[U_EV + 7])
            for h in range(RH):
                decay_sums(h)
            for hd in range(4):
                head(hd)
                event(HEAD_Q)
            mixer_units(U_EV + 7)
            all_taken(pe, before[U_EV + 13])
            for hd in range(4, 8):
                head(hd)
                event(HEAD_Q)
            pe.wait_ge(y_scaled, 1)
            transposes(20, KT, T, lambda i, k: gy[:, i, k * P:(k + 1) * P])
            pe.wait_ge(tr_lo, 28)
            for u in range(U_EVO, U_M0):
                row_unit(u, a_hi, a_lo, range(TILES), before[u])
                event(UNIT_Q[u])
            assert qn[0] == 88 and pend == [21], (qn, pend)
            event(0)

            def gate_rows(cols, n0):
                for i, c in enumerate(cols):
                    if n0 + i > 1:
                        pe.wait_ge(rowb_done, n0 + i)
                    broadcast_row(lambda k: mod[:, c + k:c + k + 1], 4)

            gate_rows((M0C + 16, M0 + 16), 1)
            pe.wait_ge(ln_n, 4)
            transposes(28, KT, T, lambda i, k: Y[:, i, k * P:(k + 1) * P])
            pe.wait_ge(tr_lo, 36)

            def mlp(u0, hi, lo, Tn, mh, ml, hid0, vecs):
                per, tiles = 8 * Tn // 256, Tn // P
                ht = 4 * Tn // 256

                def round_(r):
                    for j in range(8):
                        u, b = u0 + j, before[u0 + j]
                        wh, wl = [w[u % SPL][:, :].rearrange("p (k n) -> p k n", k=KT) for w in (whi, wlo)]
                        pe.wait_ge(lo_done, at_(u + 1, r, 8))
                        if j == 4:
                            pe.wait_ge(hid_lo, at_(hid0 + ht, r, ht))
                        n_out = 2 if j < 4 else tiles
                        per_bank = 512 // Tn if j < 4 else 2
                        for n in range(n_out):
                            bt = b + n // per_bank
                            if n % per_bank == 0:
                                pe.wait_ge(free[bt % 4], at_(bt // 4, r, per // 4))
                            w = 512 // per_bank
                            o = bank[bt % 4][:, (n % per_bank) * w:(n % per_bank + 1) * w]
                            for k in range(KT):
                                if j < 4:
                                    trio = [(wh[:, k, n * P:(n + 1) * P], hi[:, k, 0:Tn]), (wl[:, k, n * P:(n + 1) * P], hi[:, k, 0:Tn]),
                                            (wh[:, k, n * P:(n + 1) * P], lo[:, k, 0:Tn])]
                                else:
                                    trio = [(mh[:, k, n * P:(n + 1) * P], wh[:, k, :]), (mh[:, k, n * P:(n + 1) * P], wl[:, k, :]),
                                            (ml[:, k, n * P:(n + 1) * P], wh[:, k, :])]
                                for i, (x, y) in enumerate(trio):
                                    mm = nc.tensor.matmul(o, x, y, start=(k == 0 and i == 0), stop=(k == KT - 1 and i == 2))
                            if n % per_bank == per_bank - 1:
                                mm.then_inc(tile_done, 1)
                        if vecs and j in (3, 7):
                            n = 22 + j // 4
                            pe.wait_ge(vsum, at_(vops[88] + 8 * (j // 4 + 1), r, 16))
                            pe.wait_ge(mod_done, at_(n, r, 2))
                            for s_ in range(4):
                                mm = nc.tensor.matmul(bank[7][:, s_:s_ + 1], acc[:, 0, s_ * P:(s_ + 1) * P], ones[:, 0:1],
                                                      start=True, stop=True)
                            mm.then_inc(red_done, 1)

                with pe.Fori(0, 4) as r:
                    round_(r)

            mlp(U_M0, a_hi, a_lo, T, m_hi, m_lo, 0, True)
            gate_rows((M0C + 40, M0 + 40), 3)
            pe.wait_ge(ln_n, 8)
            transposes(36, KT, T, lambda i, k: Y[:, i, k * P:(k + 1) * P])

            pe.wait_ge(tr_lo, 44)

            def transpose_q(j):
                taken(pe, before[U_QKV + 2 + j])
                if j:
                    pe.wait_ge(kq_ev, KVH)
                for p_ in range(2):
                    for m in range(NT):
                        mm = nc.tensor.transpose(bank[4 + j][:, (NT * p_ + m) * P:(NT * p_ + m + 1) * P],
                                                 qrow[:, m, (2 * j + p_) * P:(2 * j + p_ + 1) * P], ident)
                mm.then_inc(kq_t, 1)

            for u in range(U_QKV, U_OD):
                j = u - U_QKV - 2
                row_unit(u, a_hi, a_lo, range(TILES) if j < 0 else range(NT, TILES), before[u])
                if j == 0:
                    all_taken(pe, before[U_QKV + 1])
                    pe.wait_ge(mod_done, len(vblocks))
                    for n in range(KVH):
                        for m in range(TILES):
                            mm = nc.tensor.transpose(bank[4 + n][:, m * P:(m + 1) * P],
                                                     krow[:, m, n, :, :].rearrange("p a b -> p (a b)"), ident)
                        mm.then_inc(kq_t, 1)
                    pe.wait_ge(kq_ev, KVH)
                if j >= 1:
                    transpose_q(j - 1)
            transpose_q(3)
            all_taken(pe, before[U_OD])
            for n in range(len(wsteps) + 2):
                if n < len(wsteps):
                    qt, h = wsteps[n]
                    lane = slice(64 * (h % 2), 64 * (h % 2) + 64)
                    pe.wait_ge(kq_ev, KVH + h // 4 + 1)
                    pe.wait_ge(kq_ev, KVH + 1 + n % 2)
                    if n >= 2:
                        pe.wait_ge(wa_exp, n - 1)
                    o = bank[4 + n % 2]
                    nc.tensor.matmul(o[:, :], qT1[lane, h // 2, qt * P:(qt + 1) * P], kT1[lane, h // 4, :],
                                     start=True, stop=False, skip_group_check=True)
                    cut = S + P * (1 - qt)
                    nc.tensor.matmul(o[:, cut:cut + P], ident, const("edge")[:, qt * P:(qt + 1) * P],
                                     start=False, stop=True, skip_group_check=True).then_inc(wa_s, 1)
                if 1 <= n <= len(wsteps):
                    i = n - 1
                    pe.wait_ge(wa_exp, i + 1)
                    pe.wait_ge(kq_ev, 8)
                    if i >= 2:
                        pe.wait_ge(wa_pt[i % 2], i // 2)
                    for b in range(4):
                        mm = nc.tensor.transpose(bank[6 + i % 2][:, b * P:(b + 1) * P], prob1[i % 2][:, b * P:(b + 1) * P], ident)
                    mm.then_inc(wa_t, 1)
                if n >= 2:
                    i = n - 2
                    qt, h = wsteps[i]
                    pe.wait_ge(wa_pt[i % 2], i // 2 + 1)
                    if i >= 2:
                        pe.wait_ge(wa_o, i - 1)
                    for b in range(4):
                        mm = nc.tensor.matmul(bank[i % 2][:, 0:AHD], probT1[i % 2][:, b, :],
                                              vrow1[:, b, (h // 4) * AHD:(h // 4 + 1) * AHD], start=(b == 0), stop=(b == 3))
                    mm.then_inc(wa_pv, 1)
            pe.wait_ge(wa_o, len(wsteps))
            transposes(44, KT, S, lambda i, k: qrow[:, i, k * P:(k + 1) * P])
            pe.wait_ge(tr_lo, 52)
            for u in range(U_OD, U_M1):
                row_unit(u, a_hi, a_lo, range(NT), before[u])
            gate_rows((M1 + 16,), 5)
            pe.wait_ge(ln_n, 10)
            transposes(52, KT, S, lambda i, k: Y[:, i, k * P:(k + 1) * P])
            pe.wait_ge(tr_lo, 60)
            mlp(U_M1, a_hi, a_lo, S, *half_m, 32, False)
            gate_rows((M1 + 40,), 6)

        @block_.scalar
        def _(act):
            def split_hi(u):
                if u >= len(units):
                    return
                _, kt, cols, _b = units[u]
                act.wait_ge(raw_full[u % RAW], 16 * (u // RAW + 1))
                if u >= SPL:
                    act.wait_ge(tile_done, before[u - SPL + 1])
                nc.scalar.activation(whi[u % SPL][:, 0:kt * cols], raw[u % RAW][:, 0:kt * cols], ACT.Copy).then_inc(hi_done, 1)

            def transposed_hi(t0, kts, T, hi, tmp):
                for kt in range(kts):
                    t = t0 + kt
                    act.wait_ge(tr_tmp, t + 1)
                    nc.scalar.activation(hi[:, kt, 0:T], tmp[t % 2][:, 0:T], ACT.Copy).then_inc(tr_hi, 1)

            def take(b):
                act.wait_ge(tile_done, b + 1)
                return bank[b % 4]

            act.wait_ge(load_x, 16)
            for m in range(NT):
                nc.scalar.activation(flat(za), xres[:, m, :], ACT.Square, accum_out=stat[:, m:m + 1]).then_inc(sq_sum, 1)
                act.wait_ge(sq_sum, m + 1)
            act.wait_ge(vec_c, 3)
            nc.scalar.activation(stat[:, 2:4], stat[:, 0:2], ACT.Sqrt, bias=stat[:, 40:41], scale=1.0 / D).then_inc(root, 1)
            c0 = ROWS["c"]
            nc.scalar.activation(cvec[:, 0, :], vecT[:, c0:c0 + 8], ACT.Copy)
            nc.scalar.activation(cvec[:, 1:3, :], vecT[:, c0 + 8:c0 + 24].rearrange("p (a b) -> p a b", a=2), ACT.Silu)\
                .then_inc(cvec_done, 1)
            for u in range(LEAD):
                split_hi(u)
            transposed_hi(0, KT, S, h_hi, trA)
            for u in range(U_GATES):
                split_hi(u + LEAD)
                b = before[u]
                src = take(b)[:, :].rearrange("p (m n) -> p m n", m=2)
                if u < 2:
                    dst, f, kw = u_row[:, :, u * UC:(u + 1) * UC], ACT.Copy, {}
                elif u < 4:
                    dst, f, kw = zpT[:, 2 * (u - 2):2 * (u - 1), :], ACT.Silu, {}
                elif u < 22:
                    g, j = divmod(u - 4, 6)
                    if j < 2:
                        dst, f, kw = qT[:, g, 2 * j:2 * j + 2, :], ACT.Copy, {"scale": HD ** -0.5}
                    elif j < 4:
                        continue
                    else:
                        dst, f, kw = vR[:, g, :, (j - 4) * UC:(j - 3) * UC], ACT.Copy, {}
                else:
                    dst, f, kw = za[:, :, (u - 22) * UC:(u - 21) * UC], ACT.Silu, {}
                nc.scalar.activation(dst, src, f, **kw).then_inc(free[b % 4], 1)
                if u == 3:
                    for g in range(2):
                        act.wait_ge(pool_mm, g + 1)
                        nc.scalar.activation(trA[g], bank[4 + g][:, :], ACT.Copy).then_inc(pool_ev, 1)
                    act.wait_ge(mz_tmp, 2)
                    nc.scalar.activation(flat(mz_hi), flat(u_row), ACT.Copy).then_inc(mz_part, 1)
            for n, (qt, h) in enumerate(steps):
                W = P * (qt + 1)
                act.wait_ge(at_mx, n + 1)
                if n:
                    act.wait_ge(at_t, rounds(n))
                nc.scalar.activation(prob[:, 0:2 * W], bank[4][:, 0:2 * W], ACT.Exp, bias=stat[:, 10:11],
                                     accum_out=stat[:, 12:13])
                nc.scalar.activation(prob[:, 2 * W:3 * W], bank[5][:, 0:W], ACT.Exp, bias=stat[:, 10:11],
                                     accum_out=stat[:, 13:14]).then_inc(at_p, 1)
                if n < 8:
                    u = U_GATES + n
                    split_hi(u + LEAD)
                    b = before[u]
                    dst = gaT if n < 4 else gpT
                    nc.scalar.activation(dst[:, 2 * (n % 4):2 * (n % 4) + 2, :],
                                         take(b)[:, :].rearrange("p (m n) -> p m n", m=2), ACT.Sigmoid)\
                        .then_inc(free[b % 4], 1)
            transposed_hi(8, 4, S, at_hi, trA)
            for u in range(32, 36):
                split_hi(u + LEAD)
            act.wait_ge(merged, 1)
            nc.scalar.activation(flat(h_hi), flat(gaT), ACT.Copy).then_inc(merged_hi, 1)
            for u in range(36, 40):
                split_hi(u + LEAD)
            act.wait_ge(x_new, 4)
            for m in range(NT):
                i = nc.scalar.activation(tmpa[:, m, :], xres[:, m, :], ACT.Square, accum_out=stat[:, m:m + 1])
            i.then_inc(sq_sum, 1)
            act.wait_ge(sq_sum, 3)
            nc.scalar.activation(stat[:, 2:4], stat[:, 0:2], ACT.Sqrt, bias=stat[:, 40:41], scale=1.0 / D).then_inc(root, 1)

            link = Count(achain)

            def step(ins):
                ins.then_inc(achain, 1)
                act.wait_ge(achain, link.up())

            transposed_hi(12, KT, T, a_hi, trB)
            split_hi(U_EV + LEAD)
            b = before[U_EV]
            nc.scalar.activation(flat(lrR), take(b)[:, 0:P], ACT.Copy).then_inc(free[b % 4], 1)
            act.wait_ge(lr_t, 1)
            act.wait_ge(filled, FILLS + 1)
            for d in range(2):
                nc.scalar.activation(lrT[0:RANK, d, :], bank[4 + d][0:RANK, :], ACT.Copy).then_inc(lr_ev, 1)
            for i in range(TILES):
                act.wait_ge(z_mm, i + 1)
                if i:
                    act.wait_ge(la_done, i)
                step(nc.scalar.activation(ex[0][:, :], bank[4 + i % 2][:, :], ACT.Abs))
                step(nc.scalar.activation(ex[0][:, :], ex[0][:, :], ACT.Exp, scale=-1.0))
                nc.scalar.activation(ex[1][:, :], ex[0][:, :], ACT.Ln, bias=1.0).then_inc(lg_done, 1)
            act.wait_ge(load_th, 32)
            step(nc.scalar.activation(lgam[:, 4:8], lgam[:, 0:4], ACT.Exp))
            step(nc.scalar.activation(lgam[:, 4:8], lgam[:, 4:8], ACT.Ln, bias=1.0, scale=-1.0))
            step(nc.scalar.activation(lgam[:, 8:12], lgam[:, 4:8], ACT.Copy, scale=-1.0))

            def mixer_units(u0, group):
                for u in range(u0, u0 + 6):
                    split_hi(u + LEAD)
                    b, j = before[u], u - u0
                    if j == 0:
                        for n in range(2):
                            if group:
                                act.wait_ge(o_mm, RH)
                            src = take(b + n)
                            for hh in range(2):
                                for half in range(2):
                                    last = nc.scalar.activation(qd[64 * half:64 * half + 64, 2 * n + hh, :],
                                                                src[64 * hh:64 * hh + 64, :], ACT.Copy,
                                                                scale=1.0 if group else DK ** -0.5)
                            last.then_inc(free[(b + n) % 4], 1)
                    elif j >= 2:
                        for i in range(2):
                            src = take(b + i)[:, :].rearrange("p (m n) -> p m n", m=2)
                            c0 = (j % 2) * UC
                            if j < 4:
                                nc.scalar.activation(vv[:, 2 * i:2 * i + 2, c0:c0 + UC], src, ACT.Copy).then_inc(free[(b + i) % 4], 1)
                            else:
                                c0 += 0 if group else 512
                                nc.scalar.activation(gy[:, 2 * i:2 * i + 2, c0:c0 + UC], src, ACT.Silu).then_inc(free[(b + i) % 4], 1)

            def decays(hd):
                gla, h = hd < RH, hd % RH
                if hd:
                    if hd >= RH:
                        act.wait_ge(ss_done, RH)
                    act.wait_ge(qk_done, hd)
                if gla:
                    act.wait_ge(bc_mm, hd + 1)
                    nc.scalar.activation(ex[0][:, :], bank[6][:, :], ACT.Exp, scale=1.0 / TAU).then_inc(ex_done, 1)
                    nc.scalar.activation(ex[1][:, :], bank[6][:, :], ACT.Exp, scale=-1.0 / TAU).then_inc(ex_done, 1)
                else:
                    nc.scalar.activation(ex[0][:, 0:CH], const("pos"), ACT.Exp, scale=lgam[:, 4 + h:5 + h]).then_inc(ex_done, 1)
                    nc.scalar.activation(ex[1][:, 0:CH], const("pos"), ACT.Exp, scale=lgam[:, 8 + h:9 + h]).then_inc(ex_done, 1)

            def head(hd):
                gla, h = hd < RH, hd % RH
                act.wait_ge(kt_mm, hd + 1)
                if hd:
                    act.wait_ge(ss_done, hd)
                nc.scalar.activation(flat(kir), bank[6][:, :], ACT.Copy).then_inc(kir_done, 1)
                act.wait_ge(kv_mm, hd + 1)
                if hd:
                    act.wait_ge(sp_done, hd)
                for i in range(2):
                    nc.scalar.activation(kv[:, i:8:2, :], bank[4 + i][:, :].rearrange("p (c n) -> p c n", c=4),
                                         ACT.Copy).then_inc(kv_done, 1)
                act.wait_ge(o_mm, hd + 1)
                col = h + (RH if gla else 0)
                for i in range(TILES):
                    last = nc.scalar.activation(ex[1][:, i * P:(i + 1) * P], bank[6][:, i * P:(i + 1) * P], ACT.Square,
                                                accum_out=ssq[:, 0, i, col:col + 1])
                last.then_inc(ss_done, 1)

            for g in range(2):
                mixer_units(U_EV + 1 + 6 * g, g)
                for hd in range(4 * g, 4 * g + 4):
                    decays(hd)
                for hd in range(4 * g, 4 * g + 4):
                    head(hd)
            act.wait_ge(ss_done, 8)
            nc.scalar.activation(ssq[:, 1, :, :], ssq[:, 0, :, :], ACT.Sqrt, bias=stat[:, 40:41], scale=1.0 / DV).then_inc(root, 1)
            transposed_hi(20, KT, T, a_hi, trB)
            for u in range(U_EVO, U_M0):
                split_hi(u + LEAD)
                b = before[u]
                cs = slice((u - U_EVO) * UC, (u - U_EVO + 1) * UC)
                for i in range(2):
                    nc.scalar.activation(Y[:, 2 * i:2 * i + 2, cs], take(b + i)[:, :].rearrange("p (m n) -> p m n", m=2),
                                         ACT.Copy).then_inc(free[(b + i) % 4], 1)

            def ln_roots(k, tiles):
                act.wait_ge(ln_var, k + 1)
                nc.scalar.activation(bna[:, 0:tiles, 2], bna[:, 0:tiles, 1], ACT.Sqrt, bias=stat[:, 41:42]).then_inc(ln_root, 1)

            ln_roots(0, TILES)
            transposed_hi(28, KT, T, a_hi, trB)

            def mlp(u0, Tn, mh, hid0, more):
                per = 8 * Tn // 256
                ht = 4 * Tn // 256

                def round_(r, lead=8):
                    for j in range(8):
                        u = u0 + j + LEAD
                        tn = Tn // 256
                        if j < lead:
                            act.wait_ge(raw_full[u % RAW], at_(16 * (u // RAW + 1), r, 16 * 8 // RAW))
                            act.wait_ge(tile_done, at_(before[u0] + tn * (j + LEAD - SPL + 1), r, per))
                            nc.scalar.activation(whi[u % SPL][:, :], raw[u % RAW][:, :], ACT.Copy).then_inc(hi_done, 1)
                        if j >= 4:
                            continue
                        if j == 0:
                            act.wait_ge(tile_done, at_(before[u0], r, per))
                        for i in range(tn):
                            bt, t = before[u0 + j] + i, tn * j + i
                            act.wait_ge(tile_done, at_(bt + 1, r, per))
                            nc.scalar.activation(rel_[:, :], bank[bt % 4][:, :], ACT.Relu).then_inc(free[bt % 4], 1)
                            act.wait_ge(sq_done, at_(hid0 + t + 1, r, ht))
                            nc.scalar.activation(flat(mh)[:, 512 * t:512 * t + 512], sq_[:, :], ACT.Copy).then_inc(hid_hi, 1)

                with act.Fori(0, 4 if more else 3) as r:
                    round_(r)
                if not more:
                    round_(3, 8 - LEAD)

            mlp(U_M0, T, m_hi, 0, True)
            ln_roots(1, TILES)
            transposed_hi(36, KT, T, a_hi, trB)

            def take_transposed(n):
                act.wait_ge(kq_t, n + 1)
                src = bank[4 + n % 4][:, :]
                if n < KVH:
                    nc.scalar.activation(kT1[:, n, :], src, ACT.Copy).then_inc(kq_ev, 1)
                else:
                    j = n - KVH
                    nc.scalar.activation(qT1[:, 2 * j:2 * j + 2, :], src.rearrange("p (a b) -> p a b", a=2), ACT.Copy,
                                         scale=AHD ** -0.5).then_inc(kq_ev, 1)

            act.wait_ge(res_mul, 12)
            for u in range(U_QKV, U_OD):
                split_hi(u + LEAD)
                b, j = before[u], u - U_QKV
                if j == 0:
                    src = take(b)[:, :].rearrange("p (m h n) -> p m h n", m=2, h=KVH)
                    for m in range(2):
                        for i in range(2):
                            last = nc.scalar.activation(krow[:, m, :, i, :], src[:, m, :, :], ACT.Copy)
                    last.then_inc(free[b % 4], 1)
                elif j == 1:
                    for i in range(2):
                        nc.scalar.activation(vrow1[:, 2 * i:2 * i + 2, :], take(b + i)[:, :].rearrange("p (m n) -> p m n", m=2),
                                             ACT.Copy).then_inc(free[(b + i) % 4], 1)
                elif j == 2:
                    for n in range(KVH):
                        take_transposed(n)
                else:
                    take_transposed(KVH + j - 3)
            take_transposed(7)
            act.wait_ge(load_sk, 16)
            for n in range(len(wsteps) + 1):
                if n < len(wsteps):
                    qt, h = wsteps[n]
                    c = 8 + 4 * (n % 2)
                    act.wait_ge(wa_max, n + 1)
                    if n >= 2:
                        act.wait_ge(wa_t, n - 1)
                        act.wait_ge(wa_o, n - 1)
                    nc.scalar.activation(prob1[n % 2][:, :], bank[4 + n % 2][:, :], ACT.Exp, bias=stat[:, c:c + 1],
                                         accum_out=stat[:, c + 1:c + 2])
                    nc.scalar.activation(stat[:, c + 2:c + 3], sink[:, h:h + 1], ACT.Exp, bias=stat[:, c:c + 1]).then_inc(wa_exp, 1)
                if n % 2:
                    i = n - 1
                    act.wait_ge(wa_t, i + 1)
                    if i >= 2:
                        act.wait_ge(wa_pv, i - 1)
                    nc.scalar.activation(flat(probT1[0]), bank[6][:, :], ACT.Copy).then_inc(wa_pt[0], 1)
            transposed_hi(44, KT, S, a_hi, trB)
            for u in range(U_OD, U_M1):
                split_hi(u + LEAD)
                b = before[u]
                cs = slice((u - U_OD) * UC, (u - U_OD + 1) * UC)
                nc.scalar.activation(Y[:, 0:2, cs], take(b)[:, :].rearrange("p (m n) -> p m n", m=2), ACT.Copy).then_inc(free[b % 4], 1)
            ln_roots(2, NT)
            transposed_hi(52, KT, S, a_hi, trB)
            mlp(U_M1, S, half_m[0], 32, False)
            ln_roots(3, NT)

        @block_.vector
        def _(dve):
            chain = Count(vchain)

            def link(ins):
                ins.then_inc(vchain, 1)
                chain.up()
                dve.wait_ge(vchain, chain.at())

            def split_lo(u):
                if u >= len(units):
                    return
                _, kt, cols, _b = units[u]
                s, n = u % SPL, kt * cols
                dve.wait_ge(hi_done, u + 1)
                if u >= SPL:
                    dve.wait_ge(tile_done, before[u - SPL + 1])
                nc.vector.tensor_tensor(wlo[s][:, 0:n], raw[u % RAW][:, 0:n], bf(whi[s], n), ALU.subtract).then_inc(lo_done, 1)

            def take(b):
                dve.wait_ge(tile_done, b + 1)
                return bank[b % 4]

            def sum_quarter(q):
                vecs = vblocks[q // 4][3]
                s, v = gfull(q)
                dve.wait_ge(s, v)
                w = vslot(q)
                for kk in range(2):
                    kt = (q % 4) * 2 + kk
                    for i, (cv, _c) in enumerate(vecs):
                        if kt == 0:
                            if i == 0:
                                dve.wait_ge(seed_full, 16 * (q // 4 + 1))
                                if q == 0:
                                    dve.wait_ge(filled, FILLS)
                                    dve.wait_ge(cvec_done, 1)
                        else:
                            dve.wait_ge(vsum, vops[q] + kk * len(vecs) + i - len(vecs) + 1)
                        nc.vector.scalar_tensor_tensor(out=acc[:, i, :], in0=w[:, kk, :], scalar=cvec[:, cv, kt:kt + 1],
                                                       in1=seed[:, :] if kt == 0 else acc[:, i, :],
                                                       op0=ALU.mult, op1=ALU.add).then_inc(vsum, 1)

            def take_mod(n):
                dve.wait_ge(red_done, n + 1)
                for i, (_cv, col) in enumerate(vblocks[n][3]):
                    last = nc.vector.tensor_copy(mod[:, col:col + 4], bank[7][:, 4 * i:4 * i + 4])
                last.then_inc(mod_done, 1)

            def transposed(t0, kts, T, hi, lo, tmp, affine):
                def low(kt):
                    dve.wait_ge(tr_hi, t0 + kt + 1)
                    nc.vector.tensor_tensor(lo[:, kt, 0:T], tmp[(t0 + kt) % 2][:, 0:T], hi[:, kt, 0:T].bitcast(f32),
                                            ALU.subtract).then_inc(tr_lo, 1)
                for kt in range(kts):
                    t = t0 + kt
                    dve.wait_ge(tr_full, t + 1)
                    if t >= 2:
                        dve.wait_ge(tr_lo, t - 1)
                    for c0, c1, sc, sh in affine(kt):
                        o, i = tmp[t % 2][:, c0:c1], bank[4 + t % 2][:, c0:c1]
                        if sc is None:
                            last = nc.vector.tensor_copy(o, i)
                        elif sh is None:
                            last = nc.vector.tensor_scalar(o, i, sc, None, ALU.mult)
                        else:
                            last = nc.vector.tensor_scalar(o, i, sc, sh, ALU.mult, ALU.add)
                    last.then_inc(tr_tmp, 1)
                    if kt:
                        low(kt - 1)
                low(kts - 1)

            dve.wait_ge(vec_t, 1)
            link(nc.vector.tensor_copy(vecT[:, :], bank[6][:, 0:NROWS]))
            nc.vector.tensor_copy(aff[:, 0, :], vecT[:, 0:KT]).then_inc(vec_c, 1)
            dve.wait_ge(vec_c, 1)
            for g in range(GROUPS):
                dve.wait_ge(line_mm, g + 1)
                nc.vector.tensor_copy(line[:, g, :], bank[4 + g][0:HEADS, 0:384]).then_inc(line_done, 1)
            dve.wait_ge(filled, FILLS)
            nc.vector.tensor_copy(stat[:, 42:43], stat[:, 40:41]).then_inc(vec_c, 2)
            dve.wait_ge(root, 1)
            link(nc.vector.reciprocal(stat[:, 4:6], stat[:, 2:4]))
            for m in range(NT):
                last = nc.vector.tensor_scalar(xrow[:, m, :], xres[:, m, :], stat[:, 4 + m:5 + m], None, ALU.mult)
            last.then_inc(x_scaled, 1)
            for u in range(LEAD):
                split_lo(u)
            for q in range(PRE_Q):
                if q and q % 4 == 0:
                    take_mod(q // 4 - 1)
                sum_quarter(q)
            take_mod(3)
            dve.wait_ge(mod_done, 4)
            link(nc.vector.scalar_tensor_tensor(out=aff[:, 0, :], in0=mod[:, 8:16], scalar=1.0, in1=aff[:, 0, :],
                                                op0=ALU.add, op1=ALU.mult))
            transposed(0, KT, S, h_hi, h_lo, trA, lambda k: [(0, S, aff[:, 0, k:k + 1], mod[:, k:k + 1])])
            q = PRE_Q
            for u in range(U_GATES):
                split_lo(u + LEAD)
                b = before[u]
                if 4 <= u < 22 and (u - 4) % 6 in (2, 3):
                    g, j = divmod(u - 4, 6)
                    nc.vector.tensor_copy(kT[:, g, 2 * j - 4:2 * j - 2, :], take(b)[:, :].rearrange("p (m n) -> p m n", m=2))\
                        .then_inc(free[b % 4], 1)
                if u and q % 4 == 0:
                    take_mod(q // 4 - 1)
                sum_quarter(q)
                q += 1
                if u == 3:
                    all_taken(dve, 4)
                    s0 = ROWS["pool_scale"]
                    for g in range(4):
                        dve.wait_ge(pool_mm, 3 + g // 2)
                        last = nc.vector.scalar_tensor_tensor(
                            out=flat(u_row)[:, g * S:(g + 1) * S], in0=bank[6 if g < 2 else 4][:, (g % 2) * S:(g % 2 + 1) * S],
                            scalar=vecT[:, s0 + g:s0 + g + 1], in1=zpT[:, g, :], op0=ALU.mult, op1=ALU.mult)
                        if g % 2:
                            last.then_inc(mz_tmp, 1)
                    dve.wait_ge(mz_part, 1)
                    nc.vector.tensor_tensor(flat(mz_lo), flat(u_row), flat(mz_hi).bitcast(f32), ALU.subtract).then_inc(mz_part, 1)
            for n, (qt, h) in enumerate(steps):
                W = P * (qt + 1)
                dve.wait_ge(at_s, n + 1)
                if n:
                    dve.wait_ge(at_p, n)
                nc.vector.tensor_reduce(stat[:, 8:9], bank[4][:, 0:2 * W], AX.X, ALU.max)
                link(nc.vector.tensor_reduce(stat[:, 9:10], bank[5][:, 0:W], AX.X, ALU.max))
                nc.vector.tensor_scalar(stat[:, 10:11], stat[:, 8:9], stat[:, 9:10], -1.0, ALU.max, ALU.mult).then_inc(at_mx, 1)
                if n < 8:
                    split_lo(U_GATES + n + LEAD)
                if q % 4 == 0:
                    take_mod(q // 4 - 1)
                sum_quarter(q)
                q += 1
                for j in range(qt + 1):
                    rc = rounds(n) + j
                    dve.wait_ge(at_t, rc + 1)
                    if rc >= 2:
                        dve.wait_ge(at_pv, rc - 1)
                    nc.vector.tensor_copy(probT[rc % 2][:, 0:3, :], bank[6][:, 0:384].rearrange("p (b q) -> p b q", b=3))\
                        .then_inc(at_pt, 1)
                dve.wait_ge(at_p, n + 1)
                link(nc.vector.tensor_tensor(stat[:, 14:15], stat[:, 12:13], stat[:, 13:14], ALU.add))
                link(nc.vector.reciprocal(stat[:, 15:16], stat[:, 14:15]))
                dve.wait_ge(at_pv, rounds(n + 1))
                z = za[:, qt, h * HD:(h + 1) * HD]
                nc.vector.scalar_tensor_tensor(out=z, in0=bank[5][:, 256:256 + HD], scalar=stat[:, 15:16], in1=z,
                                               op0=ALU.mult, op1=ALU.mult).then_inc(at_z, 1)
            transposed(8, 4, S, at_hi, at_lo, trA, lambda k: [(0, S, None, None)])
            for u in range(32, 36):
                split_lo(u + LEAD)
                t = gaT if u < 34 else gpT
                for i in range(2):
                    b = before[u] + i
                    j = 4 * (u % 2) + 2 * i
                    part = t[:, j:j + 2, :]
                    nc.vector.tensor_tensor(part, take(b)[:, :].rearrange("p (m n) -> p m n", m=2), part, ALU.mult)\
                        .then_inc(free[b % 4], 1)
            all_taken(dve, before[36])
            nc.vector.tensor_tensor(flat(gaT), flat(gaT), flat(gpT), ALU.add).then_inc(merged, 1)
            dve.wait_ge(merged_hi, 1)
            nc.vector.tensor_tensor(flat(h_lo), flat(gaT), flat(h_hi).bitcast(f32), ALU.subtract).then_inc(merged_lo, 1)
            dve.wait_ge(rowb, 1)
            for i in range(2):
                last = nc.vector.tensor_copy(grow_a[:, 512 * i:512 * i + 512], bank[4 + i][:, :])
            last.then_inc(rowb_done, 1)
            dve.wait_ge(rowb_done, 1)
            for u in range(36, 40):
                split_lo(u + LEAD)
                b, j = before[u], u - 36
                cs = slice(j * UC, (j + 1) * UC)
                v = take(b)[:, :].rearrange("p (m n) -> p m n", m=2)
                ins = nc.vector.tensor_tensor(tmpa[:, :, cs], v, spread(grow_a[:, cs], [[0, 2], [1, UC]]), ALU.mult)
                ins.then_inc(free[b % 4], 1)
                taken(dve, b)
                nc.vector.tensor_tensor(xres[:, :, cs], xres[:, :, cs], tmpa[:, :, cs], ALU.add).then_inc(x_new, 1)
            dve.wait_ge(root, 2)
            link(nc.vector.reciprocal(stat[:, 4:6], stat[:, 2:4]))
            dve.wait_ge(load_f, 48)
            for m in range(NT):
                nc.vector.scalar_tensor_tensor(out=xres[:, m, :], in0=xres[:, m, :], scalar=stat[:, 4 + m:5 + m],
                                               in1=frow[:, :], op0=ALU.mult, op1=ALU.mult).then_inc(x_new, 1)

            def quarters(n):
                nonlocal q
                for _ in range(n):
                    if q % 4 == 0:
                        take_mod(q // 4 - 1)
                    sum_quarter(q)
                    q += 1

            nc.vector.tensor_scalar(aff[:, 1, :], mod[:, M0C + 8:M0C + 16], 1.0, None, ALU.add)
            link(nc.vector.tensor_scalar(aff[:, 2, :], mod[:, M0 + 8:M0 + 16], 1.0, None, ALU.add))
            transposed(12, KT, T, a_hi, a_lo, trB,
                       lambda k: [(0, S, aff[:, 1, k:k + 1], mod[:, M0C + k:M0C + k + 1]),
                                  (S, T, aff[:, 2, k:k + 1], mod[:, M0 + k:M0 + k + 1])])
            split_lo(U_EV + LEAD)
            for i in range(TILES):
                dve.wait_ge(z_mm, i + 1)
                dve.wait_ge(lg_done, i + 1)
                nc.vector.scalar_tensor_tensor(out=la[:, i, :], in0=bank[4 + i % 2][:, :], scalar=0.0, in1=ex[1][:, :],
                                               op0=ALU.min, op1=ALU.subtract).then_inc(la_done, 1)

            def mixer_units(u0, group):
                for u in range(u0, u0 + 6):
                    split_lo(u + LEAD)
                    b = before[u]
                    if u - u0 == 1:
                        for n in range(2):
                            if group:
                                dve.wait_ge(o_mm, RH)
                            src = take(b + n)
                            for hh in range(2):
                                for half in range(2):
                                    last = nc.vector.tensor_scalar(ki[64 * half:64 * half + 64, 2 * n + hh, :],
                                                                   src[64 * hh:64 * hh + 64, :],
                                                                   DK ** -0.5 if group else 1.0, None, ALU.mult)
                            last.then_inc(free[(b + n) % 4], 1)
                    quarters(UNIT_Q[u])

            def decays(hd):
                gla, h = hd < RH, hd % RH
                dve.wait_ge(ex_done, 2 * (hd + 1))
                for t, e in ((qd, ex[0]), (ki, ex[1])):
                    if gla:
                        last = nc.vector.tensor_tensor(t[:, h, :], t[:, h, :], e[:, :], ALU.mult)
                    else:
                        v = t[:, h, :].rearrange("p (c n) -> p c n", c=8)
                        last = nc.vector.tensor_tensor(v, v, spread(e[:, 0:CH], [[0, 8], [1, CH]]), ALU.mult)
                if gla:
                    nc.vector.tensor_copy(dec[0:64, h, :], ex[0][0:64, CH - 1:T:CH])
                    last = nc.vector.tensor_copy(dec[64:P, h, :], ex[0][64:P, 0:T:CH])
                else:
                    nc.vector.tensor_copy(dec[0:64, h, :], spread(ex[0][0:64, CH - 1:CH], [[0, 8]]))
                    last = nc.vector.tensor_copy(dec[64:P, h, :], spread(ex[0][64:P, 0:1], [[0, 8]]))
                last.then_inc(qk_done, 1)

            def head(hd):
                gla, h = hd < RH, hd % RH
                dve.wait_ge(kv_done, 2 * (hd + 1))
                order = [3, 2, 1, 0, 7, 6, 5, 4]
                for s_ in range(6):
                    for rows, c, nx in ((slice(0, 64), s_, s_ + 1), (slice(64, P), order[s_], order[s_ + 1])):
                        if s_:
                            dve.wait_ge(vchain, chain.at(1))
                        nc.vector.scalar_tensor_tensor(out=kv[rows, nx, :], in0=kv[rows, c, :], scalar=dec[rows, h, c:c + 1],
                                                       in1=kv[rows, nx, :], op0=ALU.mult, op1=ALU.add).then_inc(vchain, 1)
                        chain.up()
                dve.wait_ge(vchain, chain.at())
                if hd:
                    dve.wait_ge(o_mm, hd)
                else:
                    nc.vector.memset(sp[0:64, 0, :], 0.0)
                    nc.vector.memset(sp[64:P, 3, :], 0.0)
                for rows, d0, s0, n in ((slice(0, 64), 1, 0, 7), (slice(64, P), 0, 1, 3), (slice(64, P), 4, 5, 3), (slice(64, P), 7, 0, 1)):
                    d = dec[rows, h, s0:s0 + n]
                    last = nc.vector.tensor_tensor(sp[rows, d0:d0 + n, :], kv[rows, s0:s0 + n, :],
                                                   spread(d, [[1, n], [0, DV]]), ALU.mult)
                last.then_inc(sp_done, 1)
                dve.wait_ge(s_mm, hd + 1)
                nc.vector.tensor_tensor(sc[:, :, :], bank[4][:, :].rearrange("p (i t) -> p i t", i=4),
                                        spread(const("tri_f"), [[0, 4], [1, P]]), ALU.mult)
                link(nc.vector.tensor_tensor(sc2[:, :, :], bank[5][:, :].rearrange("p (i t) -> p i t", i=4),
                                             spread(const("strict_b"), [[0, 4], [1, P]]), ALU.mult))
                nc.vector.tensor_tensor(sc[:, :, :], sc[:, :, :], sc2[:, :, :], ALU.add).then_inc(sc_done, 1)
                dve.wait_ge(o_mm, hd + 1)
                dve.wait_ge(ss_done, hd + 1)
                c0 = h * DV + (512 if gla else 0)
                v = gy[:, :, c0:c0 + DV]
                nc.vector.tensor_tensor(v, bank[6][:, :].rearrange("p (i t) -> p i t", i=4), v, ALU.mult).then_inc(gy_done, 1)

            for g in range(2):
                mixer_units(U_EV + 1 + 6 * g, g)
                for hd in range(4 * g, 4 * g + 4):
                    decays(hd)
                for hd in range(4 * g, 4 * g + 4):
                    head(hd)
                    quarters(HEAD_Q)
            dve.wait_ge(root, 3)
            dve.wait_ge(gy_done, 8)
            link(nc.vector.reciprocal(ssq[:, 2, :, :], ssq[:, 1, :, :]))
            g4 = gy[:, :, :].rearrange("p i (h n) -> p i h n", h=8)
            nc.vector.tensor_tensor(g4, g4, spread(ssq[:, 2, :, :], [[8, 4], [1, 8], [0, DV]]), ALU.mult).then_inc(y_scaled, 1)
            gg = vecT[:, ROWS["gla_g"]:ROWS["gla_g"] + 1]
            transposed(20, KT, T, a_hi, a_lo, trB, lambda k: [(0, T, gg if k >= 4 else None, None)])
            for u in range(U_EVO, U_M0):
                split_lo(u + LEAD)
                quarters(UNIT_Q[u])

            def gate_rows(n0, count=2):
                for i in range(count):
                    dve.wait_ge(rowb, n0 + i + 1)
                    for j in range(2):
                        last = nc.vector.tensor_copy(grow[:, i, 512 * j:512 * j + 512], bank[4 + j][:, :])
                    last.then_inc(rowb_done, 1)
                dve.wait_ge(rowb_done, n0 + count)

            def layer_norm(k, tiles, res, gate):
                for i in range(tiles):
                    link(nc.vector.tensor_tensor(Y[:, i, :], Y[:, i, :], gate(i), ALU.mult))
                    link(nc.vector.scalar_tensor_tensor(out=Y[:, i, :], in0=res(i), scalar=ALPHA, in1=Y[:, i, :],
                                                        op0=ALU.mult, op1=ALU.add))
                    for j in range(2):
                        last = nc.vector.bn_stats(bns[:, i, j, :], Y[:, i, 512 * j:512 * j + 512])
                    link(last)
                    last = nc.vector.bn_aggr(bna[:, i, 0:2], bns[:, i, :, :])
                last.then_inc(ln_var, 1)
                dve.wait_ge(ln_root, k + 1)
                link(nc.vector.reciprocal(bna[:, 0:tiles, 3], bna[:, 0:tiles, 2]))
                for i in range(tiles):
                    nc.vector.tensor_scalar(Y[:, i, :], Y[:, i, :], bna[:, i, 0:1], bna[:, i, 3:4], ALU.subtract, ALU.mult)\
                        .then_inc(ln_n, 1)

            def affine(rows, k, sh, sc):
                g0, b0 = ROWS["ln_g"] + 8 * k, ROWS["ln_b"] + 8 * k
                nc.vector.scalar_tensor_tensor(out=aff[:, rows, :], in0=mod[:, sc:sc + 8], scalar=1.0, in1=vecT[:, g0:g0 + 8],
                                               op0=ALU.add, op1=ALU.mult)
                link(nc.vector.scalar_tensor_tensor(out=aff[:, rows + 1, :], in0=mod[:, sc:sc + 8], scalar=1.0,
                                                    in1=vecT[:, b0:b0 + 8], op0=ALU.add, op1=ALU.mult))
                link(nc.vector.tensor_tensor(aff[:, rows + 1, :], aff[:, rows + 1, :], mod[:, sh:sh + 8], ALU.add))

            all_taken(dve, before[U_M0])
            gate_rows(1)
            dve.wait_ge(load_cr, 16)
            layer_norm(0, TILES, lambda i: cres[:, i, :] if i < 2 else xres[:, i - 2, :], lambda i: grow[:, i // 2, :])
            affine(0, 0, M0C + 24, M0C + 32)
            affine(2, 0, M0 + 24, M0 + 32)
            both = lambda k: [(0, S, aff[:, 0, k:k + 1], aff[:, 1, k:k + 1]), (S, T, aff[:, 2, k:k + 1], aff[:, 3, k:k + 1])]
            transposed(28, KT, T, a_hi, a_lo, trB, both)

            def mlp(u0, Tn, mh, ml, hid0, vecs, more):
                per = 8 * Tn // 256
                ht = 4 * Tn // 256
                tn = Tn // 256

                def round_(r, lead=8):
                    for j in range(8):
                        u = u0 + j + LEAD
                        if j < lead:
                            dve.wait_ge(hi_done, at_(u + 1, r, 8))
                            nc.vector.tensor_tensor(wlo[u % SPL][:, :], raw[u % RAW][:, :], bf(whi[u % SPL], KT * UC),
                                                    ALU.subtract).then_inc(lo_done, 1)
                        for i in range(tn):
                            bt, t = before[u0 + j] + i, tn * j + i
                            if j < 4:
                                dve.wait_ge(free[bt % 4], at_(bt // 4 + 1, r, per // 4))
                                if t:
                                    dve.wait_ge(hid_lo, at_(hid0 + t, r, ht))
                                nc.vector.tensor_tensor(sq_[:, :], rel_[:, :], rel_[:, :], ALU.mult).then_inc(sq_done, 1)
                                dve.wait_ge(hid_hi, at_(hid0 + t + 1, r, ht))
                                fs = slice(512 * t, 512 * t + 512)
                                nc.vector.tensor_tensor(flat(ml)[:, fs], sq_[:, :], flat(mh)[:, fs].bitcast(f32), ALU.subtract)\
                                    .then_inc(hid_lo, 1)
                                if t == ht - 1:
                                    dve.wait_ge(hid_lo, at_(hid0 + ht, r, ht))
                            else:
                                dve.wait_ge(tile_done, at_(bt + 1, r, per))
                                yv = Y[:, 2 * i:2 * i + 2, (j - 4) * UC:(j - 3) * UC]
                                nc.vector.tensor_tensor(yv, bank[bt % 4][:, :].rearrange("p (m n) -> p m n", m=2), yv, ALU.add)\
                                    .then_inc(free[bt % 4], 1)
                        if vecs and j in (3, 7):
                            n = 22 + j // 4
                            if j == 3:
                                take_loop_mod(n, r)
                        if vecs:
                            for i in LOOP_Q[j]:
                                qq = 88 + i
                                s_, v_ = gfull(qq)
                                dve.wait_ge(s_, at_(v_, r, 16 * 8 // GSB))
                                if i % 4 == 0:
                                    dve.wait_ge(seed_full, at_(16 * (qq // 4 + 1), r, 32))
                                for kk in range(2):
                                    kt = (i % 4) * 2 + kk
                                    if kt:
                                        dve.wait_ge(vsum, at_(vops[88] + 2 * i + kk, r, 16))
                                    nc.vector.scalar_tensor_tensor(
                                        out=acc[:, 0, :], in0=vslot(qq)[:, kk, :], scalar=cvec[:, 1, kt:kt + 1],
                                        in1=acc[:, 0, :] if kt else seed[:, :], op0=ALU.mult, op1=ALU.add).then_inc(vsum, 1)
                    if vecs:
                        take_loop_mod(23, r)

                with dve.Fori(0, 4 if more else 3) as r:
                    round_(r)
                if not more:
                    round_(3, 8 - LEAD)

            def take_loop_mod(n, r):
                dve.wait_ge(red_done, at_(n + 1, r, 2))
                nc.vector.tensor_copy(mod[:, bass.ds(r * 8 + (M1 + 16 + 4 * (n - 22)), 4)], bank[7][:, 0:4])\
                    .then_inc(mod_done, 1)

            take_mod(21)
            dve.wait_ge(y_zero, 1)
            mlp(U_M0, T, m_hi, m_lo, 0, True, True)
            gate_rows(3)
            layer_norm(1, TILES, lambda i: cres[:, i, :] if i < 2 else xres[:, i - 2, :], lambda i: grow[:, i // 2, :])
            affine(0, 1, M1C, M1C + 8)
            affine(2, 1, M1, M1 + 8)
            transposed(36, KT, T, a_hi, a_lo, trB, both)

            def rotate(src, m, dst):
                heads = lambda v: spread(v, [[AHD, 4], [AHD // 2, 2], [1, AHD // 4]])
                q4 = AHD // 4
                cs, sn = [spread(const(n)[:, m * 2 * q4:(m + 1) * 2 * q4], [[0, 4], [q4, 2], [1, q4]]) for n in ("cos", "sin")]
                t1, t2 = [prob1[i][:, m * UC:(m + 1) * UC] for i in range(2)]
                for half in (0, 1):
                    hs = slice(half * q4, UC)
                    nc.vector.tensor_tensor(heads(t1[:, hs]), heads(src[:, hs]), cs, ALU.mult)
                    last = nc.vector.tensor_tensor(heads(t2[:, hs]), heads(src[:, hs]), sn, ALU.mult)
                link(last)
                nc.vector.tensor_tensor(dst(0), heads(t1), heads(t2[:, q4:]), ALU.subtract)
                return nc.vector.tensor_tensor(dst(1), heads(t1[:, q4:]), heads(t2), ALU.add)

            dve.wait_ge(res_mul, 12)
            for u in range(U_QKV, U_OD):
                split_lo(u + LEAD)
                b, j = before[u], u - U_QKV
                if j == 0:
                    src = take(b + 1)
                    for m in range(NT):
                        kr = krow[:, NT + m, 0, 0, :]
                        last = rotate(src[:, m * UC:(m + 1) * UC], m,
                                      lambda half: spread(kr[:, half * 16:], [[2 * AHD, 4], [AHD // 2, 2], [1, 16]]))
                    link(last)
                    for m in range(NT):
                        last = nc.vector.tensor_copy(krow[:, NT + m, :, 1, :], krow[:, NT + m, :, 0, :])
                    last.then_inc(free[(b + 1) % 4], 1)
                elif j >= 2:
                    src = take(b)
                    for m in range(NT):
                        qr = qrow[:, m, (j - 2) * UC:(j - 1) * UC]
                        last = rotate(src[:, m * UC:(m + 1) * UC], m,
                                      lambda half: spread(qr[:, half * 16:], [[AHD, 4], [AHD // 2, 2], [1, 16]]))
                    last.then_inc(free[b % 4], 1)
                    taken(dve, b)
            dve.wait_ge(load_sk, 16)
            for n in range(len(wsteps) + 2):
                if n < len(wsteps):
                    qt, h = wsteps[n]
                    c = 8 + 4 * (n % 2)
                    dve.wait_ge(wa_s, n + 1)
                    link(nc.vector.tensor_reduce(stat[:, 16 + n % 2:17 + n % 2], bank[4 + n % 2][:, :], AX.X, ALU.max))
                    if n >= 2:
                        dve.wait_ge(wa_exp, n - 1)
                    nc.vector.tensor_scalar(stat[:, c:c + 1], stat[:, 16 + n % 2:17 + n % 2], sink[:, h:h + 1], -1.0,
                                            ALU.max, ALU.mult).then_inc(wa_max, 1)
                if n >= 2 and n % 2 == 0 and n <= len(wsteps):
                    i = n - 1
                    dve.wait_ge(wa_t, i + 1)
                    if i >= 2:
                        dve.wait_ge(wa_pv, i - 1)
                    nc.vector.tensor_copy(flat(probT1[1]), bank[7][:, :]).then_inc(wa_pt[1], 1)
                if n >= 2:
                    i = n - 2
                    qt, h = wsteps[i]
                    c = 8 + 4 * (i % 2)
                    dve.wait_ge(wa_exp, i + 1)
                    link(nc.vector.tensor_tensor(stat[:, 18:19], stat[:, c + 1:c + 2], stat[:, c + 2:c + 3], ALU.add))
                    link(nc.vector.reciprocal(stat[:, 19:20], stat[:, 18:19]))
                    dve.wait_ge(wa_pv, i + 1)
                    nc.vector.tensor_scalar(qrow[:, qt, h * AHD:(h + 1) * AHD], bank[i % 2][:, 0:AHD], stat[:, 19:20], None,
                                            ALU.mult).then_inc(wa_o, 1)
            transposed(44, KT, S, a_hi, a_lo, trB, lambda k: [(0, S, None, None)])
            for u in range(U_OD, U_M1):
                split_lo(u + LEAD)
            all_taken(dve, before[U_M1])
            gate_rows(5, 1)
            layer_norm(2, NT, lambda i: xres[:, i, :], lambda i: grow[:, 0, :])
            affine(0, 2, M1 + 24, M1 + 32)
            transposed(52, KT, S, a_hi, a_lo, trB, lambda k: [(0, S, aff[:, 0, k:k + 1], aff[:, 1, k:k + 1])])
            dve.wait_ge(y_zero, 2)
            mlp(U_M1, S, *half_m, 32, False, False)
            gate_rows(6, 1)
            layer_norm(3, NT, lambda i: xres[:, i, :], lambda i: grow[:, 0, :])


INS = ["x", "c", "norm_g", "w_ada", "b_ada", "w_in", "pool_w", "pool_scale", "w_attn_br", "w_pool_br", "w_out",
       "rel_bias", "final_g", "c_2", "ctx_2", "c_ctx_2", "w_mod_2", "b_mod_2", "ln_g_2", "ln_b_2", "mlp_w1_2",
       "mlp_w2_2", "ev_w_in_2", "ev_ret_theta_2", "ev_gla_gk_w_2", "ev_gla_gk_b_2", "ev_gla_norm_g_2", "ev_w_out_2",
       "od_w_qkv_2", "od_sink_2", "od_w_out_2"]


def kernel(**inputs):
    import concourse.bacc as bacc
    from concourse.bass_utils import run_bass_kernel_spmd as run

    nc = bacc.Bacc("TRN2", target_bir_lowering=False, num_devices=1)
    arrays, a = {}, {}
    for name in INS:
        v = np.ascontiguousarray(inputs[name])
        arrays[f"in_{name}"] = v
        a[name] = nc.dram_tensor(f"in_{name}", v.shape, mybir.dt.from_np(v.dtype), kind="ExternalInput").ap()
    table, at, keep = constants()
    arrays["table"] = table
    cst = nc.dram_tensor("table", table.shape, mybir.dt.float32, kind="ExternalInput").ap()
    scratch = nc.dram_tensor("distance_rows", [HEADS, GROUPS * 384], mybir.dt.float32).ap()
    out = nc.dram_tensor("out", [1, S, D], mybir.dt.float32, kind="ExternalOutput").ap()
    build(nc, a, out, cst, at, keep, scratch)
    r = run(nc, [arrays], core_ids=[0])
    return r.results[0]["out"]
```

```python
import math
from contextlib import ExitStack

import numpy as np

import concourse.bass as bass
from concourse import mybir

P = 128
D = 1024
KT = D // P
S = 256
NT = S // P
HEADS, HD, GROUPS = 8, 64, 3
DILS = (1, 4, 16)
N_BACK = 128
BUCKETS, MAX_DIST = 32, 2048
POOL_WINDOWS = (2, 4, 8, 16)
RH, DK, DV = 4, 64, 128
RANK, TAU = 16, 16.0
CH = 64
QH, KVH, AHD = 16, 4, 64
WINDOW = 128
ALPHA = (2.0 * 2) ** 0.25
EPS_RMS, EPS_LN = 1e-6, 1e-5
NEG = -1e30
UC = 256
W_IN, EV_IN, QKV, FF = 8192, 3104, 1536, 4096

RAW, SPL, LEAD, GSA, GSB = 2, 4, 3, 3, 2

ROWS = {}
_n = 0
for _name, _len in (("norm_g", 8), ("pool_scale", 4), ("ln_g", 32), ("ln_b", 32), ("c", 8), ("c_2", 8),
                    ("c_ctx", 8), ("final_g", 8), ("gla_g", 1)):
    ROWS[_name] = _n
    _n += _len
NROWS = _n


def constants():
    p = np.arange(P)
    parts, at, n = [], {}, 0

    def put(name, a):
        nonlocal n
        a = np.asarray(a, np.float32).reshape(a.shape[0], -1)
        full = np.zeros((P, a.shape[1]), np.float32)
        full[:a.shape[0]] = a
        parts.append(full)
        at[name] = (n, a.shape[1])
        n += a.shape[1]

    eye = np.eye(P)
    put("ident", eye)
    put("anti", eye[::-1])
    same = (p[:, None] // CH) == (p[None, :] // CH)
    put("tri_f", same & (p[:, None] <= p[None, :]))
    put("tri_b", same & (p[:, None] >= p[None, :]))
    put("strict_b", same & (p[:, None] > p[None, :]))
    c = np.arange(CH)
    put("pos", np.where(p[:, None] < CH, c[None] + 1, CH - c[None]))
    put("edge", np.stack([np.where(p[None, :] > p[:, None], NEG, 0), np.where(p[None, :] < p[:, None], NEG, 0)], 1))
    half = AHD // 2
    inv = (10000.0 ** (-np.arange(0, half, 2, dtype=np.float32) / half)).astype(np.float32)
    pos = np.arange(S)
    ang = np.stack([(pos // 64)[:, None].astype(np.float32) * inv, (pos % 64)[:, None].astype(np.float32) * inv], 1)
    ang = ang.reshape(NT, P, 2, half // 2).transpose(1, 0, 2, 3)
    put("cos", np.cos(ang))
    put("sin", np.sin(ang))
    keep = n
    w = np.arange(384)
    dist = 255 - w
    hot = np.zeros((BUCKETS + 1, GROUPS, 384))
    for g, dil in enumerate(DILS):
        ok = (dist >= 0) & (dist % dil == 0) & (dist <= N_BACK * dil)
        exact = BUCKETS // 2
        nf = np.maximum(dist, 1).astype(np.float32)
        large = exact + (np.log(nf / exact) / math.log(MAX_DIST / exact) * (BUCKETS - exact)).astype(np.int32)
        b = np.where(dist < exact, dist, np.minimum(large, BUCKETS - 1))
        hot[b[ok], g, w[ok]] = 1
        hot[BUCKETS, g, ~ok] = NEG
    put("hot", hot)
    t = np.arange(S)
    m = np.zeros((S, len(POOL_WINDOWS), S))
    for g, win in enumerate(POOL_WINDOWS):
        lo = np.maximum(t + 1 - win, 0)
        inside = (t[:, None] <= t[None, :]) & (t[:, None] >= lo[None, :])
        m[:, g] = inside / np.minimum(t + 1, win)[None, :] - np.eye(S)
    put("pool", m.reshape(NT, P, len(POOL_WINDOWS), S).transpose(1, 2, 0, 3))
    return np.concatenate(parts, 1), at, keep


class Count:

    def __init__(self, sem):
        self.sem, self.n, self.r, self.per = sem, 0, None, 0

    def up(self, k=1):
        self.n += k
        return self.n

    def at(self, back=0):
        v = self.n - back
        return v if self.r is None else v + self.r * self.per

    def loop(self, r, per):
        self.r, self.per = r, per

    def end(self, times):
        self.n += (times - 1) * self.per
        self.r = None


def build(nc, a, out, cst, at, keep, scratch, stop=9):
    f32, f32r = mybir.dt.float32, mybir.dt.float32r
    ALU, ACT, AX = mybir.AluOpType, mybir.ActivationFunctionType, mybir.AxisListType
    ctx = ExitStack()
    with ctx:
        sems = {}

        def sem(name):
            if name not in sems:
                sems[name] = ctx.enter_context(nc.semaphore(name))
            return sems[name]

        def sb(name, shape, dt=f32, where=ctx):
            return where.enter_context(nc.sbuf_tensor(name, shape, dt))

        def flat(t):
            return t[tuple([slice(None)] * len(t.shape))] if len(t.shape) == 2 else \
                t.rearrange({3: "p a b -> p (a b)", 4: "p a b c -> p (a b c)"}[len(t.shape)])

        def spread(v, dims):
            return bass.AP(tensor=v.tensor, offset=v.offset, ap=[list(v.ap[0])] + [list(d) for d in dims])

        C = sb("C", [P, keep])
        vecT = sb("vecT", [P, NROWS])
        cvec = sb("cvec", [P, 3, KT])
        mod = sb("mod", [P, 24 + 4 * 48])
        aff = sb("aff", [P, 8, KT])
        ones = sb("ones", [P, P])
        acc = sb("acc", [P, 2, 512])
        seed = sb("seed", [P, 512])
        stat = sb("stat", [P, 64])
        raw = [sb(f"raw{i}", [P, KT * UC]) for i in range(RAW)]
        whi = [sb(f"whi{i}", [P, KT * UC], f32r) for i in range(SPL)]
        wlo = [sb(f"wlo{i}", [P, KT * UC], f32r) for i in range(SPL)]
        bank = [ctx.enter_context(nc.psum_tensor(f"bank{i}", [P, 512], f32)) for i in range(8)]

        def const(name, rows=P):
            o, n = at[name]
            return C[0:rows, o:o + n]

        ident, anti = const("ident"), const("anti")

        xres = sb("xres", [P, NT, D])

        A = ExitStack()
        graw_a = [sb(f"graw_a{i}", [P, 2, 512], where=A) for i in range(GSA)]
        h_hi, h_lo = [sb(n, [P, KT, S], f32r, A) for n in ("h_hi", "h_lo")]
        mz_hi, mz_lo = [sb(n, [P, 4, S], f32r, A) for n in ("mz_hi", "mz_lo")]
        za = sb("za", [P, NT, 512], where=A)
        strip = [sb(f"strip{i}", [P, GROUPS, 256], where=A) for i in range(2)]
        prob = sb("prob", [P, 768], where=A)
        probT = [sb(f"probT{i}", [P, 4, P], where=A) for i in range(2)]
        trA = [flat(t) for t in probT]
        vrow = strip[0][0:NROWS, 0, 0:P]
        relb = strip[1][0:BUCKETS + 1, 0, 0:GROUPS * HEADS]
        pw = prob[:, 0:512].rearrange("p (g e) -> p g e", g=4)
        with ExitStack() as e:
            xrow = sb("xrow", [P, NT, D], where=e)
            hot = sb("hot", [BUCKETS + 1, GROUPS, 384], where=e)
            line = sb("line", [HEADS, GROUPS, 384], where=e)
        with ExitStack() as e:
            u_row = sb("u_row", [P, NT, 512], where=e)
            zpT = sb("zpT", [P, 4, S], where=e)
            poolM = sb("poolM", [P, 4, NT, S], where=e)
        gaT = sb("gaT", [P, KT, S], where=A)
        gpT = sb("gpT", [P, KT, S], where=A)
        with ExitStack() as e:
            qT = sb("qT", [P, GROUPS, 4, S], where=e)
            kT = sb("kT", [P, GROUPS, 4, S], where=e)
            vR = sb("vR", [P, GROUPS, NT, 512], where=e)
        with ExitStack() as e:
            at_hi, at_lo = [sb(n, [P, 4, S], f32r, e) for n in ("at_hi", "at_lo")]
            grow_a = sb("grow_a", [P, D], where=e)
            frow = sb("frow", [P, D], where=e)
            tmpa = sb("tmpa", [P, NT, D], where=e)
        A.close()
        T = 2 * S
        B = ExitStack()
        graw_b = [sb(f"graw_b{i}", [P, 2, 512], where=B) for i in range(GSB)]
        a_hi, a_lo = [sb(n, [P, KT, T], f32r, B) for n in ("a_hi", "a_lo")]
        trB = [sb(f"trB{i}", [P, T], where=B) for i in range(2)]
        with ExitStack() as e:
            gy = sb("gy", [P, 4, D], where=e)
            vv = sb("vv", [P, 4, 512], where=e)
            with ExitStack() as e2:
                crow = sb("crow", [P, 2, D], where=e2)
            qd = sb("qd", [P, 4, T], where=e)
            with ExitStack() as e2:
                lrT = sb("lrT", [RANK + 1, 2, T], where=e2)
                gkw = sb("gkw", [RANK + 1, 2, RH * DK], where=e2)
                lrR = sb("lrR", [P, 4, 2 * RANK], where=e2)
            ki = sb("ki", [P, 4, T], where=e)
            kir = sb("kir", [P, 4, P], where=e)
            with ExitStack() as e2:
                la = sb("la", [P, 4, 512], where=e2)
            kv = sb("kv", [P, 8, DV], where=e)
            sp = sb("sp", [P, 8, DV], where=e)
            dec = sb("dec", [P, 4, 8], where=e)
            lgam = sb("lgam", [P, 12], where=e)
            ssq = sb("ssq", [P, 3, 4, 8], where=e)
            ex = [sb(f"ex{i}", [P, T], where=e) for i in range(2)]
            sc = [sb(f"sc{i}", [P, 4, P], where=e) for i in range(2)]
            sc2 = sb("sc2", [P, 4, P], where=e)
        with ExitStack() as e:
            Y = sb("Y", [P, 4, D], where=e)
            bns = sb("bns", [P, 4, 2, 6], where=e)
            bna = sb("bna", [P, 4, 8], where=e)
            with ExitStack() as e2:
                cres = sb("cres", [P, 2, D], where=e2)
                with ExitStack() as e3:
                    grow = sb("grow", [P, 2, D], where=e3)
                    lrow = sb("lrow", [P, 2, D], where=e3)
                m_hi, m_lo = [sb(n, [P, KT, T], f32r, e2) for n in ("m_hi", "m_lo")]
                rel_ = sb("relu", [P, T], where=e2)
                sq_ = sb("sq", [P, T], where=e2)
            krow = Y[:, 0:2, :].rearrange("p i (m h c n) -> p (i m) h c n", m=2, h=KVH, c=2)
            qrow = Y[:, 2:4, :]
            prob1 = [Y[:, 2 + i // 2, (i % 2) * T:(i % 2 + 1) * T] for i in range(4)]
            v_hi, v_lo = [sb(n, [P, 4, UC], f32r, e) for n in ("v_hi", "v_lo")]
            q_both = sb("q_both", [P, QH, S], f32r, e)
            k_hi, k_lo = [sb(n, [P, KVH, T], f32r, e) for n in ("k_hi", "k_lo")]
            eye_r = sb("eye_r", [P, P], f32r, e)
            edge_r = sb("edge_r", [P, NT * P], f32r, e)
            wst = sb("wst", [P, 4, 6], where=e)
            pT_hi, pT_lo = [flat(a_lo)[:, i * 2048:(i + 1) * 2048].rearrange("p (b g q) -> p b g q", b=4, g=4) for i in range(2)]
            o_hi, o_lo = [flat(a_hi)[:, i * 2048:(i + 1) * 2048].rearrange("p (k n) -> p k n", k=KT) for i in range(2)]
            sink = stat[:, 44:60]
        half_m = [flat(t)[:, 0:KT * S].rearrange("p (k n) -> p k n", k=KT) for t in (m_hi, m_lo)]
        B.close()

        def bf(w, n):
            return w[:, 0:n].bitcast(f32)

        def block(w, k0, kt, c0, cols):
            return w[k0:k0 + kt * P, c0:c0 + cols].rearrange("(k p) n -> p k n", p=P)

        units = []

        def add(w, c0, cols, banks, kt=KT, k0=0):
            units.append((block(w, k0, kt, c0, cols), kt, cols, banks))

        w_in = a["w_in"][0]
        ATT = GROUPS * 3 * 512
        for c0 in (ATT + 512, ATT + 768, ATT + 1024, ATT + 1280):
            add(w_in, c0, UC, 1)
        for c0 in range(0, ATT + 512, UC):
            add(w_in, c0, UC, 1)
        for c0 in range(ATT + 1536, W_IN, UC):
            add(w_in, c0, UC, 1)
        for w in ("w_attn_br", "w_pool_br"):
            for c0 in (0, 512):
                add(a[w][0], c0, 512, 2, kt=4)
        for c0 in range(0, D, UC):
            add(a["w_out"][0], c0, UC, 1)
        U_GATES, U_BR, U_OUT = 24, 32, 36
        U_EV = len(units)
        ev = a["ev_w_in_2"][0]
        add(ev, EV_IN - 2 * RANK, 2 * RANK, 1)
        for c0 in (1536, 1792, 2048, 2304, 2560, 2816, 0, 256, 512, 768, 1024, 1280):
            add(ev, c0, UC, 2)
        U_EVO = len(units)
        for c0 in range(0, D, UC):
            add(a["ev_w_out_2"][0], c0, UC, 2)
        U_M0 = len(units)
        for r in range(4):
            for j in range(4):
                add(a["mlp_w1_2"][0], 1024 * r + UC * j, UC, 2)
            for j in range(4):
                add(a["mlp_w2_2"][0], UC * j, UC, 2, k0=1024 * r)
        U_QKV = len(units)
        qkv = a["od_w_qkv_2"][0]
        add(qkv, D, UC, 2)
        add(qkv, D + UC, UC, 2)
        for c0 in range(0, D, UC):
            add(qkv, c0, UC, 1)
        U_OD = len(units)
        for c0 in range(0, D, UC):
            add(a["od_w_out_2"][0], c0, UC, 1)
        U_M1 = len(units)
        for r in range(4):
            for j in range(4):
                add(a["mlp_w1_2"][1], 1024 * r + UC * j, UC, 1)
            for j in range(4):
                add(a["mlp_w2_2"][1], UC * j, UC, 1, k0=1024 * r)

        before = [0]
        for un in units:
            before.append(before[-1] + un[3])

        vblocks = [(a["w_ada"][0], a["b_ada"][0], n, [(0, 4 * n)]) for n in range(6)]
        M0, M0C, M1, M1C = 24, 72, 120, 168
        vblocks += [(a["w_mod_2"][0], a["b_mod_2"][0], n, [(1, M0 + 4 * n), (2, M0C + 4 * n)]) for n in range(12)]
        vblocks += [(a["w_mod_2"][1], a["b_mod_2"][1], n,
                     [(1, M1 + 4 * n)] + ([(2, M1C + 4 * n)] if n < 4 else [])) for n in range(12)]
        vops = [0]
        for vb in vblocks:
            for _ in range(4):
                vops.append(vops[-1] + 2 * len(vb[3]))
        Q_B = 56

        def vslot(q):
            return graw_a[q % GSA] if q < Q_B else graw_b[q % GSB]

        steps = [(qt, h) for qt in range(NT) for h in range(HEADS)]

        def rounds(n):
            return n if n < HEADS else HEADS + 2 * (n - HEADS)

        PRE_Q = 16
        FILLS = 5

        UNIT_Q = {u: 0 if u == U_EV else 2 for u in range(U_EV, U_M0)}
        U_Q = 88
        LOOP_Q = [[0, 1], [2, 3], [4, 5], [6, 7], [], [], [], []]
        LN_TILES = [4, 4, 2, 2]
        res_mul = sem("res_mul")
        res_parts = [(0, i) for i in range(4)] + [(1, i) for i in (2, 3)] + [(k, i) for k in (2, 3) for i in range(2)]
        TILES = 4

        def at_(v, r, per):
            return v if r is None else v + r * per

        def taken(eng, b):
            eng.wait_ge(free[b % 4], b // 4 + 1)

        def all_taken(eng, b):
            for i in range(min(4, b)):
                taken(eng, b - 1 - i)

        load_w, load_c, load_v, load_x, load_f = sem("load_w"), sem("load_c"), sem("load_v"), sem("load_x"), sem("load_f")
        raw_full = [sem(f"raw_full{i}") for i in range(RAW)]
        graw_full = [sem(f"graw_full{i}") for i in range(GSA + GSB)]
        seed_full = sem("seed_full")
        hi_done, lo_done, tile_done = sem("hi_done"), sem("lo_done"), sem("tile_done")
        free = [sem(f"bank_free{i}") for i in range(4)]
        vsum, red_done, mod_done = sem("vsum"), sem("red_done"), sem("mod_done")
        filled = sem("filled")
        tr_full, tr_tmp, tr_hi, tr_lo = sem("tr_full"), sem("tr_tmp"), sem("tr_hi"), sem("tr_lo")
        vchain = sem("vector_chain")
        vec_t, vec_c, cvec_done = sem("vec_t"), sem("vec_c"), sem("cvec_done")
        line_mm, line_done, line_out, strip_full = sem("line_mm"), sem("line_done"), sem("line_out"), [sem("strip_full0"), sem("strip_full1")]
        sq_sum, root, x_scaled = sem("sq_sum"), sem("root"), sem("x_scaled")
        mz_part = sem("mz_part")
        pool_mm, pool_ev, mz_tmp = sem("pool_mm"), sem("pool_ev"), sem("mz_tmp")
        at_s, at_mx, at_p, at_t, at_pt, at_pv, at_z = [sem(n) for n in ("at_s", "at_mx", "at_p", "at_t", "at_pt", "at_pv", "at_z")]
        merged, merged_hi, merged_lo = sem("merged"), sem("merged_hi"), sem("merged_lo")
        rowb, rowb_done = sem("rowb"), sem("rowb_done")
        x_new = sem("x_new")
        load_ctx, load_gk, load_th, load_ln, load_cr = [sem(n) for n in ("load_ctx", "load_gk", "load_th", "load_ln", "load_cr")]
        lr_t, lr_ev, z_mm, la_done, lg_done = [sem(n) for n in ("lr_t", "lr_ev", "z_mm", "la_done", "lg_done")]
        bc_mm, ex_done, qk_done, kt_mm, kir_done, kv_mm, kv_done, s_mm, sc_done, sp_done, o_mm, ss_done, gy_done = \
            [sem(n) for n in ("bc_mm", "ex_done", "qk_done", "kt_mm", "kir_done", "kv_mm", "kv_done", "s_mm",
                              "sc_done", "sp_done", "o_mm", "ss_done", "gy_done")]
        achain, y_scaled, y_zero = sem("act_chain"), sem("y_scaled"), sem("y_zero")
        ln_var, ln_root, ln_n = sem("ln_var"), sem("ln_root"), sem("ln_n")
        sq_done, hid_hi, hid_lo = sem("sq_done"), sem("hid_hi"), sem("hid_lo")
        out_done = sem("out_done")
        load_sk, kq_t, kq_hi, kq_ev, vhi_done = [sem(n) for n in ("load_sk", "kq_t", "kq_hi", "kq_ev", "vhi_done")]
        wa_s, wa_max, wa_exp, wa_rc, wa_n, wa_t, wa_hi, wa_lo, wa_pv, wa_oh, wa_o = [
            sem(n) for n in ("wa_s", "wa_max", "wa_exp", "wa_rc", "wa_n", "wa_t", "wa_hi", "wa_lo", "wa_pv", "wa_oh", "wa_o")]
        wsteps = [(qt, h) for qt in range(NT) for h in range(QH)]
        block_ = ctx.enter_context(nc.Block())

        def gfull(q):
            if q < Q_B:
                return graw_full[q % GSA], 16 * (q // GSA + 1)
            return graw_full[GSA + q % GSB], 16 * ((q - Q_B) // GSB + 1)

        @block_.sync
        def _(sp_):
            sp_.dma_start(C[:, :], cst[:, 0:keep]).then_inc(load_c, 16)
            for name, rows, src in (("norm_g", 8, a["norm_g"]), ("pool_scale", 4, a["pool_scale"]),
                                    ("ln_g", 32, a["ln_g_2"]), ("ln_b", 32, a["ln_b_2"]), ("c", 8, a["c"]),
                                    ("c_2", 8, a["c_2"]), ("c_ctx", 8, a["c_ctx_2"]), ("final_g", 8, a["final_g"]),
                                    ("gla_g", 1, a["ev_gla_norm_g_2"])):
                n = int(np.prod(src.shape))
                v = bass.AP(tensor=src.tensor, offset=src.offset, ap=[[P, rows], [1, P]])
                sp_.dma_start(vrow[ROWS[name]:ROWS[name] + rows, :], v).then_inc(load_v, 16)
            sp_.dma_start(xres[:, :, :], a["x"][0].rearrange("(m p) n -> p m n", p=P)).then_inc(load_x, 16)
            sp_.dma_start(hot[:, :, :], cst[0:BUCKETS + 1, at["hot"][0]:at["hot"][0] + GROUPS * 384]
                          .rearrange("p (g w) -> p g w", g=GROUPS)).then_inc(load_w, 16)
            sp_.wait_ge(filled, FILLS)
            sp_.dma_start(relb[0:BUCKETS, :], a["rel_bias"]).then_inc(load_w, 16)

            def load(u):
                src, kt, cols, _ = units[u]
                if u >= RAW:
                    sp_.wait_ge(lo_done, u - RAW + 1)
                sp_.dma_start(raw[u % RAW][:, 0:kt * cols].rearrange("p (k n) -> p k n", k=kt), src)\
                    .then_inc(raw_full[u % RAW], 16)

            for u in range(U_EV + LEAD):
                load(u)
            sp_.wait_ge(x_new, 6)
            sp_.dma_start(crow[:, :, :], a["ctx_2"][0].rearrange("(m p) n -> p m n", p=P)).then_inc(load_ctx, 16)
            for d in range(2):
                sp_.dma_start(gkw[0:RANK, d, :], a["ev_gla_gk_w_2"][0, d]).then_inc(load_gk, 16)
                sp_.dma_start(gkw[RANK:RANK + 1, d, :], a["ev_gla_gk_b_2"][0, d:d + 1]).then_inc(load_gk, 16)
                th = a["ev_ret_theta_2"]
                sp_.dma_start(lgam[64 * d:64 * d + 64, 0:4],
                              bass.AP(tensor=th.tensor, offset=th.offset + 4 * d, ap=[[0, 64], [1, 4]])).then_inc(load_th, 16)
            for u in range(U_EV + LEAD, U_EVO):
                load(u)
            for u in range(U_EVO, U_EVO + LEAD):
                load(u)

            def ln_rows(l, s):
                for i, v in enumerate((a["ln_g_2"], a["ln_b_2"])):
                    sp_.dma_start(lrow[:, i, :], bass.AP(tensor=v.tensor, offset=v.offset + (2 * l + s) * D,
                                                         ap=[[0, P], [1, D]])).then_inc(load_ln, 16)

            sp_.wait_ge(tr_full, 28)
            sp_.dma_start(cres[:, :, :], a["ctx_2"][0].rearrange("(m p) n -> p m n", p=P)).then_inc(load_cr, 16)
            ln_rows(0, 0)
            for u in range(U_EVO + LEAD, U_M0):
                load(u)

            def mlp_loads(l, u0):
                with sp_.Fori(0, 4) as r:
                    for j in range(8):
                        u = u0 + j
                        w = a["mlp_w1_2"][l][:, bass.ds(r * 1024 + UC * j, UC)] if j < 4 else \
                            a["mlp_w2_2"][l][bass.ds(r * 1024, 1024), UC * (j - 4):UC * (j - 3)]
                        sp_.wait_ge(lo_done, at_(u - RAW + 1, r, 8))
                        sp_.dma_start(raw[u % RAW][:, :].rearrange("p (k n) -> p k n", k=KT),
                                      w.rearrange("(k p) n -> p k n", p=P)).then_inc(raw_full[u % RAW], 16)

            mlp_loads(0, U_M0)
            for u in range(U_QKV, U_QKV + LEAD):
                load(u)
            sp_.wait_ge(tile_done, before[U_QKV])
            ln_rows(0, 1)
            sk = a["od_sink_2"]
            sp_.dma_start(sink, bass.AP(tensor=sk.tensor, offset=sk.offset, ap=[[0, P], [1, QH]])).then_inc(load_sk, 16)
            for u in range(U_QKV + LEAD, U_M1):
                load(u)
            sp_.wait_ge(wa_pv, len(wsteps) // 4)
            ln_rows(1, 0)
            mlp_loads(1, U_M1)
            sp_.wait_ge(tile_done, before[U_M1 + 32])
            ln_rows(1, 1)
            for m in range(NT):
                sp_.wait_ge(res_mul, 2 * (len(res_parts) - NT + m + 1))
                sp_.dma_start(out[0, m * P:(m + 1) * P, :], xres[:, m, :]).then_inc(out_done, 16)
            sp_.wait_ge(out_done, 16 * NT)
            sp_.wait_ge(line_out, 16)

        @block_.gpsimd
        def _(pool):
            pool.memset(seed[:, :], 0.0).then_inc(filled, 1)
            pool.memset(ones[:, :], 1.0).then_inc(filled, 1)
            pool.memset(relb, 1.0).then_inc(filled, 1)
            pool.memset(stat[:, 40:41], EPS_RMS).then_inc(filled, 1)
            pool.memset(stat[:, 41:42], EPS_LN).then_inc(filled, 1)
            pool.wait_ge(filled, FILLS)

            def load_q(q):
                w, b, n, vecs = vblocks[q // 4]
                if q % 4 == 0:
                    if q:
                        pool.wait_ge(vsum, vops[q - 3])
                    bias = bass.AP(tensor=b.tensor, offset=b.offset + 512 * n, ap=[[512, 1], [1, 512]])
                    pool.dma_start(seed[0:1, :], bias).then_inc(seed_full, 16)
                ring = GSA if q < Q_B else GSB
                if q >= ring:
                    pool.wait_ge(vsum, vops[q - ring + 1])
                pool.dma_start(vslot(q)[:, :, :], block(w, (q % 4) * 2 * P, 2, 512 * n, 512)).then_inc(gfull(q)[0], 16)

            for q in range(PRE_Q):
                load_q(q)
            pool.wait_ge(line_done, 3)
            pool.dma_start(scratch.rearrange("h (g w) -> h g w", g=GROUPS), line[:, :, :]).then_inc(line_out, 16)
            pool.wait_ge(tr_full, KT)
            pool.wait_ge(line_mm, 3)
            pool.wait_ge(line_out, 16)
            pool.dma_start(poolM[:, :, :, :], cst[:, at["pool"][0]:at["pool"][0] + at["pool"][1]]
                           .rearrange("p (g s t) -> p g s t", g=4, s=NT)).then_inc(load_f, 16)
            pool.dma_start(pw, a["pool_w"][0].rearrange("g c e -> c g e")).then_inc(load_f, 16)
            for u in range(U_GATES):
                load_q(PRE_Q + u)
            for n, (qt, h) in enumerate(steps):
                if n >= 2:
                    pool.wait_ge(at_s, n - 1)
                pool.dma_start(strip[n % 2][:, :, :],
                               bass.AP(tensor=scratch.tensor, offset=scratch.offset + h * GROUPS * 384,
                                       ap=[[1, P], [384, GROUPS], [1, 256]])).then_inc(strip_full[n % 2], 16)
                load_q(PRE_Q + U_GATES + n)
            pool.wait_ge(at_s, len(steps))
            pool.wait_ge(at_pv, rounds(len(steps)))
            fg = a["final_g"]
            Qn = PRE_Q + U_GATES + len(steps)
            pool.dma_start(frow[:, :], bass.AP(tensor=fg.tensor, offset=fg.offset, ap=[[0, P], [1, D]])).then_inc(load_f, 16)

            pool.wait_ge(x_new, 6)
            pool.memset(lrT[:, :, :], 1.0).then_inc(filled, 1)
            q = Qn
            while q < U_Q:
                load_q(q)
                q += 1

            done = Count(res_mul)

            def residual(l, s, parts):
                k = 2 * l + s
                pool.wait_ge(load_ln, 32 * (k + 1))
                for i, dst in parts:
                    pool.wait_ge(ln_n, sum(LN_TILES[:k]) + i + 1)
                    pool.tensor_tensor(dst, Y[:, i, :], lrow[:, 0, :], ALU.mult).then_inc(res_mul, 1)
                    pool.wait_ge(res_mul, done.up())
                    pool.tensor_tensor(dst, dst, lrow[:, 1, :], ALU.add).then_inc(res_mul, 1)
                    done.up()

            residual(0, 0, [(i, cres[:, i, :]) for i in range(2)] + [(i + 2, xres[:, i, :]) for i in range(2)])
            pool.wait_ge(tr_full, 36)
            pool.memset(Y[:, :, :], 0.0).then_inc(y_zero, 1)
            with pool.Fori(0, 4) as r:
                for j in range(8):
                    c = r * 1024 + 512 * (4 + j // 4)
                    if j % 4 == 0:
                        pool.wait_ge(vsum, at_(vops[U_Q] + 2 * (j - 3), r, 16))
                        pool.dma_start(seed[0:1, :], a["b_mod_2"][1:2, bass.ds(c, 512)]).then_inc(seed_full, 16)
                    pool.wait_ge(vsum, at_(vops[U_Q] + 2 * (j - 1), r, 16))
                    w = a["w_mod_2"][1][(j % 4) * 256:(j % 4) * 256 + 256, bass.ds(c, 512)]
                    pool.dma_start(vslot(U_Q + j)[:, :, :], w.rearrange("(k p) n -> p k n", p=P)).then_inc(gfull(U_Q + j)[0], 16)
            residual(0, 1, [(i + 2, xres[:, i, :]) for i in range(2)])
            for n in range(len(wsteps)):
                pool.wait_ge(wa_rc, n + 1)
                pool.tensor_scalar(prob1[n % 4], prob1[n % 4], wst[:, n % 4, 5:6], None, ALU.mult).then_inc(wa_n, 1)
            residual(1, 0, [(i, xres[:, i, :]) for i in range(2)])
            pool.wait_ge(tr_full, 52)
            pool.memset(Y[:, 0:NT, :], 0.0).then_inc(y_zero, 1)
            residual(1, 1, [(i, xres[:, i, :]) for i in range(2)])
            assert done.n == 2 * len(res_parts)

        @block_.tensor
        def _(pe):
            def col_unit(u, hi, lo, T, b, part=(0, 9)):
                _, kt, cols, banks = units[u]
                wh, wl = [w[u % SPL][:, 0:kt * cols].rearrange("p (k n) -> p k n", k=kt) for w in (whi, wlo)]
                pe.wait_ge(lo_done, u + 1)
                per = 512 // T
                for n in range(part[0], min(part[1], cols // P)):
                    bt = b + n // per
                    if n % per == 0 and bt >= 4:
                        pe.wait_ge(free[bt % 4], bt // 4)
                    o = bank[bt % 4][:, (n % per) * T:(n % per + 1) * T]
                    for k in range(kt):
                        for i, (w, x) in enumerate(((wh, hi), (wl, hi), (wh, lo))):
                            mm = nc.tensor.matmul(o, w[:, k, n * P:(n + 1) * P], x[:, k, 0:T],
                                                  start=(k == 0 and i == 0), stop=(k == kt - 1 and i == 2))
                    if n % per == per - 1:
                        mm.then_inc(tile_done, 1)

            def row_unit(u, hi, lo, tiles, b):
                _, kt, cols, banks = units[u]
                wh, wl = [w[u % SPL][:, 0:kt * cols].rearrange("p (k n) -> p k n", k=kt) for w in (whi, wlo)]
                pe.wait_ge(lo_done, u + 1)
                for i, m in enumerate(tiles):
                    bt = b + i // 2
                    if i % 2 == 0 and bt >= 4:
                        pe.wait_ge(free[bt % 4], bt // 4)
                    o = bank[bt % 4][:, (i % 2) * UC:(i % 2 + 1) * UC]
                    for k in range(kt):
                        for j, (w, x) in enumerate(((wh, hi), (wh, lo), (wl, hi))):
                            mm = nc.tensor.matmul(o, x[:, k, m * P:(m + 1) * P], w[:, k, :],
                                                  start=(k == 0 and j == 0), stop=(k == kt - 1 and j == 2))
                    if i % 2 == 1:
                        mm.then_inc(tile_done, 1)

            def reduce_block(n):
                vecs = vblocks[n][3]
                pe.wait_ge(vsum, vops[4 * n + 4])
                if n:
                    pe.wait_ge(mod_done, n)
                for v in range(len(vecs)):
                    for s in range(4):
                        mm = nc.tensor.matmul(bank[7][:, 4 * v + s:4 * v + s + 1], acc[:, v, s * P:(s + 1) * P],
                                              ones[:, 0:1], start=True, stop=True)
                mm.then_inc(red_done, 1)

            def transposes(t0, kts, T, src):
                for kt in range(kts):
                    t = t0 + kt
                    if t >= 2:
                        pe.wait_ge(tr_tmp, t - 1)
                    for i in range(T // P):
                        mm = nc.tensor.transpose(bank[4 + t % 2][:, i * P:(i + 1) * P], src(i, kt), ident)
                    mm.then_inc(tr_full, 1)

            def broadcast_row(col, b0):
                for k in range(KT):
                    mm = nc.tensor.matmul(bank[b0 + k // 4][:, (k % 4) * P:(k % 4 + 1) * P],
                                          spread(col(k), [[0, P]]), ident, start=True, stop=True)
                mm.then_inc(rowb, 1)

            pend = []
            qn = [0]

            def event(quarters):
                for n in pend:
                    reduce_block(n)
                pend.clear()
                if quarters and (qn[0] + quarters) // 4 > qn[0] // 4:
                    pend.append((qn[0] + quarters) // 4 - 1)
                qn[0] += quarters

            pe.wait_ge(load_c, 16)
            pe.wait_ge(load_v, 16 * 9)
            nc.tensor.transpose(bank[6][:, 0:NROWS], vrow, ident[0:NROWS, 0:NROWS]).then_inc(vec_t, 1)
            pe.wait_ge(load_w, 32)
            for g in range(GROUPS):
                if g == 2:
                    pe.wait_ge(vec_c, 1)
                nc.tensor.matmul(bank[4 + g][0:HEADS, 0:384], relb[:, g * HEADS:(g + 1) * HEADS], hot[:, g, :],
                                 start=True, stop=True).then_inc(line_mm, 1)
            pe.wait_ge(filled, FILLS)
            for n in range(4):
                reduce_block(n)
            pe.wait_ge(line_done, 3)
            pe.wait_ge(x_scaled, 1)
            transposes(0, KT, S, lambda i, k: xrow[:, i, k * P:(k + 1) * P])
            pe.wait_ge(tr_lo, KT)
            vdone = 4
            for u in range(U_GATES):
                if u in (0, 1) or (u >= 4 and (u - 4) % 6 in (4, 5) and u < 22) or u >= 22:
                    row_unit(u, h_hi, h_lo, range(NT), before[u])
                else:
                    col_unit(u, h_hi, h_lo, S, before[u])
                if u >= 4 and u % 4 == 0:
                    reduce_block(vdone)
                    vdone += 1
                if u == 3:
                    pe.wait_ge(load_f, 32)
                    all_taken(pe, 2)
                    for g in range(4):
                        for s in range(NT):
                            mm = nc.tensor.matmul(bank[4 + g // 2][:, (g % 2) * S:(g % 2 + 1) * S],
                                                  u_row[:, s, g * P:(g + 1) * P], poolM[:, g, s, :],
                                                  start=(s == 0), stop=(s == NT - 1))
                        if g % 2:
                            mm.then_inc(pool_mm, 1)
                    for g in range(4):
                        pe.wait_ge(pool_ev, g // 2 + 1)
                        mm = nc.tensor.matmul(bank[6 if g < 2 else 4][:, (g % 2) * S:(g % 2 + 1) * S], pw[:, g, :],
                                              trA[g // 2][:, (g % 2) * S:(g % 2 + 1) * S], start=True, stop=True)
                        if g % 2:
                            mm.then_inc(pool_mm, 1)

            pe.wait_ge(mz_tmp, 2)
            all_taken(pe, before[U_GATES])
            def logits(n, groups):
                qt, h = steps[n]
                W = P * (qt + 1)
                lane = slice(64 * (h % 2), 64 * (h % 2) + 64)
                if n:
                    pe.wait_ge(at_p, n)
                pe.wait_ge(strip_full[n % 2], 16 * (n // 2 + 1))
                for g in groups:
                    o = bank[4][:, g * W:(g + 1) * W] if g < 2 else bank[5][:, 0:W]
                    nc.tensor.matmul(o, qT[lane, g, h // 2, qt * P:(qt + 1) * P], kT[lane, g, h // 2, 0:W],
                                     start=True, stop=False)
                    mm = nc.tensor.matmul(o, anti, strip[n % 2][:, g, 256 - W:256], start=False, stop=True)
                if 2 in groups:
                    mm.then_inc(at_s, 1)

            def prob_transposes(n, j):
                rc = rounds(n) + j
                if rc:
                    pe.wait_ge(at_pt, rc)
                for b in range(3):
                    blk = 3 * j + b
                    mm = nc.tensor.transpose(bank[6][:, b * P:(b + 1) * P], prob[:, blk * P:(blk + 1) * P], ident)
                mm.then_inc(at_t, 1)

            def values(n, j):
                qt, h = steps[n]
                rc = rounds(n) + j
                pe.wait_ge(at_pt, rc + 1)
                pe.wait_ge(mod_done, vdone)
                for b in range(3):
                    blk = 3 * j + b
                    g, kb = divmod(blk, qt + 1)
                    mm = nc.tensor.matmul(bank[7][:, 384:384 + HD], probT[rc % 2][:, b, :], vR[:, g, kb, h * HD:(h + 1) * HD],
                                          start=(blk == 0), stop=(blk == 3 * (qt + 1) - 1), skip_group_check=True)
                mm.then_inc(at_pv, 1)

            logits(0, (0, 1, 2))
            for n, (qt, h) in enumerate(steps):
                more = n + 1 < len(steps)
                pe.wait_ge(at_p, n + 1)
                if n:
                    pe.wait_ge(at_z, n)
                prob_transposes(n, 0)
                if more:
                    logits(n + 1, (0, 1) if qt else (0, 1, 2))
                values(n, 0)
                if qt:
                    prob_transposes(n, 1)
                    if more:
                        logits(n + 1, (2,))
                    values(n, 1)
                u = U_GATES + n // 2
                col_unit(u, h_hi, h_lo, S, before[u], (n % 2, n % 2 + 1))
                if n % 4 == 0:
                    pe.wait_ge(at_z, n + 1)
                    reduce_block(vdone)
                    vdone += 1
            pe.wait_ge(at_z, len(steps))
            transposes(8, 4, S, lambda i, k: za[:, i, k * P:(k + 1) * P])
            pe.wait_ge(tr_lo, 12)
            pe.wait_ge(mz_part, 2)
            for u in (32, 33):
                col_unit(u, at_hi, at_lo, S, before[u])
            for u in (34, 35):
                col_unit(u, mz_hi, mz_lo, S, before[u])
            reduce_block(vdone)
            broadcast_row(lambda k: mod[:, 16 + k:17 + k], 4)
            pe.wait_ge(merged_lo, 1)
            for u in range(36, 40):
                row_unit(u, h_hi, h_lo, range(NT), before[u])

            qn[0] = PRE_Q + U_GATES + len(steps)
            pe.wait_ge(x_new, 6)
            pe.wait_ge(load_ctx, 16)
            transposes(12, KT, T, lambda i, k: crow[:, i, k * P:(k + 1) * P] if i < 2 else xres[:, i - 2, k * P:(k + 1) * P])
            pe.wait_ge(tr_lo, 20)
            u = U_EV
            b = before[u]
            wh, wl = [w[u % SPL][:, 0:KT * 32].rearrange("p (k n) -> p k n", k=KT) for w in (whi, wlo)]
            pe.wait_ge(lo_done, u + 1)
            pe.wait_ge(free[b % 4], b // 4)
            for m in range(TILES):
                for k in range(KT):
                    for j, (w, x) in enumerate(((wh, a_hi), (wh, a_lo), (wl, a_hi))):
                        mm = nc.tensor.matmul(bank[b % 4][:, m * 32:m * 32 + 32], x[:, k, m * P:(m + 1) * P], w[:, k, :],
                                              start=(k == 0 and j == 0), stop=(k == KT - 1 and j == 2))
            mm.then_inc(tile_done, 1)
            taken(pe, b)
            for d in range(2):
                for i in range(TILES):
                    mm = nc.tensor.transpose(bank[4 + d][0:RANK, i * P:(i + 1) * P], lrR[:, i, RANK * d:RANK * d + RANK], ident)
            mm.then_inc(lr_t, 1)
            pe.wait_ge(lr_ev, 2)
            pe.wait_ge(load_gk, 64)
            for i in range(TILES):
                if i >= 2:
                    pe.wait_ge(la_done, i - 1)
                for d in range(2):
                    mm = nc.tensor.matmul(bank[4 + i % 2][:, 256 * d:256 * d + 256], lrT[:, d, i * P:(i + 1) * P], gkw[:, d, :],
                                          start=True, stop=True)
                mm.then_inc(z_mm, 1)
            event(UNIT_Q[U_EV])

            def decay_sums(h):
                if h:
                    pe.wait_ge(ex_done, 2 * h)
                for i in range(TILES):
                    for d, tri in ((0, "tri_f"), (1, "tri_b")):
                        mm = nc.tensor.matmul(bank[6][64 * d:64 * d + 64, i * P:(i + 1) * P],
                                              la[:, i, 256 * d + DK * h:256 * d + DK * h + DK], const(tri),
                                              start=True, stop=True)
                mm.then_inc(bc_mm, 1)

            def head_sums(hd):
                gla, h = hd < RH, hd % RH
                pe.wait_ge(qk_done, 4 if gla else 8)
                if hd:
                    pe.wait_ge(kir_done, hd)
                for i in range(TILES):
                    mm = nc.tensor.transpose(bank[2][:, i * P:(i + 1) * P], ki[:, h, i * P:(i + 1) * P], ident)
                mm.then_inc(kt_mm, 1)
                if hd:
                    pe.wait_ge(sc_done, hd)
                for d in range(2):
                    rows = slice(64 * d, 64 * d + 64)
                    for i in range(TILES):
                        mm = nc.tensor.matmul(bank[d][:, i * P:(i + 1) * P], ki[rows, h, i * P:(i + 1) * P],
                                              qd[rows, h, i * P:(i + 1) * P], start=True, stop=True)
                mm.then_inc(s_mm, 1)
                if hd:
                    pe.wait_ge(kv_done, 2 * hd)
                pe.wait_ge(kir_done, hd + 1)
                for c in range(8):
                    rows = slice(64 * (c % 2), 64 * (c % 2) + 64)
                    mm = nc.tensor.matmul(bank[4 + c % 2][:, (c // 2) * DV:(c // 2 + 1) * DV], kir[rows, c // 2, :],
                                          vv[rows, c // 2, h * DV:(h + 1) * DV], start=True, stop=True)
                mm.then_inc(kv_mm, 1)

            def head_out(hd):
                h = hd % RH
                pe.wait_ge(sc_done, hd + 1)
                pe.wait_ge(sp_done, hd + 1)
                if hd:
                    pe.wait_ge(gy_done, hd)
                for i in range(TILES):
                    nc.tensor.matmul(bank[6][:, i * P:(i + 1) * P], sc[hd % 2][:, i, :], vv[:, i, h * DV:(h + 1) * DV],
                                     start=True, stop=False, skip_group_check=True)
                    for half in range(2):
                        c = 2 * i + half
                        mm = nc.tensor.matmul(bank[6][64 * half:64 * half + 64, i * P:(i + 1) * P], qd[:, h, c * CH:(c + 1) * CH],
                                              sp[:, c, :], start=False, stop=True, skip_group_check=True)
                mm.then_inc(o_mm, 1)

            def heads(first):
                head_sums(first)
                for hd in range(first, first + RH):
                    if hd + 1 < first + RH:
                        head_sums(hd + 1)
                    head_out(hd)

            def mixer_units(u0):
                for u in range(u0, u0 + 6):
                    if u - u0 < 2:
                        col_unit(u, a_hi, a_lo, T, before[u])
                    else:
                        row_unit(u, a_hi, a_lo, range(TILES), before[u])
                    event(UNIT_Q[u])

            mixer_units(U_EV + 1)
            all_taken(pe, before[U_EV + 7])
            for h in range(RH):
                decay_sums(h)
            heads(0)
            mixer_units(U_EV + 7)
            all_taken(pe, before[U_EV + 13])
            heads(RH)
            pe.wait_ge(y_scaled, 1)
            transposes(20, KT, T, lambda i, k: gy[:, i, k * P:(k + 1) * P])
            pe.wait_ge(tr_lo, 28)
            for u in range(U_EVO, U_M0):
                row_unit(u, a_hi, a_lo, range(TILES), before[u])
                event(UNIT_Q[u])
            assert qn[0] == U_Q and pend == [21], (qn, pend)
            event(0)

            def gate_rows(cols, n0):
                for i, c in enumerate(cols):
                    if n0 + i > 1:
                        pe.wait_ge(rowb_done, n0 + i)
                    broadcast_row(lambda k: mod[:, c + k:c + k + 1], 4)

            gate_rows((M0C + 16, M0 + 16), 1)
            pe.wait_ge(ln_n, 4)
            transposes(28, KT, T, lambda i, k: Y[:, i, k * P:(k + 1) * P])
            pe.wait_ge(tr_lo, 36)

            def mlp(u0, hi, lo, Tn, mh, ml, hid0, vecs):
                per, tiles = 8 * Tn // 256, Tn // P
                ht = 4 * Tn // 256

                def round_(r):
                    for j in range(8):
                        u, b = u0 + j, before[u0 + j]
                        wh, wl = [w[u % SPL][:, :].rearrange("p (k n) -> p k n", k=KT) for w in (whi, wlo)]
                        pe.wait_ge(lo_done, at_(u + 1, r, 8))
                        if j == 4:
                            pe.wait_ge(hid_lo, at_(hid0 + ht, r, ht))
                        n_out = 2 if j < 4 else tiles
                        per_bank = 512 // Tn if j < 4 else 2
                        for n in range(n_out):
                            bt = b + n // per_bank
                            if n % per_bank == 0:
                                pe.wait_ge(free[bt % 4], at_(bt // 4, r, per // 4))
                            w = 512 // per_bank
                            o = bank[bt % 4][:, (n % per_bank) * w:(n % per_bank + 1) * w]
                            for k in range(KT):
                                if j < 4:
                                    trio = [(wh[:, k, n * P:(n + 1) * P], hi[:, k, 0:Tn]), (wl[:, k, n * P:(n + 1) * P], hi[:, k, 0:Tn]),
                                            (wh[:, k, n * P:(n + 1) * P], lo[:, k, 0:Tn])]
                                else:
                                    trio = [(mh[:, k, n * P:(n + 1) * P], wh[:, k, :]), (mh[:, k, n * P:(n + 1) * P], wl[:, k, :]),
                                            (ml[:, k, n * P:(n + 1) * P], wh[:, k, :])]
                                for i, (x, y) in enumerate(trio):
                                    mm = nc.tensor.matmul(o, x, y, start=(k == 0 and i == 0), stop=(k == KT - 1 and i == 2))
                            if n % per_bank == per_bank - 1:
                                mm.then_inc(tile_done, 1)
                        if vecs and j in (1, 3):
                            n = 22 + j // 2
                            pe.wait_ge(vsum, at_(vops[U_Q] + 8 * (j // 2 + 1), r, 16))
                            pe.wait_ge(mod_done, at_(n, r, 2))
                            for s_ in range(4):
                                mm = nc.tensor.matmul(bank[7][:, s_:s_ + 1], acc[:, 0, s_ * P:(s_ + 1) * P], ones[:, 0:1],
                                                      start=True, stop=True)
                            mm.then_inc(red_done, 1)

                with pe.Fori(0, 4) as r:
                    round_(r)

            mlp(U_M0, a_hi, a_lo, T, m_hi, m_lo, 0, True)
            gate_rows((M0C + 40, M0 + 40), 3)
            pe.wait_ge(ln_n, 8)
            transposes(36, KT, T, lambda i, k: Y[:, i, k * P:(k + 1) * P])

            pe.wait_ge(tr_lo, 44)

            def transpose_q(j):
                taken(pe, before[U_QKV + 2 + j])
                if j:
                    pe.wait_ge(kq_ev, KVH)
                for p_ in range(2):
                    for m in range(NT):
                        mm = nc.tensor.transpose(bank[4 + j][:, (NT * p_ + m) * P:(NT * p_ + m + 1) * P],
                                                 qrow[:, m, (2 * j + p_) * P:(2 * j + p_ + 1) * P], ident)
                mm.then_inc(kq_t, 1)

            for u in range(U_QKV, U_OD):
                j = u - U_QKV - 2
                row_unit(u, a_hi, a_lo, range(TILES) if j < 0 else range(NT, TILES), before[u])
                if j == 0:
                    all_taken(pe, before[U_QKV + 1])
                    pe.wait_ge(mod_done, len(vblocks))
                    for n in range(KVH):
                        for m in range(TILES):
                            mm = nc.tensor.transpose(bank[4 + n][:, m * P:(m + 1) * P],
                                                     krow[:, m, n, :, :].rearrange("p a b -> p (a b)"), ident)
                        mm.then_inc(kq_t, 1)
                    pe.wait_ge(kq_ev, KVH)
                if j >= 1:
                    transpose_q(j - 1)
            transpose_q(3)
            all_taken(pe, before[U_OD])
            N = len(wsteps)
            for n in range(N + 4):
                if n < N:
                    qt, h = wsteps[n]
                    pe.wait_ge(kq_ev, KVH + max(h // 4, n % 2) + 1)
                    if n >= 2:
                        pe.wait_ge(wa_exp, n - 1)
                    o = bank[4 + n % 2]
                    cut = S + P * (1 - qt)
                    nc.tensor.matmul(o[:, :], q_both[:, h, qt * P:(qt + 1) * P], k_hi[:, h // 4, :],
                                     start=True, stop=False, skip_group_check=True)
                    nc.tensor.matmul(o[:, :], q_both[:, h, qt * P:(qt + 1) * P], k_lo[:, h // 4, :],
                                     start=False, stop=False, skip_group_check=True)
                    nc.tensor.matmul(o[:, cut:cut + P], eye_r[:, :], edge_r[:, qt * P:(qt + 1) * P],
                                     start=False, stop=True, skip_group_check=True).then_inc(wa_s, 1)
                if n >= 7 and n % 4 == 3:
                    g = (n - 7) // 4
                    kv_ = wsteps[4 * g][1] // 4
                    pe.wait_ge(wa_lo, 4 * g + 4)
                    if g >= 2:
                        pe.wait_ge(wa_o, g - 1)
                    for b in range(4):
                        vs = slice(kv_ * AHD, (kv_ + 1) * AHD)
                        for j, (x, y) in enumerate(((v_hi, pT_hi), (v_lo, pT_hi), (v_hi, pT_lo))):
                            mm = nc.tensor.matmul(bank[g % 2][0:AHD, :], x[:, b, vs], y[:, b, :, :].rearrange("p g q -> p (g q)"),
                                                  start=(b == 0 and j == 0), stop=(b == 3 and j == 2))
                    mm.then_inc(wa_pv, 1)
                if 2 <= n < N + 2:
                    i = n - 2
                    pe.wait_ge(wa_n, i + 1)
                    pe.wait_ge(kq_ev, 8)
                    if i >= 2:
                        pe.wait_ge(wa_lo, i - 1)
                    for b in range(4):
                        mm = nc.tensor.transpose(bank[6 + i % 2][:, b * P:(b + 1) * P], prob1[i % 4][:, b * P:(b + 1) * P], ident)
                    mm.then_inc(wa_t, 1)
            pe.wait_ge(wa_o, N // 4)
            for u in range(U_OD, U_M1):
                row_unit(u, o_hi, o_lo, range(NT), before[u])
            gate_rows((M1 + 16,), 5)
            pe.wait_ge(ln_n, 10)
            transposes(44, KT, S, lambda i, k: Y[:, i, k * P:(k + 1) * P])
            pe.wait_ge(tr_lo, 52)
            mlp(U_M1, a_hi, a_lo, S, *half_m, 32, False)
            gate_rows((M1 + 40,), 6)

        @block_.scalar
        def _(act):
            def split_hi(u):
                if u >= len(units):
                    return
                _, kt, cols, _b = units[u]
                act.wait_ge(raw_full[u % RAW], 16 * (u // RAW + 1))
                if u >= SPL:
                    act.wait_ge(tile_done, before[u - SPL + 1])
                nc.scalar.activation(whi[u % SPL][:, 0:kt * cols], raw[u % RAW][:, 0:kt * cols], ACT.Copy).then_inc(hi_done, 1)

            def transposed_hi(t0, kts, T, hi, tmp):
                for kt in range(kts):
                    t = t0 + kt
                    act.wait_ge(tr_tmp, t + 1)
                    nc.scalar.activation(hi[:, kt, 0:T], tmp[t % 2][:, 0:T], ACT.Copy).then_inc(tr_hi, 1)

            def take(b):
                act.wait_ge(tile_done, b + 1)
                return bank[b % 4]

            act.wait_ge(load_x, 16)
            for m in range(NT):
                nc.scalar.activation(flat(za), xres[:, m, :], ACT.Square, accum_out=stat[:, m:m + 1]).then_inc(sq_sum, 1)
                act.wait_ge(sq_sum, m + 1)
            act.wait_ge(vec_c, 3)
            nc.scalar.activation(stat[:, 2:4], stat[:, 0:2], ACT.Sqrt, bias=stat[:, 40:41], scale=1.0 / D).then_inc(root, 1)
            c0 = ROWS["c"]
            nc.scalar.activation(cvec[:, 0, :], vecT[:, c0:c0 + 8], ACT.Copy)
            nc.scalar.activation(cvec[:, 1:3, :], vecT[:, c0 + 8:c0 + 24].rearrange("p (a b) -> p a b", a=2), ACT.Silu)\
                .then_inc(cvec_done, 1)
            for u in range(LEAD):
                split_hi(u)
            transposed_hi(0, KT, S, h_hi, trA)
            for u in range(U_GATES):
                split_hi(u + LEAD)
                b = before[u]
                src = take(b)[:, :].rearrange("p (m n) -> p m n", m=2)
                if u < 2:
                    dst, f, kw = u_row[:, :, u * UC:(u + 1) * UC], ACT.Copy, {}
                elif u < 4:
                    dst, f, kw = zpT[:, 2 * (u - 2):2 * (u - 1), :], ACT.Silu, {}
                elif u < 22:
                    g, j = divmod(u - 4, 6)
                    if j < 2:
                        dst, f, kw = qT[:, g, 2 * j:2 * j + 2, :], ACT.Copy, {"scale": HD ** -0.5}
                    elif j < 4:
                        continue
                    else:
                        dst, f, kw = vR[:, g, :, (j - 4) * UC:(j - 3) * UC], ACT.Copy, {}
                else:
                    dst, f, kw = za[:, :, (u - 22) * UC:(u - 21) * UC], ACT.Silu, {}
                nc.scalar.activation(dst, src, f, **kw).then_inc(free[b % 4], 1)
                if u == 3:
                    for g in range(2):
                        act.wait_ge(pool_mm, g + 1)
                        nc.scalar.activation(trA[g], bank[4 + g][:, :], ACT.Copy).then_inc(pool_ev, 1)
                    act.wait_ge(mz_tmp, 2)
                    nc.scalar.activation(flat(mz_hi), flat(u_row), ACT.Copy).then_inc(mz_part, 1)
            def gate_unit(i):
                b = before[U_GATES + i]
                dst = gaT if i < 4 else gpT
                nc.scalar.activation(dst[:, 2 * (i % 4):2 * (i % 4) + 2, :],
                                     take(b)[:, :].rearrange("p (m n) -> p m n", m=2), ACT.Sigmoid).then_inc(free[b % 4], 1)

            for n, (qt, h) in enumerate(steps):
                W = P * (qt + 1)
                act.wait_ge(at_mx, n + 1)
                if n:
                    act.wait_ge(at_t, rounds(n))
                nc.scalar.activation(prob[:, 0:2 * W], bank[4][:, 0:2 * W], ACT.Exp, bias=stat[:, 10:11],
                                     accum_out=stat[:, 12:13])
                nc.scalar.activation(prob[:, 2 * W:3 * W], bank[5][:, 0:W], ACT.Exp, bias=stat[:, 10:11],
                                     accum_out=stat[:, 13:14]).then_inc(at_p, 1)
                if n % 2 == 0 and n:
                    gate_unit(n // 2 - 1)
                if n % 2 == 0:
                    split_hi(U_GATES + n // 2 + LEAD)
            gate_unit(7)
            transposed_hi(8, 4, S, at_hi, trA)
            for u in range(32, 36):
                split_hi(u + LEAD)
            act.wait_ge(merged, 1)
            nc.scalar.activation(flat(h_hi), flat(gaT), ACT.Copy).then_inc(merged_hi, 1)
            for u in range(36, 40):
                split_hi(u + LEAD)
            act.wait_ge(x_new, 4)
            for m in range(NT):
                i = nc.scalar.activation(tmpa[:, m, :], xres[:, m, :], ACT.Square, accum_out=stat[:, m:m + 1])
            i.then_inc(sq_sum, 1)
            act.wait_ge(sq_sum, 3)
            nc.scalar.activation(stat[:, 2:4], stat[:, 0:2], ACT.Sqrt, bias=stat[:, 40:41], scale=1.0 / D).then_inc(root, 1)

            link = Count(achain)

            def step(ins):
                ins.then_inc(achain, 1)
                act.wait_ge(achain, link.up())

            transposed_hi(12, KT, T, a_hi, trB)
            split_hi(U_EV + LEAD)
            b = before[U_EV]
            nc.scalar.activation(flat(lrR), take(b)[:, 0:P], ACT.Copy).then_inc(free[b % 4], 1)
            act.wait_ge(lr_t, 1)
            act.wait_ge(filled, FILLS + 1)
            for d in range(2):
                nc.scalar.activation(lrT[0:RANK, d, :], bank[4 + d][0:RANK, :], ACT.Copy).then_inc(lr_ev, 1)
            for i in range(TILES):
                act.wait_ge(z_mm, i + 1)
                if i:
                    act.wait_ge(la_done, i)
                step(nc.scalar.activation(ex[0][:, :], bank[4 + i % 2][:, :], ACT.Abs))
                step(nc.scalar.activation(ex[0][:, :], ex[0][:, :], ACT.Exp, scale=-1.0))
                nc.scalar.activation(ex[1][:, :], ex[0][:, :], ACT.Ln, bias=1.0).then_inc(lg_done, 1)
            act.wait_ge(load_th, 32)
            step(nc.scalar.activation(lgam[:, 4:8], lgam[:, 0:4], ACT.Exp))
            step(nc.scalar.activation(lgam[:, 4:8], lgam[:, 4:8], ACT.Ln, bias=1.0, scale=-1.0))
            step(nc.scalar.activation(lgam[:, 8:12], lgam[:, 4:8], ACT.Copy, scale=-1.0))

            def mixer_units(u0, group):
                for u in range(u0, u0 + 6):
                    split_hi(u + LEAD)
                    b, j = before[u], u - u0
                    if j == 0:
                        for n in range(2):
                            if group:
                                act.wait_ge(o_mm, RH)
                            src = take(b + n)
                            for hh in range(2):
                                for half in range(2):
                                    last = nc.scalar.activation(qd[64 * half:64 * half + 64, 2 * n + hh, :],
                                                                src[64 * hh:64 * hh + 64, :], ACT.Copy,
                                                                scale=1.0 if group else DK ** -0.5)
                            last.then_inc(free[(b + n) % 4], 1)
                    elif j >= 2:
                        for i in range(2):
                            src = take(b + i)[:, :].rearrange("p (m n) -> p m n", m=2)
                            c0 = (j % 2) * UC
                            if j < 4:
                                nc.scalar.activation(vv[:, 2 * i:2 * i + 2, c0:c0 + UC], src, ACT.Copy).then_inc(free[(b + i) % 4], 1)
                            else:
                                c0 += 0 if group else 512
                                nc.scalar.activation(gy[:, 2 * i:2 * i + 2, c0:c0 + UC], src, ACT.Silu).then_inc(free[(b + i) % 4], 1)

            def decays(hd):
                gla, h = hd < RH, hd % RH
                if hd:
                    if hd >= RH:
                        act.wait_ge(ss_done, RH)
                    act.wait_ge(qk_done, hd)
                if gla:
                    act.wait_ge(bc_mm, hd + 1)
                    nc.scalar.activation(ex[0][:, :], bank[6][:, :], ACT.Exp, scale=1.0 / TAU).then_inc(ex_done, 1)
                    nc.scalar.activation(ex[1][:, :], bank[6][:, :], ACT.Exp, scale=-1.0 / TAU).then_inc(ex_done, 1)
                else:
                    nc.scalar.activation(ex[0][:, 0:CH], const("pos"), ACT.Exp, scale=lgam[:, 4 + h:5 + h]).then_inc(ex_done, 1)
                    nc.scalar.activation(ex[1][:, 0:CH], const("pos"), ACT.Exp, scale=lgam[:, 8 + h:9 + h]).then_inc(ex_done, 1)

            def head_sums(hd):
                act.wait_ge(kt_mm, hd + 1)
                if hd:
                    act.wait_ge(kv_mm, hd)
                nc.scalar.activation(flat(kir), bank[2][:, :], ACT.Copy).then_inc(kir_done, 1)
                act.wait_ge(kv_mm, hd + 1)
                if hd:
                    act.wait_ge(sp_done, hd)
                for i in range(2):
                    nc.scalar.activation(kv[:, i:8:2, :], bank[4 + i][:, :].rearrange("p (c n) -> p c n", c=4),
                                         ACT.Copy).then_inc(kv_done, 1)

            def head_out(hd):
                gla, h = hd < RH, hd % RH
                if hd:
                    act.wait_ge(ss_done, hd)
                act.wait_ge(o_mm, hd + 1)
                col = h + (RH if gla else 0)
                for i in range(TILES):
                    last = nc.scalar.activation(ex[1][:, i * P:(i + 1) * P], bank[6][:, i * P:(i + 1) * P], ACT.Square,
                                                accum_out=ssq[:, 0, i, col:col + 1])
                last.then_inc(ss_done, 1)

            for g in range(2):
                mixer_units(U_EV + 1 + 6 * g, g)
                for hd in range(4 * g, 4 * g + 4):
                    decays(hd)
                head_sums(4 * g)
                for hd in range(4 * g, 4 * g + 4):
                    if hd < 4 * g + 3:
                        head_sums(hd + 1)
                    head_out(hd)
            act.wait_ge(ss_done, 8)
            nc.scalar.activation(ssq[:, 1, :, :], ssq[:, 0, :, :], ACT.Sqrt, bias=stat[:, 40:41], scale=1.0 / DV).then_inc(root, 1)
            transposed_hi(20, KT, T, a_hi, trB)
            for u in range(U_EVO, U_M0):
                split_hi(u + LEAD)
                b = before[u]
                cs = slice((u - U_EVO) * UC, (u - U_EVO + 1) * UC)
                for i in range(2):
                    nc.scalar.activation(Y[:, 2 * i:2 * i + 2, cs], take(b + i)[:, :].rearrange("p (m n) -> p m n", m=2),
                                         ACT.Copy).then_inc(free[(b + i) % 4], 1)

            def ln_roots(k, tiles):
                act.wait_ge(ln_var, k + 1)
                nc.scalar.activation(bna[:, 0:tiles, 2], bna[:, 0:tiles, 1], ACT.Sqrt, bias=stat[:, 41:42]).then_inc(ln_root, 1)

            ln_roots(0, TILES)
            transposed_hi(28, KT, T, a_hi, trB)

            def mlp(u0, Tn, mh, hid0, more):
                per = 8 * Tn // 256
                ht = 4 * Tn // 256

                def round_(r, lead=8):
                    for j in range(8):
                        u = u0 + j + LEAD
                        tn = Tn // 256
                        if j < lead:
                            act.wait_ge(raw_full[u % RAW], at_(16 * (u // RAW + 1), r, 16 * 8 // RAW))
                            act.wait_ge(tile_done, at_(before[u0] + tn * (j + LEAD - SPL + 1), r, per))
                            nc.scalar.activation(whi[u % SPL][:, :], raw[u % RAW][:, :], ACT.Copy).then_inc(hi_done, 1)
                        if j >= 4:
                            continue
                        if j == 0:
                            act.wait_ge(tile_done, at_(before[u0], r, per))
                        for i in range(tn):
                            bt, t = before[u0 + j] + i, tn * j + i
                            act.wait_ge(tile_done, at_(bt + 1, r, per))
                            nc.scalar.activation(rel_[:, :], bank[bt % 4][:, :], ACT.Relu).then_inc(free[bt % 4], 1)
                            act.wait_ge(sq_done, at_(hid0 + t + 1, r, ht))
                            nc.scalar.activation(flat(mh)[:, 512 * t:512 * t + 512], sq_[:, :], ACT.Copy).then_inc(hid_hi, 1)

                with act.Fori(0, 4 if more else 3) as r:
                    round_(r)
                if not more:
                    round_(3, 8 - LEAD)

            mlp(U_M0, T, m_hi, 0, True)
            ln_roots(1, TILES)
            transposed_hi(36, KT, T, a_hi, trB)

            def take_transposed(n):
                act.wait_ge(kq_t, n + 1)
                src = bank[4 + n % 4][:, :]
                if n < KVH:
                    nc.scalar.activation(k_hi[:, n, :], src, ACT.Copy).then_inc(kq_hi, 1)
                else:
                    j = n - KVH
                    for half in range(2):
                        hs = slice(64 * half, 64 * half + 64)
                        last = nc.scalar.activation(q_both[hs, 4 * j + half:4 * j + 4:2, :],
                                                    src[hs, :].rearrange("p (a b) -> p a b", a=2), ACT.Copy, scale=AHD ** -0.5)
                    last.then_inc(kq_hi, 1)

            act.wait_ge(res_mul, 12)
            nc.scalar.activation(eye_r[:, :], ident, ACT.Copy)
            nc.scalar.activation(edge_r[:, :], const("edge"), ACT.Copy)
            for u in range(U_QKV, U_OD):
                split_hi(u + LEAD)
                b, j = before[u], u - U_QKV
                if j == 0:
                    src = take(b)[:, :].rearrange("p (m h n) -> p m h n", m=2, h=KVH)
                    for m in range(2):
                        for i in range(2):
                            last = nc.scalar.activation(krow[:, m, :, i, :], src[:, m, :, :], ACT.Copy)
                    last.then_inc(free[b % 4], 1)
                elif j == 1:
                    for i in range(2):
                        nc.scalar.activation(v_hi[:, 2 * i:2 * i + 2, :], take(b + i)[:, :].rearrange("p (m n) -> p m n", m=2),
                                             ACT.Copy).then_inc(vhi_done, 1)
                elif j == 2:
                    for n in range(KVH):
                        take_transposed(n)
                else:
                    take_transposed(KVH + j - 3)
            take_transposed(7)
            act.wait_ge(load_sk, 16)
            N = len(wsteps)
            def wa_transposed(i):
                if i and i % 4 == 0:
                    g = i // 4 - 1
                    qt, kv_ = wsteps[4 * g][0], wsteps[4 * g][1] // 4
                    act.wait_ge(wa_pv, g + 1)
                    for half in range(2):
                        last = nc.scalar.activation(o_hi[64 * half:64 * half + 64, 2 * kv_:2 * kv_ + 2, qt * P:(qt + 1) * P],
                                                    bank[g % 2][0:AHD, :].rearrange("p (a b q) -> p a b q", a=2, b=2)[:, :, half, :],
                                                    ACT.Copy)
                    last.then_inc(wa_oh, 1)
                if i == N:
                    return
                act.wait_ge(wa_t, i + 1)
                nc.scalar.activation(pT_hi[:, :, i % 4, :], bank[6 + i % 2][:, :].rearrange("p (b q) -> p b q", b=4),
                                     ACT.Copy).then_inc(wa_hi, 1)

            def wa_probs(n):
                h = wsteps[n][1]
                act.wait_ge(wa_max, n + 1)
                if n >= 4:
                    act.wait_ge(wa_t, n - 3)
                nc.scalar.activation(prob1[n % 4], bank[4 + n % 2][:, :], ACT.Exp, bias=wst[:, n % 4, 1:2],
                                     accum_out=wst[:, n % 4, 2:3])
                nc.scalar.activation(wst[:, n % 4, 3:4], sink[:, h:h + 1], ACT.Exp, bias=wst[:, n % 4, 1:2]).then_inc(wa_exp, 1)

            for n in range(N + 4):
                if n >= 3:
                    wa_transposed(n - 3)
                if n < N:
                    wa_probs(n)
            for u in range(U_OD, U_M1):
                split_hi(u + LEAD)
                b = before[u]
                cs = slice((u - U_OD) * UC, (u - U_OD + 1) * UC)
                nc.scalar.activation(Y[:, 0:2, cs], take(b)[:, :].rearrange("p (m n) -> p m n", m=2), ACT.Copy).then_inc(free[b % 4], 1)
            ln_roots(2, NT)
            transposed_hi(44, KT, S, a_hi, trB)
            mlp(U_M1, S, half_m[0], 32, False)
            ln_roots(3, NT)

        @block_.vector
        def _(dve):
            chain = Count(vchain)

            def link(ins):
                ins.then_inc(vchain, 1)
                chain.up()
                dve.wait_ge(vchain, chain.at())

            def split_lo(u):
                if u >= len(units):
                    return
                _, kt, cols, _b = units[u]
                s, n = u % SPL, kt * cols
                dve.wait_ge(hi_done, u + 1)
                if u >= SPL:
                    dve.wait_ge(tile_done, before[u - SPL + 1])
                nc.vector.tensor_tensor(wlo[s][:, 0:n], raw[u % RAW][:, 0:n], bf(whi[s], n), ALU.subtract).then_inc(lo_done, 1)

            def take(b):
                dve.wait_ge(tile_done, b + 1)
                return bank[b % 4]

            def sum_quarter(q):
                vecs = vblocks[q // 4][3]
                s, v = gfull(q)
                dve.wait_ge(s, v)
                w = vslot(q)
                for kk in range(2):
                    kt = (q % 4) * 2 + kk
                    for i, (cv, _c) in enumerate(vecs):
                        if kt == 0:
                            if i == 0:
                                dve.wait_ge(seed_full, 16 * (q // 4 + 1))
                                if q == 0:
                                    dve.wait_ge(filled, FILLS)
                                    dve.wait_ge(cvec_done, 1)
                        else:
                            dve.wait_ge(vsum, vops[q] + kk * len(vecs) + i - len(vecs) + 1)
                        nc.vector.scalar_tensor_tensor(out=acc[:, i, :], in0=w[:, kk, :], scalar=cvec[:, cv, kt:kt + 1],
                                                       in1=seed[:, :] if kt == 0 else acc[:, i, :],
                                                       op0=ALU.mult, op1=ALU.add).then_inc(vsum, 1)

            def take_mod(n):
                dve.wait_ge(red_done, n + 1)
                for i, (_cv, col) in enumerate(vblocks[n][3]):
                    last = nc.vector.tensor_copy(mod[:, col:col + 4], bank[7][:, 4 * i:4 * i + 4])
                last.then_inc(mod_done, 1)

            def transposed(t0, kts, T, hi, lo, tmp, affine):
                def low(kt):
                    dve.wait_ge(tr_hi, t0 + kt + 1)
                    nc.vector.tensor_tensor(lo[:, kt, 0:T], tmp[(t0 + kt) % 2][:, 0:T], hi[:, kt, 0:T].bitcast(f32),
                                            ALU.subtract).then_inc(tr_lo, 1)
                for kt in range(kts):
                    t = t0 + kt
                    dve.wait_ge(tr_full, t + 1)
                    if t >= 2:
                        dve.wait_ge(tr_lo, t - 1)
                    for c0, c1, sc, sh in affine(kt):
                        o, i = tmp[t % 2][:, c0:c1], bank[4 + t % 2][:, c0:c1]
                        if sc is None:
                            last = nc.vector.tensor_copy(o, i)
                        elif sh is None:
                            last = nc.vector.tensor_scalar(o, i, sc, None, ALU.mult)
                        else:
                            last = nc.vector.tensor_scalar(o, i, sc, sh, ALU.mult, ALU.add)
                    last.then_inc(tr_tmp, 1)
                    if kt:
                        low(kt - 1)
                low(kts - 1)

            dve.wait_ge(vec_t, 1)
            link(nc.vector.tensor_copy(vecT[:, :], bank[6][:, 0:NROWS]))
            nc.vector.tensor_copy(aff[:, 0, :], vecT[:, 0:KT]).then_inc(vec_c, 1)
            dve.wait_ge(vec_c, 1)
            for g in range(GROUPS):
                dve.wait_ge(line_mm, g + 1)
                nc.vector.tensor_copy(line[:, g, :], bank[4 + g][0:HEADS, 0:384]).then_inc(line_done, 1)
            dve.wait_ge(filled, FILLS)
            nc.vector.tensor_copy(stat[:, 42:43], stat[:, 40:41]).then_inc(vec_c, 2)
            dve.wait_ge(root, 1)
            link(nc.vector.reciprocal(stat[:, 4:6], stat[:, 2:4]))
            for m in range(NT):
                last = nc.vector.tensor_scalar(xrow[:, m, :], xres[:, m, :], stat[:, 4 + m:5 + m], None, ALU.mult)
            last.then_inc(x_scaled, 1)
            for u in range(LEAD):
                split_lo(u)
            for q in range(PRE_Q):
                if q and q % 4 == 0:
                    take_mod(q // 4 - 1)
                sum_quarter(q)
            take_mod(3)
            dve.wait_ge(mod_done, 4)
            link(nc.vector.scalar_tensor_tensor(out=aff[:, 0, :], in0=mod[:, 8:16], scalar=1.0, in1=aff[:, 0, :],
                                                op0=ALU.add, op1=ALU.mult))
            transposed(0, KT, S, h_hi, h_lo, trA, lambda k: [(0, S, aff[:, 0, k:k + 1], mod[:, k:k + 1])])
            q = PRE_Q
            for u in range(U_GATES):
                split_lo(u + LEAD)
                b = before[u]
                if 4 <= u < 22 and (u - 4) % 6 in (2, 3):
                    g, j = divmod(u - 4, 6)
                    nc.vector.tensor_copy(kT[:, g, 2 * j - 4:2 * j - 2, :], take(b)[:, :].rearrange("p (m n) -> p m n", m=2))\
                        .then_inc(free[b % 4], 1)
                if u and q % 4 == 0:
                    take_mod(q // 4 - 1)
                sum_quarter(q)
                q += 1
                if u == 3:
                    all_taken(dve, 4)
                    s0 = ROWS["pool_scale"]
                    for g in range(4):
                        dve.wait_ge(pool_mm, 3 + g // 2)
                        last = nc.vector.scalar_tensor_tensor(
                            out=flat(u_row)[:, g * S:(g + 1) * S], in0=bank[6 if g < 2 else 4][:, (g % 2) * S:(g % 2 + 1) * S],
                            scalar=vecT[:, s0 + g:s0 + g + 1], in1=zpT[:, g, :], op0=ALU.mult, op1=ALU.mult)
                        if g % 2:
                            last.then_inc(mz_tmp, 1)
                    dve.wait_ge(mz_part, 1)
                    nc.vector.tensor_tensor(flat(mz_lo), flat(u_row), flat(mz_hi).bitcast(f32), ALU.subtract).then_inc(mz_part, 1)
            def maximum(n):
                W = P * (steps[n][0] + 1)
                dve.wait_ge(at_s, n + 1)
                nc.vector.tensor_reduce(stat[:, 8:9], bank[4][:, 0:2 * W], AX.X, ALU.max)
                link(nc.vector.tensor_reduce(stat[:, 9:10], bank[5][:, 0:W], AX.X, ALU.max))
                nc.vector.tensor_scalar(stat[:, 10:11], stat[:, 8:9], stat[:, 9:10], -1.0, ALU.max, ALU.mult).then_inc(at_mx, 1)

            maximum(0)
            for n, (qt, h) in enumerate(steps):
                for j in range(qt + 1):
                    rc = rounds(n) + j
                    dve.wait_ge(at_t, rc + 1)
                    if rc >= 2:
                        dve.wait_ge(at_pv, rc - 1)
                    nc.vector.tensor_copy(probT[rc % 2][:, 0:3, :], bank[6][:, 0:384].rearrange("p (b q) -> p b q", b=3))\
                        .then_inc(at_pt, 1)
                dve.wait_ge(at_p, n + 1)
                link(nc.vector.tensor_tensor(stat[:, 14:15], stat[:, 12:13], stat[:, 13:14], ALU.add))
                link(nc.vector.reciprocal(stat[:, 15:16], stat[:, 14:15]))
                if n + 1 < len(steps):
                    maximum(n + 1)
                dve.wait_ge(at_pv, rounds(n + 1))
                z = za[:, qt, h * HD:(h + 1) * HD]
                nc.vector.scalar_tensor_tensor(out=z, in0=bank[7][:, 384:384 + HD], scalar=stat[:, 15:16], in1=z,
                                               op0=ALU.mult, op1=ALU.mult).then_inc(at_z, 1)
                if n % 2 == 0:
                    split_lo(U_GATES + n // 2 + LEAD)
                if q % 4 == 0:
                    take_mod(q // 4 - 1)
                sum_quarter(q)
                q += 1
            transposed(8, 4, S, at_hi, at_lo, trA, lambda k: [(0, S, None, None)])
            for u in range(32, 36):
                split_lo(u + LEAD)
                t = gaT if u < 34 else gpT
                for i in range(2):
                    b = before[u] + i
                    j = 4 * (u % 2) + 2 * i
                    part = t[:, j:j + 2, :]
                    nc.vector.tensor_tensor(part, take(b)[:, :].rearrange("p (m n) -> p m n", m=2), part, ALU.mult)\
                        .then_inc(free[b % 4], 1)
            all_taken(dve, before[36])
            nc.vector.tensor_tensor(flat(gaT), flat(gaT), flat(gpT), ALU.add).then_inc(merged, 1)
            dve.wait_ge(merged_hi, 1)
            nc.vector.tensor_tensor(flat(h_lo), flat(gaT), flat(h_hi).bitcast(f32), ALU.subtract).then_inc(merged_lo, 1)
            dve.wait_ge(rowb, 1)
            for i in range(2):
                last = nc.vector.tensor_copy(grow_a[:, 512 * i:512 * i + 512], bank[4 + i][:, :])
            last.then_inc(rowb_done, 1)
            dve.wait_ge(rowb_done, 1)
            for u in range(36, 40):
                split_lo(u + LEAD)
                b, j = before[u], u - 36
                cs = slice(j * UC, (j + 1) * UC)
                v = take(b)[:, :].rearrange("p (m n) -> p m n", m=2)
                ins = nc.vector.tensor_tensor(tmpa[:, :, cs], v, spread(grow_a[:, cs], [[0, 2], [1, UC]]), ALU.mult)
                ins.then_inc(free[b % 4], 1)
                taken(dve, b)
                nc.vector.tensor_tensor(xres[:, :, cs], xres[:, :, cs], tmpa[:, :, cs], ALU.add).then_inc(x_new, 1)
            dve.wait_ge(root, 2)
            link(nc.vector.reciprocal(stat[:, 4:6], stat[:, 2:4]))
            dve.wait_ge(load_f, 48)
            for m in range(NT):
                nc.vector.scalar_tensor_tensor(out=xres[:, m, :], in0=xres[:, m, :], scalar=stat[:, 4 + m:5 + m],
                                               in1=frow[:, :], op0=ALU.mult, op1=ALU.mult).then_inc(x_new, 1)

            def quarters(n):
                nonlocal q
                for _ in range(n):
                    if q % 4 == 0:
                        take_mod(q // 4 - 1)
                    sum_quarter(q)
                    q += 1

            nc.vector.tensor_scalar(aff[:, 1, :], mod[:, M0C + 8:M0C + 16], 1.0, None, ALU.add)
            link(nc.vector.tensor_scalar(aff[:, 2, :], mod[:, M0 + 8:M0 + 16], 1.0, None, ALU.add))
            transposed(12, KT, T, a_hi, a_lo, trB,
                       lambda k: [(0, S, aff[:, 1, k:k + 1], mod[:, M0C + k:M0C + k + 1]),
                                  (S, T, aff[:, 2, k:k + 1], mod[:, M0 + k:M0 + k + 1])])
            split_lo(U_EV + LEAD)
            for i in range(TILES):
                dve.wait_ge(z_mm, i + 1)
                dve.wait_ge(lg_done, i + 1)
                nc.vector.scalar_tensor_tensor(out=la[:, i, :], in0=bank[4 + i % 2][:, :], scalar=0.0, in1=ex[1][:, :],
                                               op0=ALU.min, op1=ALU.subtract).then_inc(la_done, 1)

            def mixer_units(u0, group):
                for u in range(u0, u0 + 6):
                    split_lo(u + LEAD)
                    b = before[u]
                    if u - u0 == 1:
                        for n in range(2):
                            if group:
                                dve.wait_ge(o_mm, RH)
                            src = take(b + n)
                            for hh in range(2):
                                for half in range(2):
                                    last = nc.vector.tensor_scalar(ki[64 * half:64 * half + 64, 2 * n + hh, :],
                                                                   src[64 * hh:64 * hh + 64, :],
                                                                   DK ** -0.5 if group else 1.0, None, ALU.mult)
                            last.then_inc(free[(b + n) % 4], 1)
                    quarters(UNIT_Q[u])

            def decays(hd):
                gla, h = hd < RH, hd % RH
                dve.wait_ge(ex_done, 2 * (hd + 1))
                for t, e in ((qd, ex[0]), (ki, ex[1])):
                    if gla:
                        last = nc.vector.tensor_tensor(t[:, h, :], t[:, h, :], e[:, :], ALU.mult)
                    else:
                        v = t[:, h, :].rearrange("p (c n) -> p c n", c=8)
                        last = nc.vector.tensor_tensor(v, v, spread(e[:, 0:CH], [[0, 8], [1, CH]]), ALU.mult)
                if gla:
                    nc.vector.tensor_copy(dec[0:64, h, :], ex[0][0:64, CH - 1:T:CH])
                    last = nc.vector.tensor_copy(dec[64:P, h, :], ex[0][64:P, 0:T:CH])
                else:
                    nc.vector.tensor_copy(dec[0:64, h, :], spread(ex[0][0:64, CH - 1:CH], [[0, 8]]))
                    last = nc.vector.tensor_copy(dec[64:P, h, :], spread(ex[0][64:P, 0:1], [[0, 8]]))
                last.then_inc(qk_done, 1)

            def head_states(hd):
                h = hd % RH
                dve.wait_ge(kv_done, 2 * (hd + 1))
                order = [3, 2, 1, 0, 7, 6, 5, 4]
                for s_ in range(6):
                    for rows, c, nx in ((slice(0, 64), s_, s_ + 1), (slice(64, P), order[s_], order[s_ + 1])):
                        if s_:
                            dve.wait_ge(vchain, chain.at(1))
                        nc.vector.scalar_tensor_tensor(out=kv[rows, nx, :], in0=kv[rows, c, :], scalar=dec[rows, h, c:c + 1],
                                                       in1=kv[rows, nx, :], op0=ALU.mult, op1=ALU.add).then_inc(vchain, 1)
                        chain.up()
                dve.wait_ge(vchain, chain.at())
                if hd:
                    dve.wait_ge(o_mm, hd)
                else:
                    nc.vector.memset(sp[0:64, 0, :], 0.0)
                    nc.vector.memset(sp[64:P, 3, :], 0.0)
                for rows, d0, s0, n in ((slice(0, 64), 1, 0, 7), (slice(64, P), 0, 1, 3), (slice(64, P), 4, 5, 3), (slice(64, P), 7, 0, 1)):
                    d = dec[rows, h, s0:s0 + n]
                    last = nc.vector.tensor_tensor(sp[rows, d0:d0 + n, :], kv[rows, s0:s0 + n, :],
                                                   spread(d, [[1, n], [0, DV]]), ALU.mult)
                last.then_inc(sp_done, 1)

            def head_scores(hd):
                dve.wait_ge(s_mm, hd + 1)
                if hd >= 2:
                    dve.wait_ge(o_mm, hd - 1)
                s_ = sc[hd % 2]
                nc.vector.tensor_tensor(s_[:, :, :], bank[0][:, :].rearrange("p (i t) -> p i t", i=4),
                                        spread(const("tri_f"), [[0, 4], [1, P]]), ALU.mult)
                link(nc.vector.tensor_tensor(sc2[:, :, :], bank[1][:, :].rearrange("p (i t) -> p i t", i=4),
                                             spread(const("strict_b"), [[0, 4], [1, P]]), ALU.mult))
                nc.vector.tensor_tensor(s_[:, :, :], s_[:, :, :], sc2[:, :, :], ALU.add).then_inc(sc_done, 1)

            def head_gate(hd):
                gla, h = hd < RH, hd % RH
                dve.wait_ge(o_mm, hd + 1)
                dve.wait_ge(ss_done, hd + 1)
                c0 = h * DV + (512 if gla else 0)
                v = gy[:, :, c0:c0 + DV]
                nc.vector.tensor_tensor(v, bank[6][:, :].rearrange("p (i t) -> p i t", i=4), v, ALU.mult).then_inc(gy_done, 1)

            for g in range(2):
                mixer_units(U_EV + 1 + 6 * g, g)
                for hd in range(4 * g, 4 * g + 4):
                    decays(hd)
                head_scores(4 * g)
                for hd in range(4 * g, 4 * g + 4):
                    head_states(hd)
                    if hd < 4 * g + 3:
                        head_scores(hd + 1)
                    head_gate(hd)
            dve.wait_ge(root, 3)
            dve.wait_ge(gy_done, 8)
            link(nc.vector.reciprocal(ssq[:, 2, :, :], ssq[:, 1, :, :]))
            g4 = gy[:, :, :].rearrange("p i (h n) -> p i h n", h=8)
            nc.vector.tensor_tensor(g4, g4, spread(ssq[:, 2, :, :], [[8, 4], [1, 8], [0, DV]]), ALU.mult).then_inc(y_scaled, 1)
            gg = vecT[:, ROWS["gla_g"]:ROWS["gla_g"] + 1]
            transposed(20, KT, T, a_hi, a_lo, trB, lambda k: [(0, T, gg if k >= 4 else None, None)])
            for u in range(U_EVO, U_M0):
                split_lo(u + LEAD)
                quarters(UNIT_Q[u])

            def gate_rows(n0, count=2):
                for i in range(count):
                    dve.wait_ge(rowb, n0 + i + 1)
                    for j in range(2):
                        last = nc.vector.tensor_copy(grow[:, i, 512 * j:512 * j + 512], bank[4 + j][:, :])
                    last.then_inc(rowb_done, 1)
                dve.wait_ge(rowb_done, n0 + count)

            def layer_norm(k, tiles, res, gate):
                for i in range(tiles):
                    link(nc.vector.tensor_tensor(Y[:, i, :], Y[:, i, :], gate(i), ALU.mult))
                    link(nc.vector.scalar_tensor_tensor(out=Y[:, i, :], in0=res(i), scalar=ALPHA, in1=Y[:, i, :],
                                                        op0=ALU.mult, op1=ALU.add))
                    for j in range(2):
                        last = nc.vector.bn_stats(bns[:, i, j, :], Y[:, i, 512 * j:512 * j + 512])
                    link(last)
                    last = nc.vector.bn_aggr(bna[:, i, 0:2], bns[:, i, :, :])
                last.then_inc(ln_var, 1)
                dve.wait_ge(ln_root, k + 1)
                link(nc.vector.reciprocal(bna[:, 0:tiles, 3], bna[:, 0:tiles, 2]))
                for i in range(tiles):
                    nc.vector.tensor_scalar(Y[:, i, :], Y[:, i, :], bna[:, i, 0:1], bna[:, i, 3:4], ALU.subtract, ALU.mult)\
                        .then_inc(ln_n, 1)

            def affine(rows, k, sh, sc):
                g0, b0 = ROWS["ln_g"] + 8 * k, ROWS["ln_b"] + 8 * k
                nc.vector.scalar_tensor_tensor(out=aff[:, rows, :], in0=mod[:, sc:sc + 8], scalar=1.0, in1=vecT[:, g0:g0 + 8],
                                               op0=ALU.add, op1=ALU.mult)
                link(nc.vector.scalar_tensor_tensor(out=aff[:, rows + 1, :], in0=mod[:, sc:sc + 8], scalar=1.0,
                                                    in1=vecT[:, b0:b0 + 8], op0=ALU.add, op1=ALU.mult))
                link(nc.vector.tensor_tensor(aff[:, rows + 1, :], aff[:, rows + 1, :], mod[:, sh:sh + 8], ALU.add))

            all_taken(dve, before[U_M0])
            gate_rows(1)
            dve.wait_ge(load_cr, 16)
            layer_norm(0, TILES, lambda i: cres[:, i, :] if i < 2 else xres[:, i - 2, :], lambda i: grow[:, i // 2, :])
            affine(0, 0, M0C + 24, M0C + 32)
            affine(2, 0, M0 + 24, M0 + 32)
            both = lambda k: [(0, S, aff[:, 0, k:k + 1], aff[:, 1, k:k + 1]), (S, T, aff[:, 2, k:k + 1], aff[:, 3, k:k + 1])]
            transposed(28, KT, T, a_hi, a_lo, trB, both)

            def mlp(u0, Tn, mh, ml, hid0, vecs, more):
                per = 8 * Tn // 256
                ht = 4 * Tn // 256
                tn = Tn // 256

                def round_(r, lead=8):
                    for j in range(8):
                        u = u0 + j + LEAD
                        if j < lead:
                            dve.wait_ge(hi_done, at_(u + 1, r, 8))
                            nc.vector.tensor_tensor(wlo[u % SPL][:, :], raw[u % RAW][:, :], bf(whi[u % SPL], KT * UC),
                                                    ALU.subtract).then_inc(lo_done, 1)
                        if vecs and j == 2:
                            take_loop_mod(22, r)
                        if vecs:
                            for i in LOOP_Q[j]:
                                qq = U_Q + i
                                s_, v_ = gfull(qq)
                                dve.wait_ge(s_, at_(v_, r, 16 * 8 // GSB))
                                if i % 4 == 0:
                                    dve.wait_ge(seed_full, at_(16 * (qq // 4 + 1), r, 32))
                                for kk in range(2):
                                    kt = (i % 4) * 2 + kk
                                    if kt:
                                        dve.wait_ge(vsum, at_(vops[U_Q] + 2 * i + kk, r, 16))
                                    nc.vector.scalar_tensor_tensor(
                                        out=acc[:, 0, :], in0=vslot(qq)[:, kk, :], scalar=cvec[:, 1, kt:kt + 1],
                                        in1=acc[:, 0, :] if kt else seed[:, :], op0=ALU.mult, op1=ALU.add).then_inc(vsum, 1)
                        if vecs and j == 4:
                            take_loop_mod(23, r)
                        for i in range(tn):
                            bt, t = before[u0 + j] + i, tn * j + i
                            if j < 4:
                                dve.wait_ge(free[bt % 4], at_(bt // 4 + 1, r, per // 4))
                                if t:
                                    dve.wait_ge(hid_lo, at_(hid0 + t, r, ht))
                                nc.vector.tensor_tensor(sq_[:, :], rel_[:, :], rel_[:, :], ALU.mult).then_inc(sq_done, 1)
                                dve.wait_ge(hid_hi, at_(hid0 + t + 1, r, ht))
                                fs = slice(512 * t, 512 * t + 512)
                                nc.vector.tensor_tensor(flat(ml)[:, fs], sq_[:, :], flat(mh)[:, fs].bitcast(f32), ALU.subtract)\
                                    .then_inc(hid_lo, 1)
                                if t == ht - 1:
                                    dve.wait_ge(hid_lo, at_(hid0 + ht, r, ht))
                            else:
                                dve.wait_ge(tile_done, at_(bt + 1, r, per))
                                yv = Y[:, 2 * i:2 * i + 2, (j - 4) * UC:(j - 3) * UC]
                                nc.vector.tensor_tensor(yv, bank[bt % 4][:, :].rearrange("p (m n) -> p m n", m=2), yv, ALU.add)\
                                    .then_inc(free[bt % 4], 1)

                with dve.Fori(0, 4 if more else 3) as r:
                    round_(r)
                if not more:
                    round_(3, 8 - LEAD)

            def take_loop_mod(n, r):
                dve.wait_ge(red_done, at_(n + 1, r, 2))
                nc.vector.tensor_copy(mod[:, bass.ds(r * 8 + (M1 + 16 + 4 * (n - 22)), 4)], bank[7][:, 0:4])\
                    .then_inc(mod_done, 1)

            take_mod(21)
            dve.wait_ge(y_zero, 1)
            mlp(U_M0, T, m_hi, m_lo, 0, True, True)
            gate_rows(3)
            layer_norm(1, TILES, lambda i: cres[:, i, :] if i < 2 else xres[:, i - 2, :], lambda i: grow[:, i // 2, :])
            affine(0, 1, M1C, M1C + 8)
            affine(2, 1, M1, M1 + 8)
            transposed(36, KT, T, a_hi, a_lo, trB, both)

            def rotate(src, m, dst):
                heads = lambda v: spread(v, [[AHD, 4], [AHD // 2, 2], [1, AHD // 4]])
                q4 = AHD // 4
                cs, sn = [spread(const(n)[:, m * 2 * q4:(m + 1) * 2 * q4], [[0, 4], [q4, 2], [1, q4]]) for n in ("cos", "sin")]
                t1, t2 = [trB[i][:, m * UC:(m + 1) * UC] for i in range(2)]
                for half in (0, 1):
                    hs = slice(half * q4, UC)
                    nc.vector.tensor_tensor(heads(t1[:, hs]), heads(src[:, hs]), cs, ALU.mult)
                    last = nc.vector.tensor_tensor(heads(t2[:, hs]), heads(src[:, hs]), sn, ALU.mult)
                link(last)
                nc.vector.tensor_tensor(dst(0), heads(t1), heads(t2[:, q4:]), ALU.subtract)
                return nc.vector.tensor_tensor(dst(1), heads(t1[:, q4:]), heads(t2), ALU.add)

            def low_transposed(n):
                dve.wait_ge(kq_hi, n + 1)
                src = bank[4 + n % 4][:, :]
                if n < KVH:
                    nc.vector.tensor_tensor(k_lo[:, n, :], src, k_hi[:, n, :].bitcast(f32), ALU.subtract).then_inc(kq_ev, 1)
                else:
                    j = n - KVH
                    for half in range(2):
                        hs, ls = slice(64 * half, 64 * half + 64), slice(64 - 64 * half, P - 64 * half)
                        heads = slice(4 * j + half, 4 * j + 4, 2)
                        last = nc.vector.scalar_tensor_tensor(
                            out=q_both[ls, heads, :], in0=src[hs, :].rearrange("p (a b) -> p a b", a=2), scalar=AHD ** -0.5,
                            in1=q_both[hs, heads, :].bitcast(f32), op0=ALU.mult, op1=ALU.subtract)
                    last.then_inc(kq_ev, 1)

            dve.wait_ge(res_mul, 12)
            for u in range(U_QKV, U_OD):
                split_lo(u + LEAD)
                b, j = before[u], u - U_QKV
                if j == 0:
                    src = take(b + 1)
                    for m in range(NT):
                        kr = krow[:, NT + m, 0, 0, :]
                        last = rotate(src[:, m * UC:(m + 1) * UC], m,
                                      lambda half: spread(kr[:, half * 16:], [[2 * AHD, 4], [AHD // 2, 2], [1, 16]]))
                    link(last)
                    for m in range(NT):
                        last = nc.vector.tensor_copy(krow[:, NT + m, :, 1, :], krow[:, NT + m, :, 0, :])
                    last.then_inc(free[(b + 1) % 4], 1)
                elif j == 1:
                    for i in range(2):
                        dve.wait_ge(vhi_done, i + 1)
                        nc.vector.tensor_tensor(v_lo[:, 2 * i:2 * i + 2, :], bank[(b + i) % 4][:, :].rearrange("p (m n) -> p m n", m=2),
                                                v_hi[:, 2 * i:2 * i + 2, :].bitcast(f32), ALU.subtract).then_inc(free[(b + i) % 4], 1)
                elif j >= 2:
                    src = take(b)
                    for m in range(NT):
                        qr = qrow[:, m, (j - 2) * UC:(j - 1) * UC]
                        last = rotate(src[:, m * UC:(m + 1) * UC], m,
                                      lambda half: spread(qr[:, half * 16:], [[AHD, 4], [AHD // 2, 2], [1, 16]]))
                    last.then_inc(free[b % 4], 1)
                    taken(dve, b)
                if j == 2:
                    for n in range(KVH):
                        low_transposed(n)
                elif j > 2:
                    low_transposed(KVH + j - 3)
            low_transposed(7)
            dve.wait_ge(load_sk, 16)
            N = len(wsteps)
            for n in range(N + 4):
                if n < N:
                    h, w = wsteps[n][1], wst[:, n % 4, :]
                    dve.wait_ge(wa_s, n + 1)
                    if n >= 4:
                        dve.wait_ge(wa_n, n - 3)
                    link(nc.vector.tensor_reduce(w[:, 0:1], bank[4 + n % 2][:, :], AX.X, ALU.max))
                    nc.vector.tensor_scalar(w[:, 1:2], w[:, 0:1], sink[:, h:h + 1], -1.0, ALU.max, ALU.mult).then_inc(wa_max, 1)
                if n >= 1 and n <= N:
                    w = wst[:, (n - 1) % 4, :]
                    dve.wait_ge(wa_exp, n)
                    link(nc.vector.tensor_tensor(w[:, 4:5], w[:, 2:3], w[:, 3:4], ALU.add))
                    nc.vector.reciprocal(w[:, 5:6], w[:, 4:5]).then_inc(wa_rc, 1)
                if n >= 3:
                    i = n - 3
                    if i and i % 4 == 0:
                        g = i // 4 - 1
                        qt, kv_ = wsteps[4 * g][0], wsteps[4 * g][1] // 4
                        dve.wait_ge(wa_oh, g + 1)
                        for half in range(2):
                            w = (slice(64 * half, 64 * half + 64), slice(2 * kv_, 2 * kv_ + 2), slice(qt * P, (qt + 1) * P))
                            last = nc.vector.tensor_tensor(
                                o_lo[w], bank[g % 2][0:AHD, :].rearrange("p (a b q) -> p a b q", a=2, b=2)[:, :, half, :],
                                o_hi[w].bitcast(f32), ALU.subtract)
                        last.then_inc(wa_o, 1)
                    if i < N:
                        dve.wait_ge(wa_hi, i + 1)
                        nc.vector.tensor_tensor(pT_lo[:, :, i % 4, :], bank[6 + i % 2][:, :].rearrange("p (b q) -> p b q", b=4),
                                                pT_hi[:, :, i % 4, :].bitcast(f32), ALU.subtract).then_inc(wa_lo, 1)
            for u in range(U_OD, U_M1):
                split_lo(u + LEAD)
            all_taken(dve, before[U_M1])
            gate_rows(5, 1)
            layer_norm(2, NT, lambda i: xres[:, i, :], lambda i: grow[:, 0, :])
            affine(0, 2, M1 + 24, M1 + 32)
            transposed(44, KT, S, a_hi, a_lo, trB, lambda k: [(0, S, aff[:, 0, k:k + 1], aff[:, 1, k:k + 1])])
            dve.wait_ge(y_zero, 2)
            mlp(U_M1, S, *half_m, 32, False, False)
            gate_rows(6, 1)
            layer_norm(3, NT, lambda i: xres[:, i, :], lambda i: grow[:, 0, :])


INS = ["x", "c", "norm_g", "w_ada", "b_ada", "w_in", "pool_w", "pool_scale", "w_attn_br", "w_pool_br", "w_out",
       "rel_bias", "final_g", "c_2", "ctx_2", "c_ctx_2", "w_mod_2", "b_mod_2", "ln_g_2", "ln_b_2", "mlp_w1_2",
       "mlp_w2_2", "ev_w_in_2", "ev_ret_theta_2", "ev_gla_gk_w_2", "ev_gla_gk_b_2", "ev_gla_norm_g_2", "ev_w_out_2",
       "od_w_qkv_2", "od_sink_2", "od_w_out_2"]


def kernel(**inputs):
    import concourse.bacc as bacc
    from concourse.bass_utils import run_bass_kernel_spmd as run

    nc = bacc.Bacc("TRN2", target_bir_lowering=False, num_devices=1)
    arrays, a = {}, {}
    for name in INS:
        v = np.ascontiguousarray(inputs[name])
        arrays[f"in_{name}"] = v
        a[name] = nc.dram_tensor(f"in_{name}", v.shape, mybir.dt.from_np(v.dtype), kind="ExternalInput").ap()
    table, at, keep = constants()
    arrays["table"] = table
    cst = nc.dram_tensor("table", table.shape, mybir.dt.float32, kind="ExternalInput").ap()
    scratch = nc.dram_tensor("distance_rows", [HEADS, GROUPS * 384], mybir.dt.float32).ap()
    out = nc.dram_tensor("out", [1, S, D], mybir.dt.float32, kind="ExternalOutput").ap()
    build(nc, a, out, cst, at, keep, scratch)
    r = run(nc, [arrays], core_ids=[0])
    return r.results[0]["out"]
```

```python
import math
from contextlib import ExitStack

import numpy as np

import concourse.bass as bass
from concourse import mybir

P = 128
D = 1024
KT = D // P
S = 256
NT = S // P
HEADS, HD, GROUPS = 8, 64, 3
DILS = (1, 4, 16)
N_BACK = 128
BUCKETS, MAX_DIST = 32, 2048
POOL_WINDOWS = (2, 4, 8, 16)
RH, DK, DV = 4, 64, 128
RANK, TAU = 16, 16.0
CH = 64
QH, KVH, AHD = 16, 4, 64
ALPHA = (2.0 * 2) ** 0.25
EPS_RMS, EPS_LN = 1e-6, 1e-5
NEG = -1e30
UC = 256
W_IN, EV_IN = 8192, 3104

RAW, SPL, LEAD, GSP, GSA, GSB = 2, 4, 3, 8, 3, 2

ROWS = {}
_n = 0
for _name, _len in (("norm_g", 8), ("pool_scale", 4), ("ln_g", 32), ("ln_b", 32), ("c", 8), ("c_2", 8),
                    ("c_ctx", 8), ("final_g", 8), ("gla_g", 1)):
    ROWS[_name] = _n
    _n += _len
NROWS = _n


def constants():
    p = np.arange(P)
    parts, at, n = [], {}, 0

    def put(name, a):
        nonlocal n
        a = np.asarray(a, np.float32).reshape(a.shape[0], -1)
        full = np.zeros((P, a.shape[1]), np.float32)
        full[:a.shape[0]] = a
        parts.append(full)
        at[name] = (n, a.shape[1])
        n += a.shape[1]

    eye = np.eye(P)
    put("ident", eye)
    put("anti", eye[::-1])
    same = (p[:, None] // CH) == (p[None, :] // CH)
    put("tri_f", same & (p[:, None] <= p[None, :]))
    put("tri_b", same & (p[:, None] >= p[None, :]))
    put("strict_b", same & (p[:, None] > p[None, :]))
    c = np.arange(CH)
    put("pos", np.where(p[:, None] < CH, c[None] + 1, CH - c[None]))
    put("edge", np.stack([np.where(p[None, :] > p[:, None], NEG, 0), np.where(p[None, :] < p[:, None], NEG, 0)], 1))
    half = AHD // 2
    inv = (10000.0 ** (-np.arange(0, half, 2, dtype=np.float32) / half)).astype(np.float32)
    pos = np.arange(S)
    ang = np.stack([(pos // 64)[:, None].astype(np.float32) * inv, (pos % 64)[:, None].astype(np.float32) * inv], 1)
    ang = ang.reshape(NT, P, 2, half // 2).transpose(1, 0, 2, 3)
    put("cos", np.cos(ang))
    put("sin", np.sin(ang))
    keep = n
    w = np.arange(384)
    dist = 255 - w
    hot = np.zeros((BUCKETS + 1, GROUPS, 384))
    for g, dil in enumerate(DILS):
        ok = (dist >= 0) & (dist % dil == 0) & (dist <= N_BACK * dil)
        exact = BUCKETS // 2
        nf = np.maximum(dist, 1).astype(np.float32)
        large = exact + (np.log(nf / exact) / math.log(MAX_DIST / exact) * (BUCKETS - exact)).astype(np.int32)
        b = np.where(dist < exact, dist, np.minimum(large, BUCKETS - 1))
        hot[b[ok], g, w[ok]] = 1
        hot[BUCKETS, g, ~ok] = NEG
    put("hot", hot)
    t = np.arange(S)
    m = np.zeros((S, len(POOL_WINDOWS), S))
    for g, win in enumerate(POOL_WINDOWS):
        lo = np.maximum(t + 1 - win, 0)
        inside = (t[:, None] <= t[None, :]) & (t[:, None] >= lo[None, :])
        m[:, g] = inside / np.minimum(t + 1, win)[None, :] - np.eye(S)
    put("pool", m.reshape(NT, P, len(POOL_WINDOWS), S).transpose(1, 2, 0, 3))
    return np.concatenate(parts, 1), at, keep


class Count:

    def __init__(self):
        self.n = 0

    def up(self, k=1):
        self.n += k
        return self.n

    def at(self, back=0):
        return self.n - back


def build(nc, a, out, cst, at, keep, scratch):
    f32, f32r = mybir.dt.float32, mybir.dt.float32r
    ALU, ACT, AX = mybir.AluOpType, mybir.ActivationFunctionType, mybir.AxisListType
    ctx = ExitStack()
    with ctx:
        sems = {}

        def sem(name):
            if name not in sems:
                sems[name] = ctx.enter_context(nc.semaphore(name))
            return sems[name]

        def sb(name, shape, dt=f32, where=ctx):
            return where.enter_context(nc.sbuf_tensor(name, shape, dt))

        def flat(t):
            return t[tuple([slice(None)] * len(t.shape))] if len(t.shape) == 2 else \
                t.rearrange({3: "p a b -> p (a b)", 4: "p a b c -> p (a b c)"}[len(t.shape)])

        def spread(v, dims):
            return bass.AP(tensor=v.tensor, offset=v.offset, ap=[list(v.ap[0])] + [list(d) for d in dims])

        C = sb("C", [P, keep])
        vecT = sb("vecT", [P, NROWS])
        cvec = sb("cvec", [P, 3, KT])
        mod = sb("mod", [P, 24 + 4 * 48])
        aff = sb("aff", [P, 8, KT])
        ones = sb("ones", [P, P])
        acc = sb("acc", [P, 2, 512])
        seed = sb("seed", [P, 512])
        stat = sb("stat", [P, 64])
        raw = [sb(f"raw{i}", [P, KT * UC]) for i in range(RAW)]
        whi = [sb(f"whi{i}", [P, KT * UC], f32r) for i in range(SPL)]
        wlo = [sb(f"wlo{i}", [P, KT * UC], f32r) for i in range(SPL)]
        bank = [ctx.enter_context(nc.psum_tensor(f"bank{i}", [P, 512], f32)) for i in range(8)]

        def const(name, rows=P):
            o, n = at[name]
            return C[0:rows, o:o + n]

        ident, anti = const("ident"), const("anti")

        xres = sb("xres", [P, NT, D])

        A = ExitStack()
        graw_a = [sb(f"graw_a{i}", [P, 2, 512], where=A) for i in range(GSA)]
        h_hi, h_lo = [sb(n, [P, KT, S], f32r, A) for n in ("h_hi", "h_lo")]
        mz_hi, mz_lo = [sb(n, [P, 4, S], f32r, A) for n in ("mz_hi", "mz_lo")]
        za = sb("za", [P, NT, 512], where=A)
        strip = [sb(f"strip{i}", [P, GROUPS, 256], where=A) for i in range(2)]
        prob = sb("prob", [P, 768], where=A)
        probT = [sb(f"probT{i}", [P, 4, P], where=A) for i in range(2)]
        trA = [flat(t) for t in probT]
        vrow = strip[0][0:NROWS, 0, 0:P]
        relb = strip[1][0:BUCKETS + 1, 0, 0:GROUPS * HEADS]
        pw = prob[:, 0:512].rearrange("p (g e) -> p g e", g=4)
        with ExitStack() as e:
            xrow = sb("xrow", [P, NT, D], where=e)
            hot = sb("hot", [BUCKETS + 1, GROUPS, 384], where=e)
            line = sb("line", [HEADS, GROUPS, 384], where=e)
        with ExitStack() as e:
            u_row = sb("u_row", [P, NT, 512], where=e)
            zpT = sb("zpT", [P, 4, S], where=e)
            poolM = sb("poolM", [P, 4, NT, S], where=e)
        gaT = sb("gaT", [P, KT, S], where=A)
        gpT = sb("gpT", [P, KT, S], where=A)
        with ExitStack() as e:
            sb("beside_line", [P, 384], where=e)
            pre = [sb(f"pre{i}", [P, 2, 512], where=e) for i in range(GSP)]
        with ExitStack() as e:
            qT = sb("qT", [P, GROUPS, 4, S], where=e)
            kT = sb("kT", [P, GROUPS, 4, S], where=e)
            vR = sb("vR", [P, GROUPS, NT, 512], where=e)
        with ExitStack() as e:
            at_hi, at_lo = [sb(n, [P, 4, S], f32r, e) for n in ("at_hi", "at_lo")]
            grow_a = sb("grow_a", [P, D], where=e)
            frow = sb("frow", [P, D], where=e)
            tmpa = sb("tmpa", [P, NT, D], where=e)
        A.close()
        T = 2 * S
        B = ExitStack()
        graw_b = [sb(f"graw_b{i}", [P, 2, 512], where=B) for i in range(GSB)]
        a_hi, a_lo = [sb(n, [P, KT, T], f32r, B) for n in ("a_hi", "a_lo")]
        trB = [sb(f"trB{i}", [P, T], where=B) for i in range(2)]
        with ExitStack() as e:
            gy = sb("gy", [P, 4, D], where=e)
            vv = sb("vv", [P, 4, 512], where=e)
            with ExitStack() as e2:
                crow = sb("crow", [P, 2, D], where=e2)
            qd = sb("qd", [P, 4, T], where=e)
            with ExitStack() as e2:
                lrT = sb("lrT", [2 * RANK + 1, T], where=e2)
                gkw = sb("gkw", [2 * RANK + 1, 2 * RH * DK], where=e2)
            ki = sb("ki", [P, 4, T], where=e)
            kir = sb("kir", [P, 4, P], where=e)
            with ExitStack() as e2:
                la = sb("la", [P, 4, 512], where=e2)
            kv = sb("kv", [P, 8, DV], where=e)
            sp = sb("sp", [P, 8, DV], where=e)
            dec = sb("dec", [P, 4, 8], where=e)
            lgam = sb("lgam", [P, 12], where=e)
            ssq = sb("ssq", [P, 3, 4, 8], where=e)
            ex = [sb(f"ex{i}", [P, T], where=e) for i in range(2)]
            sc = [sb(f"sc{i}", [P, 4, P], where=e) for i in range(2)]
            sc2 = sb("sc2", [P, 4, P], where=e)
        with ExitStack() as e:
            Y = sb("Y", [P, 4, D], where=e)
            bns = sb("bns", [P, 4, 2, 6], where=e)
            bna = sb("bna", [P, 4, 8], where=e)
            with ExitStack() as e2:
                cres = sb("cres", [P, 2, D], where=e2)
                with ExitStack() as e3:
                    lrow = sb("lrow", [P, 2, D], where=e3)
                m_hi, m_lo = [sb(n, [P, KT, T], f32r, e2) for n in ("m_hi", "m_lo")]
                rel_ = sb("relu", [P, T], where=e2)
                sq_ = sb("sq", [P, T], where=e2)
            grow = Y[:, 0:2, :]
            krow = Y[:, 0:2, :].rearrange("p i (m h c n) -> p (i m) h c n", m=2, h=KVH, c=2)
            qrow = Y[:, 2:4, :]
            prob1 = [Y[:, 2 + i // 2, (i % 2) * T:(i % 2 + 1) * T] for i in range(4)]
            v_hi, v_lo = [sb(n, [P, 4, UC], f32r, e) for n in ("v_hi", "v_lo")]
            q_both = sb("q_both", [P, QH, S], f32r, e)
            k_hi, k_lo = [sb(n, [P, KVH, T], f32r, e) for n in ("k_hi", "k_lo")]
            eye_r = sb("eye_r", [P, P], f32r, e)
            edge_r = sb("edge_r", [P, NT * P], f32r, e)
            wst = sb("wst", [P, 4, 6], where=e)
            pT_hi, pT_lo = [flat(a_lo)[:, i * 2048:(i + 1) * 2048].rearrange("p (b g q) -> p b g q", b=4, g=4) for i in range(2)]
            o_hi, o_lo = [flat(a_hi)[:, i * 2048:(i + 1) * 2048].rearrange("p (k n) -> p k n", k=KT) for i in range(2)]
            sink = stat[:, 44:60]
        R = [cres[:, i, :] for i in range(2)] + [xres[:, i, :] for i in range(2)]
        half_m = [flat(t)[:, 0:KT * S].rearrange("p (k n) -> p k n", k=KT) for t in (m_hi, m_lo)]
        B.close()

        def bf(w, n):
            return w[:, 0:n].bitcast(f32)

        def block(w, k0, kt, c0, cols):
            return w[k0:k0 + kt * P, c0:c0 + cols].rearrange("(k p) n -> p k n", p=P)

        units = []

        def add(w, c0, cols, banks, kt=KT, k0=0):
            units.append((block(w, k0, kt, c0, cols), kt, cols, banks))

        w_in = a["w_in"][0]
        ATT = GROUPS * 3 * 512
        for c0 in (ATT + 512, ATT + 768, ATT + 1024, ATT + 1280):
            add(w_in, c0, UC, 1)
        for c0 in range(0, ATT + 512, UC):
            add(w_in, c0, UC, 1)
        for c0 in range(ATT + 1536, W_IN, UC):
            add(w_in, c0, UC, 1)
        for w in ("w_attn_br", "w_pool_br"):
            for c0 in (0, 512):
                add(a[w][0], c0, 512, 2, kt=4)
        for c0 in range(0, D, UC):
            add(a["w_out"][0], c0, UC, 1)
        U_GATES, U_BR = 24, 32
        U_EV = len(units)
        ev = a["ev_w_in_2"][0]
        add(ev, EV_IN - 2 * RANK, 2 * RANK, 1)
        for c0 in (1536, 1792, 2048, 2304, 2560, 2816, 0, 256, 512, 768, 1024, 1280):
            add(ev, c0, UC, 2)
        U_EVO = len(units)
        for c0 in range(0, D, UC):
            add(a["ev_w_out_2"][0], c0, UC, 2)
        U_M0 = len(units)
        for r in range(4):
            for j in range(4):
                add(a["mlp_w1_2"][0], 1024 * r + UC * j, UC, 2)
            for j in range(4):
                add(a["mlp_w2_2"][0], UC * j, UC, 2, k0=1024 * r)
        U_QKV = len(units)
        qkv = a["od_w_qkv_2"][0]
        add(qkv, D, UC, 2)
        add(qkv, D + UC, UC, 2)
        for c0 in range(0, D, UC):
            add(qkv, c0, UC, 1)
        U_OD = len(units)
        for c0 in range(0, D, UC):
            add(a["od_w_out_2"][0], c0, UC, 1)
        U_M1 = len(units)
        for r in range(4):
            for j in range(4):
                add(a["mlp_w1_2"][1], 1024 * r + UC * j, UC, 1)
            for j in range(4):
                add(a["mlp_w2_2"][1], UC * j, UC, 1, k0=1024 * r)

        before = [0]
        for un in units:
            before.append(before[-1] + un[3])

        vblocks = [(a["w_ada"][0], a["b_ada"][0], n, [(0, 4 * n)]) for n in range(6)]
        M0, M0C, M1, M1C = 24, 72, 120, 168
        vblocks += [(a["w_mod_2"][0], a["b_mod_2"][0], n, [(1, M0 + 4 * n), (2, M0C + 4 * n)]) for n in range(12)]
        vblocks += [(a["w_mod_2"][1], a["b_mod_2"][1], n,
                     [(1, M1 + 4 * n)] + ([(2, M1C + 4 * n)] if n < 4 else [])) for n in range(12)]
        vops = [0]
        for vb in vblocks:
            for _ in range(4):
                vops.append(vops[-1] + 2 * len(vb[3]))
        Q_B = 56

        def vslot(q):
            return pre[q % GSP] if q < PRE_Q else graw_a[(q - PRE_Q) % GSA] if q < Q_B else graw_b[q % GSB]

        steps = [(qt, h) for qt in range(NT) for h in range(HEADS)]

        def rounds(n):
            return n if n < HEADS else HEADS + 2 * (n - HEADS)

        PRE_Q = 16
        FILLS = 5

        UNIT_Q = dict(zip(range(U_EV, U_M0), [0, 2, 2, 4, 4, 2, 0, 2, 4, 4, 2, 0, 2, 1, 1, 1, 1]))
        U_Q = 88
        LOOP_Q = [[0, 1], [2, 3], [], [4, 5], [6, 7], [], [], []]
        LN_TILES = [4, 4, 2, 2]
        res_mul = sem("res_mul")
        RES = [0, 9, 13, 18, 22]
        b0 = before[U_M0]
        be = before[U_EVO]
        ROW_BANKS = {2: (6, 7, (be + 2) % 4, (be + 3) % 4), 3: (6, 7, (b0 + 2) % 4, (b0 + 3) % 4), 4: (2, 3), 5: (6, 7)}
        TILES = 4

        def at_(v, r, per):
            return v if r is None else v + r * per

        def taken(eng, b):
            eng.wait_ge(free[b % 4], b // 4 + 1)

        def normalised(eng, k, i):
            eng.wait_ge(ln_odd if i % 2 else ln_even, sum(LN_TILES[:k]) // 2 + i // 2 + 1)

        def all_taken(eng, b):
            for i in range(min(4, b)):
                taken(eng, b - 1 - i)

        load_w, load_c, load_v, load_x, load_f = sem("load_w"), sem("load_c"), sem("load_v"), sem("load_x"), sem("load_f")
        raw_full = [sem(f"raw_full{i}") for i in range(RAW)]
        graw_full = [sem(f"graw_full{i}") for i in range(GSA + GSB)]
        pre_full = [sem(f"pre_full{i}") for i in range(GSP)]
        pre_seed, seed_full = sem("pre_seed"), sem("seed_full")
        hi_done, lo_done, tile_done = sem("hi_done"), sem("lo_done"), sem("tile_done")
        free = [sem(f"bank_free{i}") for i in range(4)]
        vsum, red_done, mod_done = sem("vsum"), sem("red_done"), sem("mod_done")
        filled = sem("filled")
        tr_full, tr_tmp, tr_hi, tr_lo = sem("tr_full"), sem("tr_tmp"), sem("tr_hi"), sem("tr_lo")
        vchain = sem("vector_chain")
        vec_t, vec_c, cvec_done = sem("vec_t"), sem("vec_c"), sem("cvec_done")
        line_mm, line_done, line_out, strip_full = sem("line_mm"), sem("line_done"), sem("line_out"), [sem("strip_full0"), sem("strip_full1")]
        sq_sum, root, x_scaled = sem("sq_sum"), sem("root"), sem("x_scaled")
        mz_part = sem("mz_part")
        pool_mm, pool_ev, mz_tmp = sem("pool_mm"), sem("pool_ev"), sem("mz_tmp")
        at_s, at_mx, at_p, at_t, at_pt, at_pv, at_z = [sem(n) for n in ("at_s", "at_mx", "at_p", "at_t", "at_pt", "at_pv", "at_z")]
        merged, merged_hi, merged_lo = sem("merged"), sem("merged_hi"), sem("merged_lo")
        rowb, rowb_done = sem("rowb"), sem("rowb_done")
        x_new = sem("x_new")
        load_ctx, load_gk, load_th, load_ln, load_cr = [sem(n) for n in ("load_ctx", "load_gk", "load_th", "load_ln", "load_cr")]
        z_mm, la_done, lg_done = sem("z_mm"), sem("la_done"), sem("lg_done")
        bc_mm, ex_done, qk_done, kt_mm, kir_done, kv_mm, kv_done, s_mm, sc_done, sp_done, o_mm, ss_done, gy_done = \
            [sem(n) for n in ("bc_mm", "ex_done", "qk_done", "kt_mm", "kir_done", "kv_mm", "kv_done", "s_mm",
                              "sc_done", "sp_done", "o_mm", "ss_done", "gy_done")]
        achain, y_scaled = sem("act_chain"), sem("y_scaled")
        ln_var, ln_root, ln_inv, ln_even, ln_odd = [sem(n) for n in ("ln_var", "ln_root", "ln_inv", "ln_even", "ln_odd")]
        sq_done, hid_hi, hid_lo = sem("sq_done"), sem("hid_hi"), sem("hid_lo")
        out_done = sem("out_done")
        load_sk, kq_t, kq_hi, kq_ev, vhi_done = [sem(n) for n in ("load_sk", "kq_t", "kq_hi", "kq_ev", "vhi_done")]
        wa_s, wa_max, wa_exp, wa_rc, wa_n, wa_t, wa_hi, wa_lo, wa_pv, wa_oh, wa_o = [
            sem(n) for n in ("wa_s", "wa_max", "wa_exp", "wa_rc", "wa_n", "wa_t", "wa_hi", "wa_lo", "wa_pv", "wa_oh", "wa_o")]
        wa_na, PART = sem("wa_na"), 320
        wsteps = [(qt, h) for qt in range(NT) for h in range(QH)]
        block_ = ctx.enter_context(nc.Block())

        def gfull(q):
            if q < PRE_Q:
                return pre_full[q % GSP], 16 * (q // GSP + 1)
            if q < Q_B:
                return graw_full[(q - PRE_Q) % GSA], 16 * ((q - PRE_Q) // GSA + 1)
            return graw_full[GSA + q % GSB], 16 * ((q - Q_B) // GSB + 1)

        def load_seed(eng, q):
            b, n = vblocks[q // 4][1:3]
            if q:
                eng.wait_ge(vsum, vops[q - 3])
            bias = bass.AP(tensor=b.tensor, offset=b.offset + 512 * n, ap=[[512, 1], [1, 512]])
            eng.dma_start(seed[0:1, :], bias).then_inc(pre_seed if q < PRE_Q else seed_full, 16)

        def load_quarter(eng, q):
            w, _b, n, _v = vblocks[q // 4]
            ring = GSP if q < PRE_Q else GSA if q < Q_B else GSB
            if q >= ring:
                eng.wait_ge(vsum, vops[q - ring + 1])
            eng.dma_start(vslot(q)[:, :, :], block(w, (q % 4) * 2 * P, 2, 512 * n, 512)).then_inc(gfull(q)[0], 16)

        @block_.sync
        def _(sp_):
            sp_.dma_start(C[:, :], cst[:, 0:keep]).then_inc(load_c, 16)
            for name, rows, src in (("norm_g", 8, a["norm_g"]), ("pool_scale", 4, a["pool_scale"]),
                                    ("ln_g", 32, a["ln_g_2"]), ("ln_b", 32, a["ln_b_2"]), ("c", 8, a["c"]),
                                    ("c_2", 8, a["c_2"]), ("c_ctx", 8, a["c_ctx_2"]), ("final_g", 8, a["final_g"]),
                                    ("gla_g", 1, a["ev_gla_norm_g_2"])):
                n = int(np.prod(src.shape))
                v = bass.AP(tensor=src.tensor, offset=src.offset, ap=[[P, rows], [1, P]])
                sp_.dma_start(vrow[ROWS[name]:ROWS[name] + rows, :], v).then_inc(load_v, 16)
            sp_.dma_start(xres[:, :, :], a["x"][0].rearrange("(m p) n -> p m n", p=P)).then_inc(load_x, 16)
            sp_.dma_start(hot[:, :, :], cst[0:BUCKETS + 1, at["hot"][0]:at["hot"][0] + GROUPS * 384]
                          .rearrange("p (g w) -> p g w", g=GROUPS)).then_inc(load_w, 16)
            sp_.wait_ge(filled, FILLS)
            sp_.dma_start(relb[0:BUCKETS, :], a["rel_bias"]).then_inc(load_w, 16)

            def load(u):
                src, kt, cols, _ = units[u]
                if u >= RAW:
                    sp_.wait_ge(lo_done, u - RAW + 1)
                sp_.dma_start(raw[u % RAW][:, 0:kt * cols].rearrange("p (k n) -> p k n", k=kt), src)\
                    .then_inc(raw_full[u % RAW], 16)

            sp_.wait_ge(filled, FILLS)
            for q in range(PRE_Q):
                if q % 4 == 0:
                    load_seed(sp_, q)
                load_quarter(sp_, q)
                if q in (7, 11, 13):
                    load({7: 0, 11: 1, 13: 2}[q])
            for u in range(LEAD, U_EV + LEAD):
                load(u)
            sp_.wait_ge(merged_lo, 1)
            sp_.dma_start(crow[:, :, :], a["ctx_2"][0].rearrange("(m p) n -> p m n", p=P)).then_inc(load_ctx, 16)
            sp_.wait_ge(x_new, 6)
            sp_.wait_ge(filled, FILLS + 1)
            for d in range(2):
                cs = slice(d * RH * DK, (d + 1) * RH * DK)
                sp_.dma_start(gkw[d * RANK:(d + 1) * RANK, cs], a["ev_gla_gk_w_2"][0, d]).then_inc(load_gk, 16)
                sp_.dma_start(gkw[2 * RANK:2 * RANK + 1, cs], a["ev_gla_gk_b_2"][0, d:d + 1]).then_inc(load_gk, 16)
                th = a["ev_ret_theta_2"]
                sp_.dma_start(lgam[64 * d:64 * d + 64, 0:4],
                              bass.AP(tensor=th.tensor, offset=th.offset + 4 * d, ap=[[0, 64], [1, 4]])).then_inc(load_th, 16)
            for u in range(U_EV + LEAD, U_EVO):
                load(u)
            for u in range(U_EVO, U_EVO + LEAD + 1):
                load(u)

            def ln_rows(l, s):
                for i, v in enumerate((a["ln_g_2"], a["ln_b_2"])):
                    sp_.dma_start(lrow[:, i, :], bass.AP(tensor=v.tensor, offset=v.offset + (2 * l + s) * D,
                                                         ap=[[0, P], [1, D]])).then_inc(load_ln, 16)

            sp_.wait_ge(tr_full, 28)
            sp_.dma_start(cres[:, :, :], a["ctx_2"][0].rearrange("(m p) n -> p m n", p=P)).then_inc(load_cr, 16)
            ln_rows(0, 0)
            for u in range(U_EVO + LEAD + 1, U_M0):
                load(u)

            def mlp_loads(l, u0):
                with sp_.Fori(0, 4) as r:
                    for j in range(8):
                        u = u0 + j
                        w = a["mlp_w1_2"][l][:, bass.ds(r * 1024 + UC * j, UC)] if j < 4 else \
                            a["mlp_w2_2"][l][bass.ds(r * 1024, 1024), UC * (j - 4):UC * (j - 3)]
                        sp_.wait_ge(lo_done, at_(u - RAW + 1, r, 8))
                        sp_.dma_start(raw[u % RAW][:, :].rearrange("p (k n) -> p k n", k=KT),
                                      w.rearrange("(k p) n -> p k n", p=P)).then_inc(raw_full[u % RAW], 16)

            mlp_loads(0, U_M0)
            for u in range(U_QKV, U_QKV + LEAD + 1):
                load(u)
            sp_.wait_ge(tile_done, before[U_QKV])
            ln_rows(0, 1)
            sk = a["od_sink_2"]
            sp_.dma_start(sink, bass.AP(tensor=sk.tensor, offset=sk.offset, ap=[[0, P], [1, QH]])).then_inc(load_sk, 16)
            for u in range(U_QKV + LEAD + 1, U_M1):
                load(u)
            sp_.wait_ge(wa_pv, len(wsteps) // 4)
            ln_rows(1, 0)
            mlp_loads(1, U_M1)
            sp_.wait_ge(tile_done, before[U_M1 + 32])
            ln_rows(1, 1)
            for m in range(NT):
                sp_.wait_ge(res_mul, RES[3] + 2 * (m + 1))
                sp_.dma_start(out[0, m * P:(m + 1) * P, :], xres[:, m, :]).then_inc(out_done, 16)
            sp_.wait_ge(out_done, 16 * NT)
            sp_.wait_ge(line_out, 16)

        @block_.gpsimd
        def _(pool):
            pool.memset(seed[:, :], 0.0).then_inc(filled, 1)
            pool.memset(ones[:, :], 1.0).then_inc(filled, 1)
            pool.memset(relb, 1.0).then_inc(filled, 1)
            pool.memset(stat[:, 40:41], EPS_RMS).then_inc(filled, 1)
            pool.memset(stat[:, 41:42], EPS_LN).then_inc(filled, 1)
            pool.wait_ge(filled, FILLS)

            def load_q(q):
                if q % 4 == 0:
                    load_seed(pool, q)
                load_quarter(pool, q)

            for u in range(2):
                pool.wait_ge(hi_done, u + 1)
                pool.tensor_tensor(wlo[u][:, :], raw[u][:, :], bf(whi[u], KT * UC), ALU.subtract).then_inc(lo_done, 1)
            pool.wait_ge(line_done, 3)
            pool.dma_start(scratch.rearrange("h (g w) -> h g w", g=GROUPS), line[:, :, :]).then_inc(line_out, 16)
            pool.wait_ge(tr_full, KT)
            pool.wait_ge(line_mm, 3)
            pool.wait_ge(line_out, 16)
            pool.dma_start(poolM[:, :, :, :], cst[:, at["pool"][0]:at["pool"][0] + at["pool"][1]]
                           .rearrange("p (g s t) -> p g s t", g=4, s=NT)).then_inc(load_f, 16)
            pool.dma_start(pw, a["pool_w"][0].rearrange("g c e -> c g e")).then_inc(load_f, 16)
            for u in range(U_GATES):
                load_q(PRE_Q + u)
            for n, (qt, h) in enumerate(steps):
                if n >= 2:
                    pool.wait_ge(at_s, n - 1)
                pool.dma_start(strip[n % 2][:, :, :],
                               bass.AP(tensor=scratch.tensor, offset=scratch.offset + h * GROUPS * 384,
                                       ap=[[1, P], [384, GROUPS], [1, 256]])).then_inc(strip_full[n % 2], 16)
                load_q(PRE_Q + U_GATES + n)
            pool.wait_ge(at_s, len(steps))
            pool.wait_ge(at_pv, rounds(len(steps)))
            fg = a["final_g"]
            Qn = PRE_Q + U_GATES + len(steps)
            pool.dma_start(frow[:, :], bass.AP(tensor=fg.tensor, offset=fg.offset, ap=[[0, P], [1, D]])).then_inc(load_f, 16)

            pool.wait_ge(x_new, 6)
            pool.memset(gkw[:, :], 0.0).then_inc(filled, 1)
            pool.memset(lrT[:, :], 1.0).then_inc(filled, 1)
            q = Qn
            while q < U_Q:
                load_q(q)
                q += 1

            done = Count()

            def residual(k, tiles):
                pool.wait_ge(load_ln, 32 * (k + 1))
                if k % 2 == 0:
                    pool.tensor_scalar(lrow[:, :, :], lrow[:, :, :], ALPHA, None, ALU.mult).then_inc(res_mul, 1)
                    pool.wait_ge(res_mul, done.up())
                for i in tiles:
                    normalised(pool, k, i)
                    dst = R[i if LN_TILES[k] == 4 else i + 2]
                    pool.tensor_tensor(dst, Y[:, i, :], lrow[:, 0, :], ALU.mult).then_inc(res_mul, 1)
                    pool.wait_ge(res_mul, done.up())
                    pool.tensor_tensor(dst, dst, lrow[:, 1, :], ALU.add).then_inc(res_mul, 1)
                    done.up()

            residual(0, range(4))
            with pool.Fori(0, 4) as r:
                for j in range(8):
                    c = r * 1024 + 512 * (4 + j // 4)
                    if j % 4 == 0:
                        pool.wait_ge(vsum, at_(vops[U_Q] + 2 * (j - 3), r, 16))
                        pool.dma_start(seed[0:1, :], a["b_mod_2"][1:2, bass.ds(c, 512)]).then_inc(seed_full, 16)
                    pool.wait_ge(vsum, at_(vops[U_Q] + 2 * (j - 1), r, 16))
                    w = a["w_mod_2"][1][(j % 4) * 256:(j % 4) * 256 + 256, bass.ds(c, 512)]
                    pool.dma_start(vslot(U_Q + j)[:, :, :], w.rearrange("(k p) n -> p k n", p=P)).then_inc(gfull(U_Q + j)[0], 16)
            residual(1, (2, 3))
            for n in range(len(wsteps)):
                pool.wait_ge(wa_rc, n + 1)
                v = prob1[n % 4][:, 0:PART]
                pool.tensor_scalar(v, v, wst[:, n % 4, 5:6], None, ALU.mult).then_inc(wa_n, 1)
            residual(2, range(2))
            residual(3, range(2))
            assert done.n == RES[4]

        @block_.tensor
        def _(pe):
            def col_unit(u, hi, lo, T, b, part=(0, 9)):
                _, kt, cols, banks = units[u]
                wh, wl = [w[u % SPL][:, 0:kt * cols].rearrange("p (k n) -> p k n", k=kt) for w in (whi, wlo)]
                pe.wait_ge(lo_done, u + 1)
                per = 512 // T
                for n in range(part[0], min(part[1], cols // P)):
                    bt = b + n // per
                    if n % per == 0 and bt >= 4:
                        pe.wait_ge(free[bt % 4], bt // 4)
                    o = bank[bt % 4][:, (n % per) * T:(n % per + 1) * T]
                    for k in range(kt):
                        for i, (w, x) in enumerate(((wh, hi), (wl, hi), (wh, lo))):
                            mm = nc.tensor.matmul(o, w[:, k, n * P:(n + 1) * P], x[:, k, 0:T],
                                                  start=(k == 0 and i == 0), stop=(k == kt - 1 and i == 2))
                    if n % per == per - 1:
                        mm.then_inc(tile_done, 1)

            def row_unit(u, hi, lo, tiles, b):
                _, kt, cols, banks = units[u]
                wh, wl = [w[u % SPL][:, 0:kt * cols].rearrange("p (k n) -> p k n", k=kt) for w in (whi, wlo)]
                pe.wait_ge(lo_done, u + 1)
                for i, m in enumerate(tiles):
                    bt = b + i // 2
                    if i % 2 == 0 and bt >= 4:
                        pe.wait_ge(free[bt % 4], bt // 4)
                    o = bank[bt % 4][:, (i % 2) * UC:(i % 2 + 1) * UC]
                    for k in range(kt):
                        for j, (w, x) in enumerate(((wh, hi), (wh, lo), (wl, hi))):
                            mm = nc.tensor.matmul(o, x[:, k, m * P:(m + 1) * P], w[:, k, :],
                                                  start=(k == 0 and j == 0), stop=(k == kt - 1 and j == 2))
                    if i % 2 == 1:
                        mm.then_inc(tile_done, 1)

            def reduce_block(n):
                vecs = vblocks[n][3]
                pe.wait_ge(vsum, vops[4 * n + 4])
                if n:
                    pe.wait_ge(mod_done, n)
                for v in range(len(vecs)):
                    for s in range(4):
                        mm = nc.tensor.matmul(bank[7][:, 4 * v + s:4 * v + s + 1], acc[:, v, s * P:(s + 1) * P],
                                              ones[:, 0:1], start=True, stop=True)
                mm.then_inc(red_done, 1)

            def broadcast_row(col, b0):
                for k in range(KT):
                    mm = nc.tensor.matmul(bank[b0 + k // 4][:, (k % 4) * P:(k % 4 + 1) * P],
                                          spread(col(k), [[0, P]]), ident, start=True, stop=True)
                mm.then_inc(rowb, 1)

            def transposed_unit(t0, T, src, u, hi, lo, tiles, b, on_columns=False):
                _, kt, cols, _b = units[u]
                wh, wl = [w[u % SPL][:, 0:kt * cols].rearrange("p (k n) -> p k n", k=kt) for w in (whi, wlo)]
                outs = []
                if on_columns:
                    width, per = T, 512 // T
                    for n in range(max(1, cols // P)):
                        outs.append((n, slice(n * P, min((n + 1) * P, cols)), slice(0, T)))
                else:
                    width, per = UC, 2
                    for n, m in enumerate(tiles):
                        outs.append((n, slice(0, UC), slice(m * P, (m + 1) * P)))

                def turn(k):
                    t = t0 + k
                    if t >= 2:
                        pe.wait_ge(tr_tmp, t - 1)
                    for i in range(T // P):
                        mm = nc.tensor.transpose(bank[4 + t % 2][:, i * P:(i + 1) * P], src(i, k), ident)
                    mm.then_inc(tr_full, 1)

                turn(0)
                turn(1)
                pe.wait_ge(lo_done, u + 1)
                for bt in sorted({b + n // per for n, _w, _x in outs}):
                    if bt >= 4:
                        pe.wait_ge(free[bt % 4], bt // 4)
                for k in range(kt):
                    pe.wait_ge(tr_lo, t0 + k + 1)
                    for n, ws, xs in outs:
                        bt = b + n // per
                        o = bank[bt % 4][0:min(P, cols), (n % per) * width:(n % per + 1) * width]
                        for j, (w, x) in enumerate(((wh, hi), (wl, hi), (wh, lo))):
                            w, x = w[:, k, ws], x[:, k, xs]
                            mm = nc.tensor.matmul(o, *((w, x) if on_columns else (x, w)), skip_group_check=True,
                                                  start=(k == 0 and j == 0 and n % per == 0), stop=(k == kt - 1 and j == 2))
                        if k == kt - 1 and (n % per == per - 1 or n == len(outs) - 1):
                            mm.then_inc(tile_done, 1)
                    if k + 2 < kt:
                        turn(k + 2)

            def gate_rows(cols, banks):
                for i, c in enumerate(cols):
                    for k in range(KT):
                        mm = nc.tensor.matmul(bank[banks[2 * i + k // 4]][:, (k % 4) * P:(k % 4 + 1) * P],
                                              spread(mod[:, c + k:c + k + 1], [[0, P]]), ident, start=True, stop=True)
                mm.then_inc(rowb, 1)

            pend = []
            qn = [0]

            def event(quarters):
                for n in pend:
                    reduce_block(n)
                pend.clear()
                if quarters and (qn[0] + quarters) // 4 > qn[0] // 4:
                    pend.append((qn[0] + quarters) // 4 - 1)
                qn[0] += quarters

            pe.wait_ge(load_c, 16)
            pe.wait_ge(load_v, 16 * 9)
            nc.tensor.transpose(bank[6][:, 0:NROWS], vrow, ident[0:NROWS, 0:NROWS]).then_inc(vec_t, 1)
            pe.wait_ge(load_w, 32)
            for g in range(GROUPS):
                if g == 2:
                    pe.wait_ge(vec_c, 1)
                nc.tensor.matmul(bank[4 + g][0:HEADS, 0:384], relb[:, g * HEADS:(g + 1) * HEADS], hot[:, g, :],
                                 start=True, stop=True).then_inc(line_mm, 1)
            pe.wait_ge(filled, FILLS)
            for n in range(4):
                reduce_block(n)
            pe.wait_ge(line_done, 3)
            pe.wait_ge(x_scaled, 1)
            transposed_unit(0, S, lambda i, k: xrow[:, i, k * P:(k + 1) * P], 0, h_hi, h_lo, range(NT), 0)
            vdone = 4
            for u in range(U_GATES):
                if u == 0:
                    pass
                elif u == 1 or (u >= 4 and (u - 4) % 6 in (4, 5) and u < 22) or u >= 22:
                    row_unit(u, h_hi, h_lo, range(NT), before[u])
                else:
                    col_unit(u, h_hi, h_lo, S, before[u])
                if u >= 4 and u % 4 == 0:
                    reduce_block(vdone)
                    vdone += 1
                if u == 3:
                    pe.wait_ge(load_f, 32)
                    all_taken(pe, 2)
                    for g in range(4):
                        for s in range(NT):
                            mm = nc.tensor.matmul(bank[4 + g // 2][:, (g % 2) * S:(g % 2 + 1) * S],
                                                  u_row[:, s, g * P:(g + 1) * P], poolM[:, g, s, :],
                                                  start=(s == 0), stop=(s == NT - 1))
                        if g % 2:
                            mm.then_inc(pool_mm, 1)
                    for g in range(4):
                        pe.wait_ge(pool_ev, g // 2 + 1)
                        mm = nc.tensor.matmul(bank[6 if g < 2 else 4][:, (g % 2) * S:(g % 2 + 1) * S], pw[:, g, :],
                                              trA[g // 2][:, (g % 2) * S:(g % 2 + 1) * S], start=True, stop=True)
                        if g % 2:
                            mm.then_inc(pool_mm, 1)

            pe.wait_ge(mz_tmp, 2)
            all_taken(pe, before[U_GATES])
            def logits(n, groups):
                qt, h = steps[n]
                W = P * (qt + 1)
                lane = slice(64 * (h % 2), 64 * (h % 2) + 64)
                if n:
                    pe.wait_ge(at_p, n)
                pe.wait_ge(strip_full[n % 2], 16 * (n // 2 + 1))
                for g in groups:
                    o = bank[4][:, g * W:(g + 1) * W] if g < 2 else bank[5][:, 0:W]
                    nc.tensor.matmul(o, qT[lane, g, h // 2, qt * P:(qt + 1) * P], kT[lane, g, h // 2, 0:W],
                                     start=True, stop=False)
                    mm = nc.tensor.matmul(o, anti, strip[n % 2][:, g, 256 - W:256], start=False, stop=True)
                if 2 in groups:
                    mm.then_inc(at_s, 1)

            def prob_transposes(n, j):
                rc = rounds(n) + j
                if rc:
                    pe.wait_ge(at_pt, rc)
                for b in range(3):
                    blk = 3 * j + b
                    mm = nc.tensor.transpose(bank[6][:, b * P:(b + 1) * P], prob[:, blk * P:(blk + 1) * P], ident)
                mm.then_inc(at_t, 1)

            def values(n, j):
                qt, h = steps[n]
                rc = rounds(n) + j
                pe.wait_ge(at_pt, rc + 1)
                pe.wait_ge(mod_done, vdone)
                for b in range(3):
                    blk = 3 * j + b
                    g, kb = divmod(blk, qt + 1)
                    mm = nc.tensor.matmul(bank[7][:, 384:384 + HD], probT[rc % 2][:, b, :], vR[:, g, kb, h * HD:(h + 1) * HD],
                                          start=(blk == 0), stop=(blk == 3 * (qt + 1) - 1), skip_group_check=True)
                mm.then_inc(at_pv, 1)

            logits(0, (0, 1, 2))
            for n, (qt, h) in enumerate(steps):
                more = n + 1 < len(steps)
                pe.wait_ge(at_p, n + 1)
                if n:
                    pe.wait_ge(at_z, n)
                prob_transposes(n, 0)
                if more:
                    logits(n + 1, (0, 1) if qt else (0, 1, 2))
                values(n, 0)
                if qt:
                    prob_transposes(n, 1)
                    if more:
                        logits(n + 1, (2,))
                    values(n, 1)
                u = U_GATES + n // 2
                col_unit(u, h_hi, h_lo, S, before[u], (n % 2, n % 2 + 1))
                if n % 4 == 0:
                    pe.wait_ge(at_z, n + 1)
                    reduce_block(vdone)
                    vdone += 1
            pe.wait_ge(at_z, len(steps))
            transposed_unit(8, S, lambda i, k: za[:, i, k * P:(k + 1) * P], U_BR, at_hi, at_lo, None, before[U_BR], True)
            col_unit(U_BR + 1, at_hi, at_lo, S, before[U_BR + 1])
            pe.wait_ge(mz_part, 2)
            for u in (34, 35):
                col_unit(u, mz_hi, mz_lo, S, before[u])
            reduce_block(vdone)
            broadcast_row(lambda k: mod[:, 16 + k:17 + k], 4)
            pe.wait_ge(merged_lo, 1)
            for u in range(36, 40):
                row_unit(u, h_hi, h_lo, range(NT), before[u])

            qn[0] = PRE_Q + U_GATES + len(steps)
            pe.wait_ge(x_new, 6)
            pe.wait_ge(load_ctx, 16)
            transposed_unit(12, T, lambda i, k: crow[:, i, k * P:(k + 1) * P] if i < 2 else xres[:, i - 2, k * P:(k + 1) * P],
                            U_EV, a_hi, a_lo, None, before[U_EV], True)
            taken(pe, before[U_EV])
            pe.wait_ge(load_gk, 64)
            for i in range(TILES):
                if i >= 2:
                    pe.wait_ge(la_done, i - 1)
                nc.tensor.matmul(bank[4 + i % 2][:, :], lrT[:, i * P:(i + 1) * P], gkw[:, :], start=True, stop=True)\
                    .then_inc(z_mm, 1)
            event(UNIT_Q[U_EV])

            def decay_sums(h):
                if h:
                    pe.wait_ge(ex_done, 2 * h)
                for i in range(TILES):
                    for d, tri in ((0, "tri_f"), (1, "tri_b")):
                        mm = nc.tensor.matmul(bank[6][64 * d:64 * d + 64, i * P:(i + 1) * P],
                                              la[:, i, 256 * d + DK * h:256 * d + DK * h + DK], const(tri),
                                              start=True, stop=True)
                mm.then_inc(bc_mm, 1)

            def head_sums(hd):
                h = hd % RH
                pe.wait_ge(qk_done, hd + 1)
                if hd:
                    pe.wait_ge(kir_done, hd)
                for i in range(TILES):
                    mm = nc.tensor.transpose(bank[2][:, i * P:(i + 1) * P], ki[:, h, i * P:(i + 1) * P], ident)
                mm.then_inc(kt_mm, 1)
                if hd:
                    pe.wait_ge(sc_done, hd)
                for d in range(2):
                    rows = slice(64 * d, 64 * d + 64)
                    for i in range(TILES):
                        mm = nc.tensor.matmul(bank[d][:, i * P:(i + 1) * P], ki[rows, h, i * P:(i + 1) * P],
                                              qd[rows, h, i * P:(i + 1) * P], start=True, stop=True)
                mm.then_inc(s_mm, 1)
                if hd:
                    pe.wait_ge(kv_done, 2 * hd)
                pe.wait_ge(kir_done, hd + 1)
                for c in range(8):
                    rows = slice(64 * (c % 2), 64 * (c % 2) + 64)
                    mm = nc.tensor.matmul(bank[4 + c % 2][:, (c // 2) * DV:(c // 2 + 1) * DV], kir[rows, c // 2, :],
                                          vv[rows, c // 2, h * DV:(h + 1) * DV], start=True, stop=True)
                mm.then_inc(kv_mm, 1)

            def head_out(hd):
                h = hd % RH
                pe.wait_ge(sc_done, hd + 1)
                pe.wait_ge(sp_done, hd + 1)
                if hd:
                    pe.wait_ge(gy_done, hd)
                for i in range(TILES):
                    nc.tensor.matmul(bank[6][:, i * P:(i + 1) * P], sc[hd % 2][:, i, :], vv[:, i, h * DV:(h + 1) * DV],
                                     start=True, stop=False, skip_group_check=True)
                    for half in range(2):
                        c = 2 * i + half
                        mm = nc.tensor.matmul(bank[6][64 * half:64 * half + 64, i * P:(i + 1) * P], qd[:, h, c * CH:(c + 1) * CH],
                                              sp[:, c, :], start=False, stop=True, skip_group_check=True)
                mm.then_inc(o_mm, 1)

            def heads(first):
                head_sums(first)
                for hd in range(first, first + RH):
                    if hd + 1 < first + RH:
                        head_sums(hd + 1)
                    head_out(hd)

            def mixer_units(u0):
                for u in range(u0, u0 + 6):
                    if u - u0 < 2:
                        col_unit(u, a_hi, a_lo, T, before[u])
                    else:
                        row_unit(u, a_hi, a_lo, range(TILES), before[u])
                    event(UNIT_Q[u])

            mixer_units(U_EV + 1)
            all_taken(pe, before[U_EV + 7])
            for h in range(RH):
                decay_sums(h)
            heads(0)
            mixer_units(U_EV + 7)
            all_taken(pe, before[U_EV + 13])
            heads(RH)
            pe.wait_ge(gy_done, 2 * RH)
            pe.wait_ge(mod_done, qn[0] // 4 - 1)
            gate_rows((M0C + 16, M0 + 16), ROW_BANKS[2])
            pe.wait_ge(y_scaled, 2)
            transposed_unit(20, T, lambda i, k: gy[:, i, k * P:(k + 1) * P], U_EVO, a_hi, a_lo, range(TILES), before[U_EVO])
            for u in range(U_EVO, U_M0):
                if u > U_EVO:
                    row_unit(u, a_hi, a_lo, range(TILES), before[u])
                else:
                    pe.wait_ge(rowb_done, 2)
                event(UNIT_Q[u])
            assert qn[0] == U_Q and pend == [21], (qn, pend)
            event(0)

            all_taken(pe, before[U_M0])
            pe.wait_ge(mod_done, 22)
            gate_rows((M0C + 40, M0 + 40), ROW_BANKS[3])
            for i in range(TILES):
                normalised(pe, 0, i)

            def mlp(u0, hi, lo, Tn, mh, ml, hid0, vecs, t0, rows):
                per, tiles = 8 * Tn // 256, Tn // P
                ht = 4 * Tn // 256

                def round_(r):
                    later = r is not None

                    def at_(v, r, per):
                        return v + (r + 1) * per if later else v

                    for j in range(8):
                        u, b = u0 + j, before[u0 + j]
                        if not later and j == 0:
                            transposed_unit(t0, Tn, lambda i, k: Y[:, i, k * P:(k + 1) * P], u0, hi, lo, None, b, True)
                            pe.wait_ge(rowb_done, rows)
                            continue
                        wh, wl = [w[u % SPL][:, :].rearrange("p (k n) -> p k n", k=KT) for w in (whi, wlo)]
                        pe.wait_ge(lo_done, at_(u + 1, r, 8))
                        n_out = 2 if j < 4 else tiles
                        per_bank = 512 // Tn if j < 4 else 2
                        for n in range(n_out):
                            bt = b + n // per_bank
                            if n % per_bank == 0:
                                pe.wait_ge(free[bt % 4], at_(bt // 4, r, per // 4))
                            w = 512 // per_bank
                            o = bank[bt % 4][:, (n % per_bank) * w:(n % per_bank + 1) * w]
                            for k in range(KT):
                                if j == 4 and n == 0:
                                    pe.wait_ge(hid_lo, at_(hid0 + k * ht // KT + 1, r, ht))
                                if j < 4:
                                    trio = [(wh[:, k, n * P:(n + 1) * P], hi[:, k, 0:Tn]), (wl[:, k, n * P:(n + 1) * P], hi[:, k, 0:Tn]),
                                            (wh[:, k, n * P:(n + 1) * P], lo[:, k, 0:Tn])]
                                else:
                                    trio = [(mh[:, k, n * P:(n + 1) * P], wh[:, k, :]), (mh[:, k, n * P:(n + 1) * P], wl[:, k, :]),
                                            (ml[:, k, n * P:(n + 1) * P], wh[:, k, :])]
                                for i, (x, y) in enumerate(trio):
                                    mm = nc.tensor.matmul(o, x, y, start=(k == 0 and i == 0), stop=(k == KT - 1 and i == 2))
                            if n % per_bank == per_bank - 1:
                                mm.then_inc(tile_done, 1)
                        if vecs and j in (2, 5):
                            n = 22 + j // 3
                            pe.wait_ge(vsum, at_(vops[U_Q] + 8 * (j // 3 + 1), r, 16))
                            pe.wait_ge(mod_done, at_(n, r, 2))
                            for s_ in range(4):
                                mm = nc.tensor.matmul(bank[7][:, s_:s_ + 1], acc[:, 0, s_ * P:(s_ + 1) * P], ones[:, 0:1],
                                                      start=True, stop=True)
                            mm.then_inc(red_done, 1)

                round_(None)
                with pe.Fori(0, 3) as r:
                    round_(r)

            mlp(U_M0, a_hi, a_lo, T, m_hi, m_lo, 0, True, 28, 3)
            for i in range(TILES):
                normalised(pe, 1, i)

            def transpose_q(j):
                taken(pe, before[U_QKV + 2 + j])
                if j:
                    pe.wait_ge(kq_ev, KVH)
                for p_ in range(2):
                    for m in range(NT):
                        mm = nc.tensor.transpose(bank[4 + j][:, (NT * p_ + m) * P:(NT * p_ + m + 1) * P],
                                                 qrow[:, m, (2 * j + p_) * P:(2 * j + p_ + 1) * P], ident)
                mm.then_inc(kq_t, 1)

            for u in range(U_QKV, U_OD):
                j = u - U_QKV - 2
                if j == -2:
                    transposed_unit(36, T, lambda i, k: Y[:, i, k * P:(k + 1) * P], u, a_hi, a_lo, range(TILES), before[u])
                else:
                    row_unit(u, a_hi, a_lo, range(TILES) if j < 0 else range(NT, TILES), before[u])
                if j == 0:
                    all_taken(pe, before[U_QKV + 1])
                    pe.wait_ge(mod_done, len(vblocks))
                    for n in range(KVH):
                        for m in range(TILES):
                            mm = nc.tensor.transpose(bank[4 + n][:, m * P:(m + 1) * P],
                                                     krow[:, m, n, :, :].rearrange("p a b -> p (a b)"), ident)
                        mm.then_inc(kq_t, 1)
                    pe.wait_ge(kq_ev, KVH)
                if j >= 1:
                    transpose_q(j - 1)
            transpose_q(3)
            all_taken(pe, before[U_OD])
            gate_rows((M1 + 16,), ROW_BANKS[4])
            N = len(wsteps)
            for n in range(N + 4):
                if n < N:
                    qt, h = wsteps[n]
                    pe.wait_ge(kq_ev, KVH + max(h // 4, n % 2) + 1)
                    if n >= 2:
                        pe.wait_ge(wa_exp, n - 1)
                    o = bank[4 + n % 2]
                    cut = S + P * (1 - qt)
                    nc.tensor.matmul(o[:, :], q_both[:, h, qt * P:(qt + 1) * P], k_hi[:, h // 4, :],
                                     start=True, stop=False, skip_group_check=True)
                    nc.tensor.matmul(o[:, :], q_both[:, h, qt * P:(qt + 1) * P], k_lo[:, h // 4, :],
                                     start=False, stop=False, skip_group_check=True)
                    nc.tensor.matmul(o[:, cut:cut + P], eye_r[:, :], edge_r[:, qt * P:(qt + 1) * P],
                                     start=False, stop=True, skip_group_check=True).then_inc(wa_s, 1)
                if n >= 7 and n % 4 == 3:
                    g = (n - 7) // 4
                    kv_ = wsteps[4 * g][1] // 4
                    pe.wait_ge(wa_lo, 4 * g + 4)
                    if g >= 2:
                        pe.wait_ge(wa_o, g - 1)
                    for b in range(4):
                        vs = slice(kv_ * AHD, (kv_ + 1) * AHD)
                        for j, (x, y) in enumerate(((v_hi, pT_hi), (v_lo, pT_hi), (v_hi, pT_lo))):
                            mm = nc.tensor.matmul(bank[g % 2][0:AHD, :], x[:, b, vs], y[:, b, :, :].rearrange("p g q -> p (g q)"),
                                                  start=(b == 0 and j == 0), stop=(b == 3 and j == 2))
                    mm.then_inc(wa_pv, 1)
                if 2 <= n < N + 2:
                    i = n - 2
                    pe.wait_ge(wa_n, i + 1)
                    pe.wait_ge(wa_na, i + 1)
                    pe.wait_ge(kq_ev, 8)
                    if i >= 2:
                        pe.wait_ge(wa_lo, i - 1)
                    for b in range(4):
                        mm = nc.tensor.transpose(bank[6 + i % 2][:, b * P:(b + 1) * P], prob1[i % 4][:, b * P:(b + 1) * P], ident)
                    mm.then_inc(wa_t, 1)
            pe.wait_ge(wa_o, N // 4)
            for u in range(U_OD, U_M1):
                row_unit(u, o_hi, o_lo, range(NT), before[u])
            all_taken(pe, before[U_M1])
            gate_rows((M1 + 40,), ROW_BANKS[5])
            for i in range(NT):
                normalised(pe, 2, i)
            mlp(U_M1, a_hi, a_lo, S, *half_m, 32, False, 44, 5)

        @block_.scalar
        def _(act):
            def split_hi(u):
                if u >= len(units):
                    return
                _, kt, cols, _b = units[u]
                act.wait_ge(raw_full[u % RAW], 16 * (u // RAW + 1))
                if u >= SPL:
                    act.wait_ge(tile_done, before[u - SPL + 1])
                nc.scalar.activation(whi[u % SPL][:, 0:kt * cols], raw[u % RAW][:, 0:kt * cols], ACT.Copy).then_inc(hi_done, 1)

            def transposed_hi(t0, kts, T, hi, tmp):
                for kt in range(kts):
                    t = t0 + kt
                    act.wait_ge(tr_tmp, t + 1)
                    nc.scalar.activation(hi[:, kt, 0:T], tmp[t % 2][:, 0:T], ACT.Copy).then_inc(tr_hi, 1)

            def take(b):
                act.wait_ge(tile_done, b + 1)
                return bank[b % 4]

            act.wait_ge(load_x, 16)
            for m in range(NT):
                nc.scalar.activation(flat(za), xres[:, m, :], ACT.Square, accum_out=stat[:, m:m + 1]).then_inc(sq_sum, 1)
                act.wait_ge(sq_sum, m + 1)
            act.wait_ge(vec_c, 3)
            nc.scalar.activation(stat[:, 2:4], stat[:, 0:2], ACT.Sqrt, bias=stat[:, 40:41], scale=1.0 / D).then_inc(root, 1)
            c0 = ROWS["c"]
            nc.scalar.activation(cvec[:, 0, :], vecT[:, c0:c0 + 8], ACT.Copy)
            nc.scalar.activation(cvec[:, 1:3, :], vecT[:, c0 + 8:c0 + 24].rearrange("p (a b) -> p a b", a=2), ACT.Silu)\
                .then_inc(cvec_done, 1)
            for u in range(2):
                split_hi(u)
            transposed_hi(0, KT, S, h_hi, trA)
            split_hi(2)
            for u in range(U_GATES):
                split_hi(u + LEAD)
                b = before[u]
                src = take(b)[:, :].rearrange("p (m n) -> p m n", m=2)
                if u < 2:
                    dst, f, kw = u_row[:, :, u * UC:(u + 1) * UC], ACT.Copy, {}
                elif u < 4:
                    dst, f, kw = zpT[:, 2 * (u - 2):2 * (u - 1), :], ACT.Silu, {}
                elif u < 22:
                    g, j = divmod(u - 4, 6)
                    if j < 2:
                        dst, f, kw = qT[:, g, 2 * j:2 * j + 2, :], ACT.Copy, {"scale": HD ** -0.5}
                    elif j < 4:
                        continue
                    else:
                        dst, f, kw = vR[:, g, :, (j - 4) * UC:(j - 3) * UC], ACT.Copy, {}
                else:
                    dst, f, kw = za[:, :, (u - 22) * UC:(u - 21) * UC], ACT.Silu, {}
                nc.scalar.activation(dst, src, f, **kw).then_inc(free[b % 4], 1)
                if u == 3:
                    for g in range(2):
                        act.wait_ge(pool_mm, g + 1)
                        nc.scalar.activation(trA[g], bank[4 + g][:, :], ACT.Copy).then_inc(pool_ev, 1)
                    act.wait_ge(mz_tmp, 2)
                    nc.scalar.activation(flat(mz_hi), flat(u_row), ACT.Copy).then_inc(mz_part, 1)
            def gate_unit(i):
                b = before[U_GATES + i]
                dst = gaT if i < 4 else gpT
                nc.scalar.activation(dst[:, 2 * (i % 4):2 * (i % 4) + 2, :],
                                     take(b)[:, :].rearrange("p (m n) -> p m n", m=2), ACT.Sigmoid).then_inc(free[b % 4], 1)

            for n, (qt, h) in enumerate(steps):
                W = P * (qt + 1)
                act.wait_ge(at_mx, n + 1)
                if n:
                    act.wait_ge(at_t, rounds(n))
                nc.scalar.activation(prob[:, 0:2 * W], bank[4][:, 0:2 * W], ACT.Exp, bias=stat[:, 10:11],
                                     accum_out=stat[:, 12:13])
                nc.scalar.activation(prob[:, 2 * W:3 * W], bank[5][:, 0:W], ACT.Exp, bias=stat[:, 10:11],
                                     accum_out=stat[:, 13:14]).then_inc(at_p, 1)
                if n % 2 == 0 and n:
                    gate_unit(n // 2 - 1)
                if n % 2 == 0:
                    split_hi(U_GATES + n // 2 + LEAD)
            gate_unit(7)
            transposed_hi(8, 4, S, at_hi, trA)
            for u in range(32, 36):
                split_hi(u + LEAD)
            act.wait_ge(merged, 1)
            nc.scalar.activation(flat(h_hi), flat(gaT), ACT.Copy).then_inc(merged_hi, 1)
            for u in range(36, 40):
                split_hi(u + LEAD)
            act.wait_ge(x_new, 4)
            for m in range(NT):
                i = nc.scalar.activation(tmpa[:, m, :], xres[:, m, :], ACT.Square, accum_out=stat[:, m:m + 1])
            i.then_inc(sq_sum, 1)
            act.wait_ge(sq_sum, 3)
            nc.scalar.activation(stat[:, 2:4], stat[:, 0:2], ACT.Sqrt, bias=stat[:, 40:41], scale=1.0 / D).then_inc(root, 1)

            link = Count()

            def step(ins):
                ins.then_inc(achain, 1)
                act.wait_ge(achain, link.up())

            transposed_hi(12, KT, T, a_hi, trB)
            split_hi(U_EV + LEAD)
            b = before[U_EV]
            act.wait_ge(filled, FILLS + 2)
            nc.scalar.activation(lrT[0:2 * RANK, :], take(b)[0:2 * RANK, :], ACT.Copy).then_inc(free[b % 4], 1)
            for i in range(TILES):
                act.wait_ge(z_mm, i + 1)
                if i:
                    act.wait_ge(la_done, i)
                step(nc.scalar.activation(ex[0][:, :], bank[4 + i % 2][:, :], ACT.Abs))
                step(nc.scalar.activation(ex[0][:, :], ex[0][:, :], ACT.Exp, scale=-1.0))
                nc.scalar.activation(ex[1][:, :], ex[0][:, :], ACT.Ln, bias=1.0).then_inc(lg_done, 1)
            act.wait_ge(load_th, 32)
            step(nc.scalar.activation(lgam[:, 4:8], lgam[:, 0:4], ACT.Exp))
            step(nc.scalar.activation(lgam[:, 4:8], lgam[:, 4:8], ACT.Ln, bias=1.0, scale=-1.0))
            step(nc.scalar.activation(lgam[:, 8:12], lgam[:, 4:8], ACT.Copy, scale=-1.0))

            def take_rows(n):
                act.wait_ge(rowb, n)
                for i, b in enumerate(ROW_BANKS[n]):
                    last = nc.scalar.activation(grow[:, i // 2, 512 * (i % 2):512 * (i % 2) + 512], bank[b][:, :], ACT.Copy)
                last.then_inc(rowb_done, 1)

            def mixer_units(u0, group):
                for u in range(u0, u0 + 6):
                    split_hi(u + LEAD)
                    b, j = before[u], u - u0
                    if j == 0:
                        for n in range(2):
                            if group:
                                act.wait_ge(o_mm, RH)
                            src = take(b + n)
                            for hh in range(2):
                                for half in range(2):
                                    last = nc.scalar.activation(qd[64 * half:64 * half + 64, 2 * n + hh, :],
                                                                src[64 * hh:64 * hh + 64, :], ACT.Copy,
                                                                scale=1.0 if group else DK ** -0.5)
                            last.then_inc(free[(b + n) % 4], 1)
                    elif j >= 2:
                        for i in range(2):
                            src = take(b + i)[:, :].rearrange("p (m n) -> p m n", m=2)
                            c0 = (j % 2) * UC
                            if j < 4:
                                nc.scalar.activation(vv[:, 2 * i:2 * i + 2, c0:c0 + UC], src, ACT.Copy).then_inc(free[(b + i) % 4], 1)
                            else:
                                c0 += 0 if group else 512
                                nc.scalar.activation(gy[:, 2 * i:2 * i + 2, c0:c0 + UC], src, ACT.Silu).then_inc(free[(b + i) % 4], 1)

            def decays(hd):
                gla, h = hd < RH, hd % RH
                if hd:
                    if hd >= RH:
                        act.wait_ge(ss_done, RH)
                    act.wait_ge(qk_done, hd)
                if gla:
                    act.wait_ge(bc_mm, hd + 1)
                    nc.scalar.activation(ex[0][:, :], bank[6][:, :], ACT.Exp, scale=1.0 / TAU).then_inc(ex_done, 1)
                    nc.scalar.activation(ex[1][:, :], bank[6][:, :], ACT.Exp, scale=-1.0 / TAU).then_inc(ex_done, 1)
                else:
                    nc.scalar.activation(ex[0][:, 0:CH], const("pos"), ACT.Exp, scale=lgam[:, 4 + h:5 + h]).then_inc(ex_done, 1)
                    nc.scalar.activation(ex[1][:, 0:CH], const("pos"), ACT.Exp, scale=lgam[:, 8 + h:9 + h]).then_inc(ex_done, 1)

            def head_sums(hd):
                act.wait_ge(kt_mm, hd + 1)
                if hd:
                    act.wait_ge(kv_mm, hd)
                nc.scalar.activation(flat(kir), bank[2][:, :], ACT.Copy).then_inc(kir_done, 1)
                act.wait_ge(kv_mm, hd + 1)
                if hd:
                    act.wait_ge(sp_done, hd)
                for i in range(2):
                    nc.scalar.activation(kv[:, i:8:2, :], bank[4 + i][:, :].rearrange("p (c n) -> p c n", c=4),
                                         ACT.Copy).then_inc(kv_done, 1)

            def head_out(hd):
                gla, h = hd < RH, hd % RH
                if hd:
                    act.wait_ge(ss_done, hd)
                act.wait_ge(o_mm, hd + 1)
                col = h + (RH if gla else 0)
                for i in range(TILES):
                    last = nc.scalar.activation(ex[1][:, i * P:(i + 1) * P], bank[6][:, i * P:(i + 1) * P], ACT.Square,
                                                accum_out=ssq[:, 0, i, col:col + 1])
                last.then_inc(ss_done, 1)

            for g in range(2):
                mixer_units(U_EV + 1 + 6 * g, g)
                for hd in range(4 * g, 4 * g + 4):
                    decays(hd)
                for hd in range(4 * g, 4 * g + 5):
                    if hd < 4 * g + 4:
                        head_sums(hd)
                    if hd > 4 * g:
                        head_out(hd - 1)
                cs = slice(4 - 4 * g, 8 - 4 * g)
                act.wait_ge(ss_done, 4 * g + 4)
                nc.scalar.activation(ssq[:, 1, :, cs], ssq[:, 0, :, cs], ACT.Sqrt, bias=stat[:, 40:41], scale=1.0 / DV)\
                    .then_inc(root, 1)
            transposed_hi(20, KT, T, a_hi, trB)
            for u in range(U_EVO, U_M0):
                split_hi(u + LEAD)
                if u == U_EVO:
                    take_rows(2)

            def ln_part(k):
                tiles = LN_TILES[k]
                act.wait_ge(ln_var, k + 1)
                nc.scalar.activation(bna[:, 0:tiles, 2], bna[:, 0:tiles, 1], ACT.Sqrt, bias=stat[:, 41:42]).then_inc(ln_root, 1)
                act.wait_ge(ln_inv, k + 1)
                for i in range(1, tiles, 2):
                    nc.scalar.activation(Y[:, i, :], R[i + 4 - tiles], ACT.Identity, bias=bna[:, i, 4:5],
                                         scale=bna[:, i, 3:4]).then_inc(ln_odd, 1)

            ln_part(0)
            transposed_hi(28, KT, T, a_hi, trB)
            act.wait_ge(res_mul, 4)
            take_rows(3)

            def mlp(u0, Tn, mh, hid0, more):
                per = 8 * Tn // 256
                ht = 4 * Tn // 256

                def round_(r, lead=8):
                    for j in range(8):
                        u = u0 + j + LEAD
                        tn = Tn // 256
                        if j < lead:
                            act.wait_ge(raw_full[u % RAW], at_(16 * (u // RAW + 1), r, 16 * 8 // RAW))
                            act.wait_ge(tile_done, at_(before[u0] + tn * (j + LEAD - SPL + 1), r, per))
                            nc.scalar.activation(whi[u % SPL][:, :], raw[u % RAW][:, :], ACT.Copy).then_inc(hi_done, 1)
                        if j >= 4:
                            continue
                        if j == 0:
                            act.wait_ge(tile_done, at_(before[u0], r, per))
                        for i in range(tn):
                            bt, t = before[u0 + j] + i, tn * j + i
                            act.wait_ge(tile_done, at_(bt + 1, r, per))
                            nc.scalar.activation(rel_[:, :], bank[bt % 4][:, :], ACT.Relu).then_inc(free[bt % 4], 1)
                            act.wait_ge(sq_done, at_(hid0 + t + 1, r, ht))
                            nc.scalar.activation(flat(mh)[:, 512 * t:512 * t + 512], sq_[:, :], ACT.Copy).then_inc(hid_hi, 1)

                with act.Fori(0, 4 if more else 3) as r:
                    round_(r)
                if not more:
                    round_(3, 8 - LEAD)

            mlp(U_M0, T, m_hi, 0, True)
            ln_part(1)
            transposed_hi(36, KT, T, a_hi, trB)

            def take_transposed(n):
                act.wait_ge(kq_t, n + 1)
                src = bank[4 + n % 4][:, :]
                if n < KVH:
                    nc.scalar.activation(k_hi[:, n, :], src, ACT.Copy).then_inc(kq_hi, 1)
                else:
                    j = n - KVH
                    for half in range(2):
                        hs = slice(64 * half, 64 * half + 64)
                        last = nc.scalar.activation(q_both[hs, 4 * j + half:4 * j + 4:2, :],
                                                    src[hs, :].rearrange("p (a b) -> p a b", a=2), ACT.Copy, scale=AHD ** -0.5)
                    last.then_inc(kq_hi, 1)

            act.wait_ge(res_mul, RES[2])
            nc.scalar.activation(eye_r[:, :], ident, ACT.Copy)
            nc.scalar.activation(edge_r[:, :], const("edge"), ACT.Copy)
            for u in range(U_QKV, U_OD):
                split_hi(u + LEAD)
                b, j = before[u], u - U_QKV
                if j == 0:
                    src = take(b)[:, :].rearrange("p (m h n) -> p m h n", m=2, h=KVH)
                    for m in range(2):
                        for i in range(2):
                            last = nc.scalar.activation(krow[:, m, :, i, :], src[:, m, :, :], ACT.Copy)
                    last.then_inc(free[b % 4], 1)
                elif j == 1:
                    for i in range(2):
                        nc.scalar.activation(v_hi[:, 2 * i:2 * i + 2, :], take(b + i)[:, :].rearrange("p (m n) -> p m n", m=2),
                                             ACT.Copy).then_inc(vhi_done, 1)
                elif j == 2:
                    for n in range(KVH):
                        take_transposed(n)
                else:
                    take_transposed(KVH + j - 3)
            take_transposed(7)
            act.wait_ge(load_sk, 16)
            take_rows(4)
            N = len(wsteps)
            def wa_transposed(i):
                if i and i % 4 == 0:
                    g = i // 4 - 1
                    qt, kv_ = wsteps[4 * g][0], wsteps[4 * g][1] // 4
                    act.wait_ge(wa_pv, g + 1)
                    for half in range(2):
                        last = nc.scalar.activation(o_hi[64 * half:64 * half + 64, 2 * kv_:2 * kv_ + 2, qt * P:(qt + 1) * P],
                                                    bank[g % 2][0:AHD, :].rearrange("p (a b q) -> p a b q", a=2, b=2)[:, :, half, :],
                                                    ACT.Copy)
                    last.then_inc(wa_oh, 1)
                if i == N:
                    return
                act.wait_ge(wa_t, i + 1)
                nc.scalar.activation(pT_hi[:, :, i % 4, :], bank[6 + i % 2][:, :].rearrange("p (b q) -> p b q", b=4),
                                     ACT.Copy).then_inc(wa_hi, 1)

            def wa_probs(n):
                h = wsteps[n][1]
                act.wait_ge(wa_max, n + 1)
                if n >= 4:
                    act.wait_ge(wa_t, n - 3)
                nc.scalar.activation(prob1[n % 4], bank[4 + n % 2][:, :], ACT.Exp, bias=wst[:, n % 4, 1:2],
                                     accum_out=wst[:, n % 4, 2:3])
                nc.scalar.activation(wst[:, n % 4, 3:4], sink[:, h:h + 1], ACT.Exp, bias=wst[:, n % 4, 1:2]).then_inc(wa_exp, 1)

            for n in range(N + 4):
                if n >= 3:
                    wa_transposed(n - 3)
                if n < N:
                    wa_probs(n)
                if 1 <= n <= N:
                    act.wait_ge(wa_rc, n)
                    v = prob1[(n - 1) % 4][:, PART:]
                    nc.scalar.activation(v, v, ACT.Copy, scale=wst[:, (n - 1) % 4, 5:6]).then_inc(wa_na, 1)
            for u in range(U_OD, U_M1):
                split_hi(u + LEAD)
            ln_part(2)
            transposed_hi(44, KT, S, a_hi, trB)
            act.wait_ge(res_mul, RES[2] + 2)
            take_rows(5)
            mlp(U_M1, S, half_m[0], 32, False)
            ln_part(3)

        @block_.vector
        def _(dve):
            chain = Count()

            def link(ins):
                ins.then_inc(vchain, 1)
                chain.up()
                dve.wait_ge(vchain, chain.at())

            def split_lo(u):
                if u >= len(units):
                    return
                _, kt, cols, _b = units[u]
                s, n = u % SPL, kt * cols
                dve.wait_ge(hi_done, u + 1)
                if u >= SPL:
                    dve.wait_ge(tile_done, before[u - SPL + 1])
                nc.vector.tensor_tensor(wlo[s][:, 0:n], raw[u % RAW][:, 0:n], bf(whi[s], n), ALU.subtract).then_inc(lo_done, 1)

            def take(b):
                dve.wait_ge(tile_done, b + 1)
                return bank[b % 4]

            def sum_quarter(q):
                vecs = vblocks[q // 4][3]
                s, v = gfull(q)
                dve.wait_ge(s, v)
                w = vslot(q)
                for kk in range(2):
                    kt = (q % 4) * 2 + kk
                    for i, (cv, _c) in enumerate(vecs):
                        if kt == 0:
                            if i == 0:
                                if q < PRE_Q:
                                    dve.wait_ge(pre_seed, 16 * (q // 4 + 1))
                                else:
                                    dve.wait_ge(seed_full, 16 * ((q - PRE_Q) // 4 + 1))
                                if q == 0:
                                    dve.wait_ge(filled, FILLS)
                                    dve.wait_ge(cvec_done, 1)
                        else:
                            dve.wait_ge(vsum, vops[q] + kk * len(vecs) + i - len(vecs) + 1)
                        nc.vector.scalar_tensor_tensor(out=acc[:, i, :], in0=w[:, kk, :], scalar=cvec[:, cv, kt:kt + 1],
                                                       in1=seed[:, :] if kt == 0 else acc[:, i, :],
                                                       op0=ALU.mult, op1=ALU.add).then_inc(vsum, 1)

            def take_mod(n):
                dve.wait_ge(red_done, n + 1)
                for i, (_cv, col) in enumerate(vblocks[n][3]):
                    last = nc.vector.tensor_copy(mod[:, col:col + 4], bank[7][:, 4 * i:4 * i + 4])
                last.then_inc(mod_done, 1)

            def transposed(t0, kts, T, hi, lo, tmp, affine):
                def low(kt):
                    dve.wait_ge(tr_hi, t0 + kt + 1)
                    nc.vector.tensor_tensor(lo[:, kt, 0:T], tmp[(t0 + kt) % 2][:, 0:T], hi[:, kt, 0:T].bitcast(f32),
                                            ALU.subtract).then_inc(tr_lo, 1)
                for kt in range(kts):
                    t = t0 + kt
                    dve.wait_ge(tr_full, t + 1)
                    if t >= 2:
                        dve.wait_ge(tr_lo, t - 1)
                    for c0, c1, sc, sh in affine(kt):
                        o, i = tmp[t % 2][:, c0:c1], bank[4 + t % 2][:, c0:c1]
                        if sc is None:
                            last = nc.vector.tensor_copy(o, i)
                        elif sh is None:
                            last = nc.vector.tensor_scalar(o, i, sc, None, ALU.mult)
                        else:
                            last = nc.vector.tensor_scalar(o, i, sc, sh, ALU.mult, ALU.add)
                    last.then_inc(tr_tmp, 1)
                    if kt:
                        low(kt - 1)
                low(kts - 1)

            dve.wait_ge(vec_t, 1)
            link(nc.vector.tensor_copy(vecT[:, :], bank[6][:, 0:NROWS]))
            nc.vector.tensor_copy(aff[:, 0, :], vecT[:, 0:KT]).then_inc(vec_c, 1)
            dve.wait_ge(vec_c, 1)
            for g in range(GROUPS):
                dve.wait_ge(line_mm, g + 1)
                nc.vector.tensor_copy(line[:, g, :], bank[4 + g][0:HEADS, 0:384]).then_inc(line_done, 1)
            dve.wait_ge(filled, FILLS)
            nc.vector.tensor_copy(stat[:, 42:43], stat[:, 40:41]).then_inc(vec_c, 2)
            dve.wait_ge(root, 1)
            link(nc.vector.reciprocal(stat[:, 4:6], stat[:, 2:4]))
            for m in range(NT):
                last = nc.vector.tensor_scalar(xrow[:, m, :], xres[:, m, :], stat[:, 4 + m:5 + m], None, ALU.mult)
            last.then_inc(x_scaled, 1)
            for q in range(PRE_Q):
                if q and q % 4 == 0:
                    take_mod(q // 4 - 1)
                sum_quarter(q)
            take_mod(3)
            dve.wait_ge(mod_done, 4)
            link(nc.vector.scalar_tensor_tensor(out=aff[:, 0, :], in0=mod[:, 8:16], scalar=1.0, in1=aff[:, 0, :],
                                                op0=ALU.add, op1=ALU.mult))
            transposed(0, KT, S, h_hi, h_lo, trA, lambda k: [(0, S, aff[:, 0, k:k + 1], mod[:, k:k + 1])])
            dve.wait_ge(lo_done, 2)
            split_lo(2)
            q = PRE_Q
            for u in range(U_GATES):
                split_lo(u + LEAD)
                b = before[u]
                if 4 <= u < 22 and (u - 4) % 6 in (2, 3):
                    g, j = divmod(u - 4, 6)
                    nc.vector.tensor_copy(kT[:, g, 2 * j - 4:2 * j - 2, :], take(b)[:, :].rearrange("p (m n) -> p m n", m=2))\
                        .then_inc(free[b % 4], 1)
                if u and q % 4 == 0:
                    take_mod(q // 4 - 1)
                sum_quarter(q)
                q += 1
                if u == 3:
                    all_taken(dve, 4)
                    s0 = ROWS["pool_scale"]
                    for g in range(4):
                        dve.wait_ge(pool_mm, 3 + g // 2)
                        last = nc.vector.scalar_tensor_tensor(
                            out=flat(u_row)[:, g * S:(g + 1) * S], in0=bank[6 if g < 2 else 4][:, (g % 2) * S:(g % 2 + 1) * S],
                            scalar=vecT[:, s0 + g:s0 + g + 1], in1=zpT[:, g, :], op0=ALU.mult, op1=ALU.mult)
                        if g % 2:
                            last.then_inc(mz_tmp, 1)
                    dve.wait_ge(mz_part, 1)
                    nc.vector.tensor_tensor(flat(mz_lo), flat(u_row), flat(mz_hi).bitcast(f32), ALU.subtract).then_inc(mz_part, 1)
            def maximum(n):
                W = P * (steps[n][0] + 1)
                dve.wait_ge(at_s, n + 1)
                nc.vector.tensor_reduce(stat[:, 8:9], bank[4][:, 0:2 * W], AX.X, ALU.max)
                link(nc.vector.tensor_reduce(stat[:, 9:10], bank[5][:, 0:W], AX.X, ALU.max))
                nc.vector.tensor_scalar(stat[:, 10:11], stat[:, 8:9], stat[:, 9:10], -1.0, ALU.max, ALU.mult).then_inc(at_mx, 1)

            maximum(0)
            for n, (qt, h) in enumerate(steps):
                for j in range(qt + 1):
                    rc = rounds(n) + j
                    dve.wait_ge(at_t, rc + 1)
                    if rc >= 2:
                        dve.wait_ge(at_pv, rc - 1)
                    nc.vector.tensor_copy(probT[rc % 2][:, 0:3, :], bank[6][:, 0:384].rearrange("p (b q) -> p b q", b=3))\
                        .then_inc(at_pt, 1)
                dve.wait_ge(at_p, n + 1)
                link(nc.vector.tensor_tensor(stat[:, 14:15], stat[:, 12:13], stat[:, 13:14], ALU.add))
                link(nc.vector.reciprocal(stat[:, 15:16], stat[:, 14:15]))
                if n + 1 < len(steps):
                    maximum(n + 1)
                dve.wait_ge(at_pv, rounds(n + 1))
                z = za[:, qt, h * HD:(h + 1) * HD]
                nc.vector.scalar_tensor_tensor(out=z, in0=bank[7][:, 384:384 + HD], scalar=stat[:, 15:16], in1=z,
                                               op0=ALU.mult, op1=ALU.mult).then_inc(at_z, 1)
                if n % 2 == 0:
                    split_lo(U_GATES + n // 2 + LEAD)
                if q % 4 == 0:
                    take_mod(q // 4 - 1)
                sum_quarter(q)
                q += 1
            transposed(8, 4, S, at_hi, at_lo, trA, lambda k: [(0, S, None, None)])
            for u in range(32, 36):
                split_lo(u + LEAD)
                t = gaT if u < 34 else gpT
                for i in range(2):
                    b = before[u] + i
                    j = 4 * (u % 2) + 2 * i
                    part = t[:, j:j + 2, :]
                    nc.vector.tensor_tensor(part, take(b)[:, :].rearrange("p (m n) -> p m n", m=2), part, ALU.mult)\
                        .then_inc(free[b % 4], 1)
            all_taken(dve, before[36])
            nc.vector.tensor_tensor(flat(gaT), flat(gaT), flat(gpT), ALU.add).then_inc(merged, 1)
            dve.wait_ge(merged_hi, 1)
            nc.vector.tensor_tensor(flat(h_lo), flat(gaT), flat(h_hi).bitcast(f32), ALU.subtract).then_inc(merged_lo, 1)
            dve.wait_ge(rowb, 1)
            for i in range(2):
                last = nc.vector.tensor_copy(grow_a[:, 512 * i:512 * i + 512], bank[4 + i][:, :])
            last.then_inc(rowb_done, 1)
            dve.wait_ge(rowb_done, 1)
            for u in range(36, 40):
                split_lo(u + LEAD)
                b, j = before[u], u - 36
                cs = slice(j * UC, (j + 1) * UC)
                v = take(b)[:, :].rearrange("p (m n) -> p m n", m=2)
                ins = nc.vector.tensor_tensor(tmpa[:, :, cs], v, spread(grow_a[:, cs], [[0, 2], [1, UC]]), ALU.mult)
                ins.then_inc(free[b % 4], 1)
                taken(dve, b)
                nc.vector.tensor_tensor(xres[:, :, cs], xres[:, :, cs], tmpa[:, :, cs], ALU.add).then_inc(x_new, 1)
            dve.wait_ge(root, 2)
            link(nc.vector.reciprocal(stat[:, 4:6], stat[:, 2:4]))
            dve.wait_ge(load_f, 48)
            for m in range(NT):
                nc.vector.scalar_tensor_tensor(out=xres[:, m, :], in0=xres[:, m, :], scalar=stat[:, 4 + m:5 + m],
                                               in1=frow[:, :], op0=ALU.mult, op1=ALU.mult).then_inc(x_new, 1)

            def quarters(n):
                nonlocal q
                for _ in range(n):
                    if q % 4 == 0:
                        take_mod(q // 4 - 1)
                    sum_quarter(q)
                    q += 1

            nc.vector.tensor_scalar(aff[:, 1, :], mod[:, M0C + 8:M0C + 16], 1.0, None, ALU.add)
            link(nc.vector.tensor_scalar(aff[:, 2, :], mod[:, M0 + 8:M0 + 16], 1.0, None, ALU.add))
            transposed(12, KT, T, a_hi, a_lo, trB,
                       lambda k: [(0, S, aff[:, 1, k:k + 1], mod[:, M0C + k:M0C + k + 1]),
                                  (S, T, aff[:, 2, k:k + 1], mod[:, M0 + k:M0 + k + 1])])
            split_lo(U_EV + LEAD)
            for i in range(TILES):
                dve.wait_ge(z_mm, i + 1)
                dve.wait_ge(lg_done, i + 1)
                nc.vector.scalar_tensor_tensor(out=la[:, i, :], in0=bank[4 + i % 2][:, :], scalar=0.0, in1=ex[1][:, :],
                                               op0=ALU.min, op1=ALU.subtract).then_inc(la_done, 1)
            quarters(UNIT_Q[U_EV])

            def mixer_units(u0, group):
                for u in range(u0, u0 + 6):
                    split_lo(u + LEAD)
                    b = before[u]
                    if u - u0 == 1:
                        for n in range(2):
                            if group:
                                dve.wait_ge(o_mm, RH)
                            src = take(b + n)
                            for hh in range(2):
                                for half in range(2):
                                    last = nc.vector.tensor_scalar(ki[64 * half:64 * half + 64, 2 * n + hh, :],
                                                                   src[64 * hh:64 * hh + 64, :],
                                                                   DK ** -0.5 if group else 1.0, None, ALU.mult)
                            last.then_inc(free[(b + n) % 4], 1)
                    quarters(UNIT_Q[u])

            def decays(hd):
                gla, h = hd < RH, hd % RH
                dve.wait_ge(ex_done, 2 * (hd + 1))
                for t, e in ((qd, ex[0]), (ki, ex[1])):
                    if gla:
                        last = nc.vector.tensor_tensor(t[:, h, :], t[:, h, :], e[:, :], ALU.mult)
                    else:
                        v = t[:, h, :].rearrange("p (c n) -> p c n", c=8)
                        last = nc.vector.tensor_tensor(v, v, spread(e[:, 0:CH], [[0, 8], [1, CH]]), ALU.mult)
                if gla:
                    nc.vector.tensor_copy(dec[0:64, h, :], ex[0][0:64, CH - 1:T:CH])
                    last = nc.vector.tensor_copy(dec[64:P, h, :], ex[0][64:P, 0:T:CH])
                else:
                    nc.vector.tensor_copy(dec[0:64, h, :], spread(ex[0][0:64, CH - 1:CH], [[0, 8]]))
                    last = nc.vector.tensor_copy(dec[64:P, h, :], spread(ex[0][64:P, 0:1], [[0, 8]]))
                last.then_inc(qk_done, 1)

            def head_states(hd):
                h = hd % RH
                dve.wait_ge(kv_done, 2 * (hd + 1))
                order = [3, 2, 1, 0, 7, 6, 5, 4]
                for s_ in range(6):
                    for rows, c, nx in ((slice(0, 64), s_, s_ + 1), (slice(64, P), order[s_], order[s_ + 1])):
                        if s_:
                            dve.wait_ge(vchain, chain.at(1))
                        nc.vector.scalar_tensor_tensor(out=kv[rows, nx, :], in0=kv[rows, c, :], scalar=dec[rows, h, c:c + 1],
                                                       in1=kv[rows, nx, :], op0=ALU.mult, op1=ALU.add).then_inc(vchain, 1)
                        chain.up()
                dve.wait_ge(vchain, chain.at())
                if hd:
                    dve.wait_ge(o_mm, hd)
                else:
                    nc.vector.memset(sp[0:64, 0, :], 0.0)
                    nc.vector.memset(sp[64:P, 3, :], 0.0)
                for rows, d0, s0, n in ((slice(0, 64), 1, 0, 7), (slice(64, P), 0, 1, 3), (slice(64, P), 4, 5, 3), (slice(64, P), 7, 0, 1)):
                    d = dec[rows, h, s0:s0 + n]
                    last = nc.vector.tensor_tensor(sp[rows, d0:d0 + n, :], kv[rows, s0:s0 + n, :],
                                                   spread(d, [[1, n], [0, DV]]), ALU.mult)
                last.then_inc(sp_done, 1)

            def head_scores(hd):
                dve.wait_ge(s_mm, hd + 1)
                if hd >= 2:
                    dve.wait_ge(o_mm, hd - 1)
                s_ = sc[hd % 2]
                nc.vector.tensor_tensor(s_[:, :, :], bank[0][:, :].rearrange("p (i t) -> p i t", i=4),
                                        spread(const("tri_f"), [[0, 4], [1, P]]), ALU.mult)
                link(nc.vector.tensor_tensor(sc2[:, :, :], bank[1][:, :].rearrange("p (i t) -> p i t", i=4),
                                             spread(const("strict_b"), [[0, 4], [1, P]]), ALU.mult))
                nc.vector.tensor_tensor(s_[:, :, :], s_[:, :, :], sc2[:, :, :], ALU.add).then_inc(sc_done, 1)

            def head_gate(hd):
                gla, h = hd < RH, hd % RH
                dve.wait_ge(o_mm, hd + 1)
                dve.wait_ge(ss_done, hd + 1)
                c0 = h * DV + (512 if gla else 0)
                v = gy[:, :, c0:c0 + DV]
                nc.vector.tensor_tensor(v, bank[6][:, :].rearrange("p (i t) -> p i t", i=4), v, ALU.mult).then_inc(gy_done, 1)

            for g in range(2):
                mixer_units(U_EV + 1 + 6 * g, g)
                for hd in range(4 * g, 4 * g + 4):
                    decays(hd)
                head_scores(4 * g)
                for hd in range(4 * g, 4 * g + 4):
                    head_states(hd)
                    if hd < 4 * g + 3:
                        head_scores(hd + 1)
                    head_gate(hd)
                cs = slice(4 - 4 * g, 8 - 4 * g)
                dve.wait_ge(root, 3 + g)
                dve.wait_ge(gy_done, 4 * g + 4)
                link(nc.vector.reciprocal(ssq[:, 2, :, cs], ssq[:, 1, :, cs]))
                g4 = gy[:, :, 512 - 512 * g:1024 - 512 * g].rearrange("p i (h n) -> p i h n", h=4)
                nc.vector.tensor_tensor(g4, g4, spread(ssq[:, 2, :, cs], [[8, 4], [1, 4], [0, DV]]), ALU.mult).then_inc(y_scaled, 1)
            gg = vecT[:, ROWS["gla_g"]:ROWS["gla_g"] + 1]
            transposed(20, KT, T, a_hi, a_lo, trB, lambda k: [(0, T, gg if k >= 4 else None, None)])
            def add_gated(b, at, row, dst, cs, alpha=None):
                tmp = trB[b % 2][:, :].rearrange("p (m n) -> p m n", m=2)
                nc.vector.tensor_tensor(tmp, bank[b % 4][:, :].rearrange("p (m n) -> p m n", m=2),
                                        spread(grow[:, row, cs], [[0, 2], [1, UC]]), ALU.mult).then_inc(free[b % 4], 1)
                dve.wait_ge(free[b % 4], at)
                if alpha is None:
                    nc.vector.tensor_tensor(dst[:, :, cs], dst[:, :, cs], tmp, ALU.add).then_inc(vchain, 1)
                else:
                    nc.vector.scalar_tensor_tensor(out=dst[:, :, cs], in0=dst[:, :, cs], scalar=alpha, in1=tmp,
                                                   op0=ALU.mult, op1=ALU.add).then_inc(vchain, 1)
                return chain.up()

            for u in range(U_EVO, U_M0):
                split_lo(u + LEAD)
                quarters(UNIT_Q[u])
                if u == U_EVO:
                    dve.wait_ge(rowb_done, 2)
                    dve.wait_ge(load_cr, 16)
                for i, dst in enumerate((cres, xres)):
                    b = before[u] + i
                    take(b)
                    add_gated(b, b // 4 + 1, i, dst, slice((u - U_EVO) * UC, (u - U_EVO + 1) * UC), ALPHA)

            def layer_norm(k):
                tiles = LN_TILES[k]
                r0 = 4 - tiles
                dve.wait_ge(vchain, chain.at())
                for i in range(tiles):
                    for j in range(2):
                        last = nc.vector.bn_stats(bns[:, i, j, :], R[r0 + i][:, 512 * j:512 * j + 512])
                link(last)
                for i in range(tiles):
                    last = nc.vector.bn_aggr(bna[:, i, 0:2], bns[:, i, :, :])
                last.then_inc(ln_var, 1)
                dve.wait_ge(ln_root, k + 1)
                link(nc.vector.reciprocal(bna[:, 0:tiles, 3], bna[:, 0:tiles, 2]))
                nc.vector.scalar_tensor_tensor(out=bna[:, 0:tiles, 4], in0=bna[:, 0:tiles, 0], scalar=-1.0,
                                               in1=bna[:, 0:tiles, 3], op0=ALU.mult, op1=ALU.mult).then_inc(ln_inv, 1)
                for i in range(0, tiles, 2):
                    nc.vector.tensor_scalar(Y[:, i, :], R[r0 + i], bna[:, i, 0:1], bna[:, i, 3:4], ALU.subtract, ALU.mult)\
                        .then_inc(ln_even, 1)

            def affine(rows, k, sh, sc):
                g0, b0 = ROWS["ln_g"] + 8 * k, ROWS["ln_b"] + 8 * k
                nc.vector.scalar_tensor_tensor(out=aff[:, rows, :], in0=mod[:, sc:sc + 8], scalar=1.0, in1=vecT[:, g0:g0 + 8],
                                               op0=ALU.add, op1=ALU.mult)
                link(nc.vector.scalar_tensor_tensor(out=aff[:, rows + 1, :], in0=mod[:, sc:sc + 8], scalar=1.0,
                                                    in1=vecT[:, b0:b0 + 8], op0=ALU.add, op1=ALU.mult))
                link(nc.vector.tensor_tensor(aff[:, rows + 1, :], aff[:, rows + 1, :], mod[:, sh:sh + 8], ALU.add))

            take_mod(21)
            layer_norm(0)
            affine(0, 0, M0C + 24, M0C + 32)
            affine(2, 0, M0 + 24, M0 + 32)
            both = lambda k: [(0, S, aff[:, 0, k:k + 1], aff[:, 1, k:k + 1]), (S, T, aff[:, 2, k:k + 1], aff[:, 3, k:k + 1])]
            transposed(28, KT, T, a_hi, a_lo, trB, both)

            def mlp(u0, Tn, mh, ml, hid0, vecs, more):
                per = 8 * Tn // 256
                ht = 4 * Tn // 256
                tn = Tn // 256

                def round_(r, lead=8):
                    for j in range(8):
                        u = u0 + j + LEAD
                        if j < lead:
                            dve.wait_ge(hi_done, at_(u + 1, r, 8))
                            nc.vector.tensor_tensor(wlo[u % SPL][:, :], raw[u % RAW][:, :], bf(whi[u % SPL], KT * UC),
                                                    ALU.subtract).then_inc(lo_done, 1)
                        if vecs and j == 3:
                            take_loop_mod(22, r)
                        if vecs:
                            for i in LOOP_Q[j]:
                                qq = U_Q + i
                                s_, v_ = gfull(qq)
                                dve.wait_ge(s_, at_(v_, r, 16 * 8 // GSB))
                                if i % 4 == 0:
                                    dve.wait_ge(seed_full, at_(16 * ((qq - PRE_Q) // 4 + 1), r, 32))
                                for kk in range(2):
                                    kt = (i % 4) * 2 + kk
                                    if kt:
                                        dve.wait_ge(vsum, at_(vops[U_Q] + 2 * i + kk, r, 16))
                                    nc.vector.scalar_tensor_tensor(
                                        out=acc[:, 0, :], in0=vslot(qq)[:, kk, :], scalar=cvec[:, 1, kt:kt + 1],
                                        in1=acc[:, 0, :] if kt else seed[:, :], op0=ALU.mult, op1=ALU.add).then_inc(vsum, 1)
                        if vecs and j == 6:
                            take_loop_mod(23, r)
                        for i in range(tn):
                            bt, t = before[u0 + j] + i, tn * j + i
                            if j < 4:
                                dve.wait_ge(free[bt % 4], at_(bt // 4 + 1, r, per // 4))
                                if t:
                                    dve.wait_ge(hid_lo, at_(hid0 + t, r, ht))
                                nc.vector.tensor_tensor(sq_[:, :], rel_[:, :], rel_[:, :], ALU.mult).then_inc(sq_done, 1)
                                dve.wait_ge(hid_hi, at_(hid0 + t + 1, r, ht))
                                fs = slice(512 * t, 512 * t + 512)
                                nc.vector.tensor_tensor(flat(ml)[:, fs], sq_[:, :], flat(mh)[:, fs].bitcast(f32), ALU.subtract)\
                                    .then_inc(hid_lo, 1)
                                if t == ht - 1:
                                    dve.wait_ge(hid_lo, at_(hid0 + ht, r, ht))
                            else:
                                dve.wait_ge(tile_done, at_(bt + 1, r, per))
                                add_gated(bt, at_(bt // 4 + 1, r, per // 4), i, (cres, xres)[i] if tn == 2 else xres,
                                          slice((j - 4) * UC, (j - 3) * UC))

                with dve.Fori(0, 4 if more else 3) as r:
                    round_(r)
                if not more:
                    round_(3, 8 - LEAD)

            def take_loop_mod(n, r):
                dve.wait_ge(red_done, at_(n + 1, r, 2))
                nc.vector.tensor_copy(mod[:, bass.ds(r * 8 + (M1 + 16 + 4 * (n - 22)), 4)], bank[7][:, 0:4])\
                    .then_inc(mod_done, 1)

            dve.wait_ge(res_mul, RES[1])
            dve.wait_ge(rowb_done, 3)
            mlp(U_M0, T, m_hi, m_lo, 0, True, True)
            chain.n += 3 * 8
            layer_norm(1)
            affine(0, 1, M1C, M1C + 8)
            affine(2, 1, M1, M1 + 8)
            transposed(36, KT, T, a_hi, a_lo, trB, both)

            def rotate(src, m, dst):
                heads = lambda v: spread(v, [[AHD, 4], [AHD // 2, 2], [1, AHD // 4]])
                q4 = AHD // 4
                cs, sn = [spread(const(n)[:, m * 2 * q4:(m + 1) * 2 * q4], [[0, 4], [q4, 2], [1, q4]]) for n in ("cos", "sin")]
                t1, t2 = [trB[i][:, m * UC:(m + 1) * UC] for i in range(2)]
                for half in (0, 1):
                    hs = slice(half * q4, UC)
                    nc.vector.tensor_tensor(heads(t1[:, hs]), heads(src[:, hs]), cs, ALU.mult)
                    last = nc.vector.tensor_tensor(heads(t2[:, hs]), heads(src[:, hs]), sn, ALU.mult)
                link(last)
                nc.vector.tensor_tensor(dst(0), heads(t1), heads(t2[:, q4:]), ALU.subtract)
                return nc.vector.tensor_tensor(dst(1), heads(t1[:, q4:]), heads(t2), ALU.add)

            def low_transposed(n):
                dve.wait_ge(kq_hi, n + 1)
                src = bank[4 + n % 4][:, :]
                if n < KVH:
                    nc.vector.tensor_tensor(k_lo[:, n, :], src, k_hi[:, n, :].bitcast(f32), ALU.subtract).then_inc(kq_ev, 1)
                else:
                    j = n - KVH
                    for half in range(2):
                        hs, ls = slice(64 * half, 64 * half + 64), slice(64 - 64 * half, P - 64 * half)
                        heads = slice(4 * j + half, 4 * j + 4, 2)
                        last = nc.vector.scalar_tensor_tensor(
                            out=q_both[ls, heads, :], in0=src[hs, :].rearrange("p (a b) -> p a b", a=2), scalar=AHD ** -0.5,
                            in1=q_both[hs, heads, :].bitcast(f32), op0=ALU.mult, op1=ALU.subtract)
                    last.then_inc(kq_ev, 1)

            dve.wait_ge(res_mul, RES[2])
            for u in range(U_QKV, U_OD):
                split_lo(u + LEAD)
                b, j = before[u], u - U_QKV
                if j == 0:
                    src = take(b + 1)
                    for m in range(NT):
                        kr = krow[:, NT + m, 0, 0, :]
                        last = rotate(src[:, m * UC:(m + 1) * UC], m,
                                      lambda half: spread(kr[:, half * 16:], [[2 * AHD, 4], [AHD // 2, 2], [1, 16]]))
                    link(last)
                    for m in range(NT):
                        last = nc.vector.tensor_copy(krow[:, NT + m, :, 1, :], krow[:, NT + m, :, 0, :])
                    last.then_inc(free[(b + 1) % 4], 1)
                elif j == 1:
                    for i in range(2):
                        dve.wait_ge(vhi_done, i + 1)
                        nc.vector.tensor_tensor(v_lo[:, 2 * i:2 * i + 2, :], bank[(b + i) % 4][:, :].rearrange("p (m n) -> p m n", m=2),
                                                v_hi[:, 2 * i:2 * i + 2, :].bitcast(f32), ALU.subtract).then_inc(free[(b + i) % 4], 1)
                elif j >= 2:
                    src = take(b)
                    for m in range(NT):
                        qr = qrow[:, m, (j - 2) * UC:(j - 1) * UC]
                        last = rotate(src[:, m * UC:(m + 1) * UC], m,
                                      lambda half: spread(qr[:, half * 16:], [[AHD, 4], [AHD // 2, 2], [1, 16]]))
                    last.then_inc(free[b % 4], 1)
                    taken(dve, b)
                if j == 2:
                    for n in range(KVH):
                        low_transposed(n)
                elif j > 2:
                    low_transposed(KVH + j - 3)
            low_transposed(7)
            dve.wait_ge(load_sk, 16)
            N = len(wsteps)
            for n in range(N + 4):
                if n < N:
                    h, w = wsteps[n][1], wst[:, n % 4, :]
                    dve.wait_ge(wa_s, n + 1)
                    if n >= 4:
                        dve.wait_ge(wa_n, n - 3)
                    link(nc.vector.tensor_reduce(w[:, 0:1], bank[4 + n % 2][:, :], AX.X, ALU.max))
                    nc.vector.tensor_scalar(w[:, 1:2], w[:, 0:1], sink[:, h:h + 1], -1.0, ALU.max, ALU.mult).then_inc(wa_max, 1)
                if n >= 1 and n <= N:
                    w = wst[:, (n - 1) % 4, :]
                    dve.wait_ge(wa_exp, n)
                    link(nc.vector.tensor_tensor(w[:, 4:5], w[:, 2:3], w[:, 3:4], ALU.add))
                    nc.vector.reciprocal(w[:, 5:6], w[:, 4:5]).then_inc(wa_rc, 1)
                if n >= 3:
                    i = n - 3
                    if i and i % 4 == 0:
                        g = i // 4 - 1
                        qt, kv_ = wsteps[4 * g][0], wsteps[4 * g][1] // 4
                        dve.wait_ge(wa_oh, g + 1)
                        for half in range(2):
                            w = (slice(64 * half, 64 * half + 64), slice(2 * kv_, 2 * kv_ + 2), slice(qt * P, (qt + 1) * P))
                            last = nc.vector.tensor_tensor(
                                o_lo[w], bank[g % 2][0:AHD, :].rearrange("p (a b q) -> p a b q", a=2, b=2)[:, :, half, :],
                                o_hi[w].bitcast(f32), ALU.subtract)
                        last.then_inc(wa_o, 1)
                    if i < N:
                        dve.wait_ge(wa_hi, i + 1)
                        nc.vector.tensor_tensor(pT_lo[:, :, i % 4, :], bank[6 + i % 2][:, :].rearrange("p (b q) -> p b q", b=4),
                                                pT_hi[:, :, i % 4, :].bitcast(f32), ALU.subtract).then_inc(wa_lo, 1)
            dve.wait_ge(rowb_done, 4)
            for u in range(U_OD, U_M1):
                split_lo(u + LEAD)
                take(before[u])
                add_gated(before[u], before[u] // 4 + 1, 0, xres, slice((u - U_OD) * UC, (u - U_OD + 1) * UC), ALPHA)
            layer_norm(2)
            affine(0, 2, M1 + 24, M1 + 32)
            transposed(44, KT, S, a_hi, a_lo, trB, lambda k: [(0, S, aff[:, 0, k:k + 1], aff[:, 1, k:k + 1])])
            dve.wait_ge(res_mul, RES[3])
            dve.wait_ge(rowb_done, 5)
            mlp(U_M1, S, *half_m, 32, False, False)
            chain.n += 2 * 4
            layer_norm(3)


INS = ["x", "c", "norm_g", "w_ada", "b_ada", "w_in", "pool_w", "pool_scale", "w_attn_br", "w_pool_br", "w_out",
       "rel_bias", "final_g", "c_2", "ctx_2", "c_ctx_2", "w_mod_2", "b_mod_2", "ln_g_2", "ln_b_2", "mlp_w1_2",
       "mlp_w2_2", "ev_w_in_2", "ev_ret_theta_2", "ev_gla_gk_w_2", "ev_gla_gk_b_2", "ev_gla_norm_g_2", "ev_w_out_2",
       "od_w_qkv_2", "od_sink_2", "od_w_out_2"]


def kernel(**inputs):
    import concourse.bacc as bacc
    from concourse.bass_utils import run_bass_kernel_spmd as run

    nc = bacc.Bacc("TRN2", target_bir_lowering=False, num_devices=1)
    arrays, a = {}, {}
    for name in INS:
        v = np.ascontiguousarray(inputs[name])
        arrays[f"in_{name}"] = v
        a[name] = nc.dram_tensor(f"in_{name}", v.shape, mybir.dt.from_np(v.dtype), kind="ExternalInput").ap()
    table, at, keep = constants()
    arrays["table"] = table
    cst = nc.dram_tensor("table", table.shape, mybir.dt.float32, kind="ExternalInput").ap()
    scratch = nc.dram_tensor("distance_rows", [HEADS, GROUPS * 384], mybir.dt.float32).ap()
    out = nc.dram_tensor("out", [1, S, D], mybir.dt.float32, kind="ExternalOutput").ap()
    build(nc, a, out, cst, at, keep, scratch)
    r = run(nc, [arrays], core_ids=[0])
    return r.results[0]["out"]
```
